# Optimizing a Trainium2 kernel written in Bass

```python
import math
import jax, jax.numpy as jnp
from jax import lax
import numpy as np

D_MODEL = 1024
BATCH = 1
SEQ = 512
DEPTH = 2

HEAD_DIM = 64
A_Q_HEADS = 8
A_KV_HEADS = 2
A_GROUP = A_Q_HEADS // A_KV_HEADS
WINDOW = 128
BLOCK = 128
B_HEADS = 8
A_WIDTH = A_Q_HEADS * HEAD_DIM
A_KV_WIDTH = A_KV_HEADS * HEAD_DIM
B_WIDTH = B_HEADS * HEAD_DIM
ATTN_WIDTH = A_WIDTH + B_WIDTH
ATTN_SPLITS = (A_WIDTH, A_KV_WIDTH, A_KV_WIDTH, B_WIDTH, B_WIDTH, B_WIDTH, B_HEADS, ATTN_WIDTH)
ATTN_IN = sum(ATTN_SPLITS)
REL_BUCKETS = 32
REL_MAX_EXACT = 16
REL_MAX_DIST = 128
LRU_WIDTH = D_MODEL
LRU_BLOCKS = 8
LRU_BLOCK_W = LRU_WIDTH // LRU_BLOCKS
CONV_WIDTH = 4
LRU_C = 8.0
N_ATTN_LAYERS = (DEPTH + 1) // 2
N_LRU_LAYERS = DEPTH // 2
EPS = 1e-6


def rmsnorm(x, g):
    x32 = x.astype(jnp.float32)
    y = x32 * lax.rsqrt(jnp.mean(x32 * x32, axis=-1, keepdims=True) + EPS)
    return (y * g.astype(jnp.float32)).astype(x.dtype)

def t5_causal_bucket(rel):
    n = jnp.maximum(rel, 0)
    nf = jnp.maximum(n, 1).astype(jnp.float32)
    large = REL_MAX_EXACT + (jnp.log(nf / REL_MAX_EXACT) / math.log(REL_MAX_DIST / REL_MAX_EXACT)
                             * (REL_BUCKETS - REL_MAX_EXACT)).astype(jnp.int32)
    large = jnp.minimum(large, REL_BUCKETS - 1)
    return jnp.where(n < REL_MAX_EXACT, n, large)

def swa_sink_attention(q, k, v, sinks, rel_bias):
    B, S = q.shape[0], q.shape[1]
    nb = S // BLOCK
    qb = q.reshape(B, nb, BLOCK, A_KV_HEADS, A_GROUP, HEAD_DIM)
    pad = ((0, 0), (BLOCK, 0), (0, 0), (0, 0))
    kp = jnp.pad(k, pad)[:, :S].reshape(B, nb, BLOCK, A_KV_HEADS, HEAD_DIM)
    vp = jnp.pad(v, pad)[:, :S].reshape(B, nb, BLOCK, A_KV_HEADS, HEAD_DIM)
    kb = jnp.concatenate([kp, k.reshape(B, nb, BLOCK, A_KV_HEADS, HEAD_DIM)], axis=2)
    vb = jnp.concatenate([vp, v.reshape(B, nb, BLOCK, A_KV_HEADS, HEAD_DIM)], axis=2)
    scores = jnp.einsum('bnqhgd,bnkhd->bhgnqk', qb, kb).astype(jnp.float32) * (HEAD_DIM ** -0.5)
    qi = jnp.arange(BLOCK)[:, None]
    kj = jnp.arange(2 * BLOCK)[None, :]
    rel = qi - kj + BLOCK
    bias = rel_bias.astype(jnp.float32)[t5_causal_bucket(rel)]
    bias = jnp.transpose(bias, (2, 0, 1)).reshape(A_KV_HEADS, A_GROUP, 1, BLOCK, 2 * BLOCK)
    valid = (rel >= 0) & (rel < WINDOW)
    first = (jnp.arange(nb)[:, None, None] == 0) & (kj[None] < BLOCK)
    mask = valid[None] & ~first
    logits = jnp.where(mask, scores + bias, -jnp.inf)
    sink = jnp.broadcast_to(sinks.astype(jnp.float32).reshape(1, A_KV_HEADS, A_GROUP, 1, 1, 1),
                            logits.shape[:-1] + (1,))
    probs = jax.nn.softmax(jnp.concatenate([logits, sink], axis=-1), axis=-1)[..., :-1]
    out = jnp.einsum('bhgnqk,bnkhd->bnqhgd', probs.astype(v.dtype), vb)
    return out.reshape(B, S, A_WIDTH)

def forgetting_attention(q, k, v, log_f):
    B, S = q.shape[0], q.shape[1]
    nb = S // BLOCK
    F = jnp.cumsum(log_f, axis=1)
    outs = []
    for n in range(nb):
        q0, kend = n * BLOCK, (n + 1) * BLOCK
        qs = q[:, q0:kend]
        ks, vs = k[:, :kend], v[:, :kend]
        s = jnp.einsum('bqhd,bkhd->bhqk', qs, ks).astype(jnp.float32) * (HEAD_DIM ** -0.5)
        decay = jnp.transpose(F[:, q0:kend], (0, 2, 1))[..., :, None] - jnp.transpose(F[:, :kend], (0, 2, 1))[..., None, :]
        tpos = q0 + jnp.arange(BLOCK)[:, None]
        spos = jnp.arange(kend)[None, :]
        p = jax.nn.softmax(jnp.where(spos <= tpos, s + decay, -jnp.inf), axis=-1)
        outs.append(jnp.einsum('bhqk,bkhd->bqhd', p.astype(v.dtype), vs))
    return jnp.concatenate(outs, axis=1).reshape(B, S, B_WIDTH)

def attention_mixer(h, w_in, sinks, b_f, w_out, rel_bias):
    B, S, _ = h.shape
    proj = h @ w_in
    idx = np.cumsum(ATTN_SPLITS)[:-1].tolist()
    a_q, a_k, a_v, b_q, b_k, b_v, f_logit, gate = jnp.split(proj, idx, axis=-1)
    a_out = swa_sink_attention(a_q.reshape(B, S, A_Q_HEADS, HEAD_DIM),
                               a_k.reshape(B, S, A_KV_HEADS, HEAD_DIM),
                               a_v.reshape(B, S, A_KV_HEADS, HEAD_DIM), sinks, rel_bias)
    log_f = jax.nn.log_sigmoid((f_logit + b_f).astype(jnp.float32))
    b_out = forgetting_attention(b_q.reshape(B, S, B_HEADS, HEAD_DIM),
                                 b_k.reshape(B, S, B_HEADS, HEAD_DIM),
                                 b_v.reshape(B, S, B_HEADS, HEAD_DIM), log_f)
    y = jnp.concatenate([a_out, b_out], axis=-1) * jax.nn.silu(gate)
    return y @ w_out

def rglru_mixer(h, w_in, conv_w, conv_b, w_a, b_a, w_x, b_x, lam, w_out):
    B, S, _ = h.shape
    proj = h @ w_in
    xr, gate = proj[..., :LRU_WIDTH], proj[..., LRU_WIDTH:]
    xp = jnp.pad(xr, ((0, 0), (CONV_WIDTH - 1, 0), (0, 0)))
    xc = conv_b
    for j in range(CONV_WIDTH):
        xc = xc + xp[:, j:j + S] * conv_w[j]
    xblk = xc.reshape(B, S, LRU_BLOCKS, LRU_BLOCK_W)
    r = jax.nn.sigmoid((jnp.einsum('bsnw,nwv->bsnv', xblk, w_a).reshape(B, S, LRU_WIDTH) + b_a).astype(jnp.float32))
    i = jax.nn.sigmoid((jnp.einsum('bsnw,nwv->bsnv', xblk, w_x).reshape(B, S, LRU_WIDTH) + b_x).astype(jnp.float32))
    log_a = -LRU_C * r * jax.nn.softplus(-lam.astype(jnp.float32))
    a = jnp.exp(log_a)
    u = jnp.sqrt(-jnp.expm1(2.0 * log_a)) * (i * xc.astype(jnp.float32))

    def step(state, inp):
        a_t, u_t = inp
        state = a_t * state + u_t
        return state, state

    _, hs = lax.scan(step, jnp.zeros((B, LRU_WIDTH), jnp.float32),
                     (jnp.transpose(a, (1, 0, 2)), jnp.transpose(u, (1, 0, 2))))
    y = jnp.transpose(hs, (1, 0, 2)).astype(h.dtype) * jax.nn.silu(gate)
    return y @ w_out

def first_inputs(seed: int = 0) -> dict:
    key = jax.random.key(seed)
    ks = jax.random.split(key, 22)
    nrm = lambda k, shape, s: jax.random.normal(k, shape, jnp.float32) * s
    a0 = jax.random.uniform(ks[19], (N_LRU_LAYERS, LRU_WIDTH), jnp.float32, 0.9, 0.999) ** (1.0 / LRU_C)
    return {
        "x": nrm(ks[0], (BATCH, SEQ, D_MODEL), 1.0),
        "c": nrm(ks[1], (BATCH, D_MODEL), 1.0),
        "rel_bias": nrm(ks[2], (REL_BUCKETS, A_Q_HEADS), 0.2),
        "norm_g": 1.0 + nrm(ks[3], (DEPTH, D_MODEL), 0.05),
        "ada_w": nrm(ks[4], (DEPTH, D_MODEL, 3 * D_MODEL), 0.3 * D_MODEL ** -0.5),
        "ada_b": nrm(ks[5], (DEPTH, 3 * D_MODEL), 0.02),
        "attn_w_in": nrm(ks[6], (N_ATTN_LAYERS, D_MODEL, ATTN_IN), D_MODEL ** -0.5),
        "attn_sinks": nrm(ks[7], (N_ATTN_LAYERS, A_Q_HEADS), 0.5),
        "attn_b_f": jax.random.uniform(ks[8], (N_ATTN_LAYERS, B_HEADS), jnp.float32, 1.0, 4.0),
        "attn_w_out": nrm(ks[9], (N_ATTN_LAYERS, ATTN_WIDTH, D_MODEL), ATTN_WIDTH ** -0.5),
        "lru_w_in": nrm(ks[10], (N_LRU_LAYERS, D_MODEL, 2 * LRU_WIDTH), D_MODEL ** -0.5),
        "lru_conv_w": nrm(ks[11], (N_LRU_LAYERS, CONV_WIDTH, LRU_WIDTH), CONV_WIDTH ** -0.5),
        "lru_conv_b": nrm(ks[12], (N_LRU_LAYERS, LRU_WIDTH), 0.02),
        "lru_w_a": nrm(ks[13], (N_LRU_LAYERS, LRU_BLOCKS, LRU_BLOCK_W, LRU_BLOCK_W), LRU_BLOCK_W ** -0.5),
        "lru_b_a": nrm(ks[14], (N_LRU_LAYERS, LRU_WIDTH), 0.02),
        "lru_w_x": nrm(ks[15], (N_LRU_LAYERS, LRU_BLOCKS, LRU_BLOCK_W, LRU_BLOCK_W), LRU_BLOCK_W ** -0.5),
        "lru_b_x": nrm(ks[16], (N_LRU_LAYERS, LRU_WIDTH), 0.02),
        "lru_lambda": jnp.log(a0) - jnp.log1p(-a0),
        "lru_w_out": nrm(ks[17], (N_LRU_LAYERS, LRU_WIDTH, D_MODEL), LRU_WIDTH ** -0.5),
        "final_g": 1.0 + nrm(ks[18], (D_MODEL,), 0.05),
    }

def first_block(x, c, rel_bias, norm_g, ada_w, ada_b, attn_w_in, attn_sinks, attn_b_f, attn_w_out,
              lru_w_in, lru_conv_w, lru_conv_b, lru_w_a, lru_b_a, lru_w_x, lru_b_x, lru_lambda,
              lru_w_out, final_g):
    c_act = jax.nn.silu(c)
    for layer in range(DEPTH):
        mod = c_act @ ada_w[layer] + ada_b[layer]
        shift, scale, gate = jnp.split(mod, 3, axis=-1)
        h = rmsnorm(x, norm_g[layer]) * (1.0 + scale[:, None, :]) + shift[:, None, :]
        if layer % 2 == 0:
            j = layer // 2
            y = attention_mixer(h, attn_w_in[j], attn_sinks[j], attn_b_f[j], attn_w_out[j], rel_bias)
        else:
            j = layer // 2
            y = rglru_mixer(h, lru_w_in[j], lru_conv_w[j], lru_conv_b[j], lru_w_a[j], lru_b_a[j],
                            lru_w_x[j], lru_b_x[j], lru_lambda[j], lru_w_out[j])
        x = x + gate[:, None, :] * y
    return rmsnorm(x, final_g)


NSA_HEADS = 8
NSA_GROUPS = 2
NSA_HPG = NSA_HEADS // NSA_GROUPS
CMP_LEN = 32
CMP_STRIDE = 16
CMP_HIDDEN = 256
SEL_BLK = 64
N_SEL = 16
WINDOW_2 = 512
DSA_HEADS = 8
DSA_KV_RANK = 128
IDX_HEADS = 8
IDX_DIM = 64
DSA_TOPK = 256
DIFF_HEADS = 8
DIFF_DIM = 64
D_FF = 4 * D_MODEL
NUM_BUCKETS = 32
MAX_DISTANCE = 128
REL_HEADS = NSA_HEADS + DSA_HEADS
QBLK = 128
N_EVEN = (DEPTH + 1) // 2
N_ODD = DEPTH // 2
ALPHA = (2 * DEPTH) ** 0.25
BETA = (8 * DEPTH) ** -0.25
NEG_INF = -1e30
BIG = 1e9
EPS_2 = 1e-5
NSA_Q = NSA_HEADS * HEAD_DIM
NSA_KV = 2 * NSA_GROUPS * HEAD_DIM
NSA_GATE = NSA_HEADS * 3
DSA_Q = DSA_HEADS * HEAD_DIM
EVEN_SIZES = (NSA_Q, NSA_KV, NSA_KV, NSA_KV, NSA_GATE, DSA_Q, DSA_KV_RANK, IDX_HEADS * IDX_DIM, IDX_DIM, IDX_HEADS)
EVEN_IN = sum(EVEN_SIZES)
EVEN_OUT = NSA_Q + DSA_HEADS * HEAD_DIM
ODD_IN = 3 * DIFF_HEADS * 2 * DIFF_DIM
ODD_OUT = DIFF_HEADS * 2 * DIFF_DIM


def _split(x, sizes):
    offs = np.cumsum(sizes)[:-1].tolist()
    return jnp.split(x, offs, axis=-1)

def layer_norm(x, g, b):
    xf = x.astype(jnp.float32)
    mu = jnp.mean(xf, axis=-1, keepdims=True)
    var = jnp.mean(jnp.square(xf - mu), axis=-1, keepdims=True)
    return ((xf - mu) * lax.rsqrt(var + EPS_2) * g + b).astype(x.dtype)

def rms_norm(x, g):
    xf = x.astype(jnp.float32)
    return (xf * lax.rsqrt(jnp.mean(jnp.square(xf), axis=-1, keepdims=True) + EPS_2) * g).astype(x.dtype)

def masked_softmax(logits, mask):
    z = jnp.where(mask, logits.astype(jnp.float32), NEG_INF)
    z = z - jnp.max(z, axis=-1, keepdims=True)
    e = jnp.where(mask, jnp.exp(z), 0.0)
    return e / jnp.maximum(jnp.sum(e, axis=-1, keepdims=True), 1e-30)

def t5_bucket(dist):
    n = jnp.maximum(dist, 0)
    exact = NUM_BUCKETS // 2
    nf = jnp.maximum(n, 1).astype(jnp.float32)
    large = exact + (jnp.log(nf / exact) / math.log(MAX_DISTANCE / exact) * (NUM_BUCKETS - exact)).astype(jnp.int32)
    return jnp.where(n < exact, n, jnp.minimum(large, NUM_BUCKETS - 1))

def sweep_query_blocks(fn, B, S):
    out = lax.map(fn, jnp.arange(S // QBLK))
    return jnp.moveaxis(out, 0, 1).reshape(B, S, -1)

def nsa_compress(k_raw, pe, w1, w2):
    B, S, G, Dh = k_raw.shape
    nc = (S - CMP_LEN) // CMP_STRIDE + 1
    idx = np.arange(nc)[:, None] * CMP_STRIDE + np.arange(CMP_LEN)[None, :]
    blk = k_raw[:, idx] + pe[:, None, :]
    blk = blk.transpose(0, 1, 3, 2, 4).reshape(B, nc, G, CMP_LEN * Dh)
    return jax.nn.gelu(blk @ w1) @ w2

def nsa_attention(q, kvc, kvs, kvw, gate_logits, pe_k, pe_v, w1_k, w2_k, w1_v, w2_v, bias_tab):
    B, S = q.shape[:2]
    G, HPG, Dh = NSA_GROUPS, NSA_HPG, HEAD_DIM
    q = q.reshape(B, S, G, HPG, Dh)
    kc_raw, vc_raw = [a.reshape(B, S, G, Dh) for a in jnp.split(kvc, 2, axis=-1)]
    kc = nsa_compress(kc_raw, pe_k, w1_k, w2_k)
    vc = nsa_compress(vc_raw, pe_v, w1_v, w2_v)
    ks, vs = [a.reshape(B, S, G, Dh).transpose(0, 2, 1, 3) for a in jnp.split(kvs, 2, axis=-1)]
    kw, vw = [jnp.pad(a.reshape(B, S, G, Dh), ((0, 0), (WINDOW_2, 0), (0, 0), (0, 0))) for a in jnp.split(kvw, 2, axis=-1)]
    gates = jax.nn.sigmoid(gate_logits.astype(jnp.float32)).astype(q.dtype).reshape(B, S, G, HPG, 3)
    nc = kc.shape[1]
    nb = S // SEL_BLK
    n_sel = min(N_SEL, nb)
    cs = np.arange(nc) * CMP_STRIDE
    ss = np.arange(nb) * SEL_BLK
    overlap = np.clip(np.minimum(cs[:, None] + CMP_LEN, ss[None, :] + SEL_BLK) - np.maximum(cs[:, None], ss[None, :]), 0, None)
    imp = jnp.asarray(overlap / CMP_STRIDE, dtype=jnp.float32)
    cmp_end = jnp.asarray(cs + CMP_LEN - 1, dtype=jnp.int32)
    tab = bias_tab.reshape(NUM_BUCKETS, G, HPG)
    scale = Dh ** -0.5
    bi = jnp.arange(B)[:, None, None, None]
    gi = jnp.arange(G)[None, :, None, None]
    jblk = jnp.arange(nb)

    def block(qb):
        q0 = qb * QBLK
        t = q0 + jnp.arange(QBLK)
        qq = lax.dynamic_slice_in_dim(q, q0, QBLK, axis=1)
        gg = lax.dynamic_slice_in_dim(gates, q0, QBLK, axis=1)
        dc = t[:, None] - cmp_end[None, :]
        bias_c = tab[t5_bucket(dc)].transpose(2, 3, 0, 1)
        lc = jnp.einsum('bqghd,bngd->bghqn', qq, kc) * scale + bias_c
        pc = masked_softmax(lc, dc >= 0)
        oc = jnp.einsum('bghqn,bngd->bqghd', pc.astype(vc.dtype), vc)
        score = jnp.einsum('bghqn,nj->bgqj', pc, imp)
        cb = (t // SEL_BLK)[:, None]
        allowed = jblk[None, :] * SEL_BLK <= t[:, None]
        forced = (jblk[None, :] == 0) | (jblk[None, :] == cb) | (jblk[None, :] == cb - 1)
        score = jnp.where(forced, BIG, jnp.where(allowed, score, -BIG))
        _, sel = lax.top_k(score, n_sel)
        tok = (sel[..., None] * SEL_BLK + jnp.arange(SEL_BLK)).reshape(B, G, QBLK, n_sel * SEL_BLK)
        k_sel = ks[bi, gi, tok]
        v_sel = vs[bi, gi, tok]
        dist = t[None, None, :, None] - tok
        bias_s = tab[t5_bucket(dist), gi].transpose(0, 1, 4, 2, 3)
        ls = jnp.einsum('bqghd,bgqtd->bghqt', qq, k_sel) * scale + bias_s
        ps = masked_softmax(ls, (dist >= 0)[:, :, None])
        o_s = jnp.einsum('bghqt,bgqtd->bqghd', ps.astype(v_sel.dtype), v_sel)
        kwb = lax.dynamic_slice_in_dim(kw, q0, WINDOW_2 + QBLK, axis=1)
        vwb = lax.dynamic_slice_in_dim(vw, q0, WINDOW_2 + QBLK, axis=1)
        s = q0 - WINDOW_2 + jnp.arange(WINDOW_2 + QBLK)
        dw = t[:, None] - s[None, :]
        mask_w = (dw >= 0) & (dw < WINDOW_2) & (s[None, :] >= 0)
        bias_w = tab[t5_bucket(dw)].transpose(2, 3, 0, 1)
        lw = jnp.einsum('bqghd,bsgd->bghqs', qq, kwb) * scale + bias_w
        pw = masked_softmax(lw, mask_w)
        o_w = jnp.einsum('bghqs,bsgd->bqghd', pw.astype(vwb.dtype), vwb)
        out = gg[..., 0:1] * oc + gg[..., 1:2] * o_s + gg[..., 2:3] * o_w
        return out.reshape(B, QBLK, G * HPG * Dh)

    return sweep_query_blocks(block, B, S)

def dsa_attention(q, kv_lat, iq, ik, iw, kv_norm, w_uk, w_uv, bias_tab):
    B, S = q.shape[:2]
    ckv = rms_norm(kv_lat, kv_norm)
    q_lat = jnp.einsum('bshd,rhd->bshr', q, w_uk)
    iq = iq.reshape(B, S, IDX_HEADS, IDX_DIM)
    iw = iw * (IDX_HEADS ** -0.5 * IDX_DIM ** -0.5)
    topk = min(DSA_TOPK, S // 4)
    scale = HEAD_DIM ** -0.5
    bi = jnp.arange(B)[:, None, None]
    spos = jnp.arange(S)

    def block(qb):
        q0 = qb * QBLK
        t = q0 + jnp.arange(QBLK)
        iqb = lax.dynamic_slice_in_dim(iq, q0, QBLK, axis=1)
        iwb = lax.dynamic_slice_in_dim(iw, q0, QBLK, axis=1)
        qlb = lax.dynamic_slice_in_dim(q_lat, q0, QBLK, axis=1)
        rel = jax.nn.relu(jnp.einsum('bqjd,bsd->bqjs', iqb, ik))
        isc = jnp.einsum('bqj,bqjs->bqs', iwb, rel).astype(jnp.float32)
        isc = jnp.where(spos[None, None, :] <= t[None, :, None], isc, NEG_INF)
        _, idx = lax.top_k(isc, topk)
        c_sel = ckv[bi, idx]
        dist = t[None, :, None] - idx
        bias = bias_tab[t5_bucket(dist)].transpose(0, 3, 1, 2)
        logits = jnp.einsum('bqhr,bqkr->bhqk', qlb, c_sel) * scale + bias
        p = masked_softmax(logits, (dist >= 0)[:, None])
        o_lat = jnp.einsum('bhqk,bqkr->bqhr', p.astype(c_sel.dtype), c_sel)
        o = jnp.einsum('bqhr,rhd->bqhd', o_lat, w_uv)
        return o.reshape(B, QBLK, DSA_HEADS * HEAD_DIM)

    return sweep_query_blocks(block, B, S)

def even_mixer(h, w_in, w_out, pe_k, pe_v, w1_k, w2_k, w1_v, w2_v, kv_norm, w_uk, w_uv, rel_bias):
    B, S, _ = h.shape
    nsa_q, kvc, kvs, kvw, gate, dsa_q, dsa_kv, idx_q, idx_k, idx_w = _split(h @ w_in, EVEN_SIZES)
    o_a = nsa_attention(nsa_q, kvc, kvs, kvw, gate, pe_k, pe_v, w1_k, w2_k, w1_v, w2_v, rel_bias[:, :NSA_HEADS])
    o_b = dsa_attention(dsa_q.reshape(B, S, DSA_HEADS, HEAD_DIM), dsa_kv, idx_q, idx_k, idx_w, kv_norm, w_uk, w_uv, rel_bias[:, NSA_HEADS:])
    return jnp.concatenate([o_a, o_b], axis=-1) @ w_out

def diff_mixer(h, w_in, w_out, lam, subln, rel_bias, lambda_init):
    B, S, _ = h.shape
    q, k, v = jnp.split(h @ w_in, 3, axis=-1)
    q = q.reshape(B, S, DIFF_HEADS, 2, DIFF_DIM)
    k = k.reshape(B, S, DIFF_HEADS, 2, DIFF_DIM)
    v = v.reshape(B, S, DIFF_HEADS, 2 * DIFF_DIM)
    lamf = lam.astype(jnp.float32)
    lam_full = jnp.exp(jnp.sum(lamf[0] * lamf[1])) - jnp.exp(jnp.sum(lamf[2] * lamf[3])) + lambda_init
    tab = rel_bias.reshape(NUM_BUCKETS, DIFF_HEADS, 2)
    scale = DIFF_DIM ** -0.5
    spos = jnp.arange(S)

    def block(qb):
        q0 = qb * QBLK
        t = q0 + jnp.arange(QBLK)
        qq = lax.dynamic_slice_in_dim(q, q0, QBLK, axis=1)
        dist = t[:, None] - spos[None, :]
        bias = tab[t5_bucket(dist)].transpose(2, 3, 0, 1)
        logits = jnp.einsum('bqhmd,bshmd->bhmqs', qq, k) * scale + bias
        p = masked_softmax(logits, dist >= 0)
        pd = p[:, :, 0] - lam_full * p[:, :, 1]
        o = jnp.einsum('bhqs,bshe->bqhe', pd.astype(v.dtype), v)
        o = rms_norm(o, subln) * (1.0 - lambda_init)
        return o.reshape(B, QBLK, DIFF_HEADS * 2 * DIFF_DIM)

    return sweep_query_blocks(block, B, S) @ w_out

def sq_relu_mlp(h, w1, w2):
    return jnp.square(jax.nn.relu(h @ w1)) @ w2

def modulate(x, shift, scale):
    return x * (1.0 + scale[:, None, :]) + shift[:, None, :]

def second_inputs(seed: int = 0) -> dict:
    key = jax.random.key(seed)
    ks = jax.random.split(key, 26)
    f32 = jnp.float32

    def nrm(k, shape, fan_in, s=1.0):
        return jax.random.normal(k, shape, f32) * (s * fan_in ** -0.5)

    D = D_MODEL
    return {
        "x": jax.random.normal(ks[0], (BATCH, SEQ, D), f32),
        "c": jax.random.normal(ks[1], (BATCH, D), f32),
        "rel_bias": 0.5 * jax.random.normal(ks[2], (NUM_BUCKETS, REL_HEADS), f32),
        "ada_w": nrm(ks[3], (DEPTH, D, 6 * D), D, 0.2),
        "ada_b": 0.01 * jax.random.normal(ks[4], (DEPTH, 6 * D), f32),
        "ln_g": 1.0 + 0.02 * jax.random.normal(ks[5], (DEPTH, 2, D), f32),
        "ln_b": 0.02 * jax.random.normal(ks[6], (DEPTH, 2, D), f32),
        "ev_w_in": nrm(ks[7], (N_EVEN, D, EVEN_IN), D),
        "ev_w_out": nrm(ks[8], (N_EVEN, EVEN_OUT, D), EVEN_OUT, BETA),
        "nsa_pe_k": 0.5 * jax.random.normal(ks[9], (N_EVEN, CMP_LEN, HEAD_DIM), f32),
        "nsa_pe_v": 0.5 * jax.random.normal(ks[10], (N_EVEN, CMP_LEN, HEAD_DIM), f32),
        "nsa_w1_k": nrm(ks[11], (N_EVEN, CMP_LEN * HEAD_DIM, CMP_HIDDEN), CMP_LEN * HEAD_DIM),
        "nsa_w2_k": nrm(ks[12], (N_EVEN, CMP_HIDDEN, HEAD_DIM), CMP_HIDDEN),
        "nsa_w1_v": nrm(ks[13], (N_EVEN, CMP_LEN * HEAD_DIM, CMP_HIDDEN), CMP_LEN * HEAD_DIM),
        "nsa_w2_v": nrm(ks[14], (N_EVEN, CMP_HIDDEN, HEAD_DIM), CMP_HIDDEN),
        "dsa_kv_norm": 1.0 + 0.02 * jax.random.normal(ks[15], (N_EVEN, DSA_KV_RANK), f32),
        "dsa_w_uk": nrm(ks[16], (N_EVEN, DSA_KV_RANK, DSA_HEADS, HEAD_DIM), DSA_KV_RANK),
        "dsa_w_uv": nrm(ks[17], (N_EVEN, DSA_KV_RANK, DSA_HEADS, HEAD_DIM), DSA_KV_RANK),
        "od_w_in": nrm(ks[18], (N_ODD, D, ODD_IN), D),
        "od_w_out": nrm(ks[19], (N_ODD, ODD_OUT, D), ODD_OUT, BETA),
        "diff_lam": 0.1 * jax.random.normal(ks[20], (N_ODD, 4, DIFF_DIM), f32),
        "diff_subln": 1.0 + 0.02 * jax.random.normal(ks[21], (N_ODD, 2 * DIFF_DIM), f32),
        "mlp_w1": nrm(ks[22], (DEPTH, D, D_FF), D),
        "mlp_w2": nrm(ks[23], (DEPTH, D_FF, D), D_FF, BETA),
    }

def second_block(x, c, rel_bias, ada_w, ada_b, ln_g, ln_b, ev_w_in, ev_w_out, nsa_pe_k, nsa_pe_v, nsa_w1_k, nsa_w2_k, nsa_w1_v, nsa_w2_v, dsa_kv_norm, dsa_w_uk, dsa_w_uv, od_w_in, od_w_out, diff_lam, diff_subln, mlp_w1, mlp_w2):
    c_act = jax.nn.silu(c)
    for l in range(DEPTH):
        ada = c_act @ ada_w[l] + ada_b[l]
        sh1, sc1, g1, sh2, sc2, g2 = jnp.split(ada, 6, axis=-1)
        h = modulate(x, sh1, sc1)
        i = l // 2
        if l % 2 == 0:
            y = even_mixer(h, ev_w_in[i], ev_w_out[i], nsa_pe_k[i], nsa_pe_v[i], nsa_w1_k[i], nsa_w2_k[i], nsa_w1_v[i], nsa_w2_v[i], dsa_kv_norm[i], dsa_w_uk[i], dsa_w_uv[i], rel_bias)
        else:
            lambda_init = 0.8 - 0.6 * math.exp(-0.3 * l)
            y = diff_mixer(h, od_w_in[i], od_w_out[i], diff_lam[i], diff_subln[i], rel_bias, lambda_init)
        x = layer_norm(ALPHA * x + (1.0 + g1[:, None, :]) * y, ln_g[l, 0], ln_b[l, 0])
        h = modulate(x, sh2, sc2)
        y = sq_relu_mlp(h, mlp_w1[l], mlp_w2[l])
        x = layer_norm(ALPHA * x + (1.0 + g2[:, None, :]) * y, ln_g[l, 1], ln_b[l, 1])
    return x


def setup_inputs(seed=0):
    out = dict(first_inputs(seed))
    for name, value in second_inputs(seed + 1).items():
        if name != "x":
            out[name + "_2"] = value
    return out


def reference(
    x, c, rel_bias, norm_g, ada_w, ada_b, attn_w_in, attn_sinks, attn_b_f, attn_w_out, lru_w_in,
    lru_conv_w, lru_conv_b, lru_w_a, lru_b_a, lru_w_x, lru_b_x, lru_lambda, lru_w_out, final_g,
    c_2, rel_bias_2, ada_w_2, ada_b_2, ln_g_2, ln_b_2, ev_w_in_2, ev_w_out_2, nsa_pe_k_2,
    nsa_pe_v_2, nsa_w1_k_2, nsa_w2_k_2, nsa_w1_v_2, nsa_w2_v_2, dsa_kv_norm_2, dsa_w_uk_2,
    dsa_w_uv_2, od_w_in_2, od_w_out_2, diff_lam_2, diff_subln_2, mlp_w1_2, mlp_w2_2,
):
    x = first_block(
        x, c, rel_bias, norm_g, ada_w, ada_b, attn_w_in, attn_sinks, attn_b_f, attn_w_out,
        lru_w_in, lru_conv_w, lru_conv_b, lru_w_a, lru_b_a, lru_w_x, lru_b_x, lru_lambda,
        lru_w_out, final_g,
    )
    return second_block(
        x, c_2, rel_bias_2, ada_w_2, ada_b_2, ln_g_2, ln_b_2, ev_w_in_2, ev_w_out_2, nsa_pe_k_2,
        nsa_pe_v_2, nsa_w1_k_2, nsa_w2_k_2, nsa_w1_v_2, nsa_w2_v_2, dsa_kv_norm_2, dsa_w_uk_2,
        dsa_w_uv_2, od_w_in_2, od_w_out_2, diff_lam_2, diff_subln_2, mlp_w1_2, mlp_w2_2,
    )


_drawn_inputs = setup_inputs


def setup_inputs(seed=0):
    import zlib

    import numpy as np

    out = dict(_drawn_inputs(seed))
    spreads = {}
    factors = {'rel_bias': 8.0,
     'norm_g': 6.516,
     'ada_b': 2.855,
     'attn_sinks': 8.0,
     'attn_b_f': 3.394,
     'lru_conv_b': 4.838,
     'lru_b_a': 8.0,
     'lru_b_x': 8.0,
     'ada_b_2': 3.618,
     'nsa_pe_k_2': 8.0,
     'nsa_w1_k_2': 3.467,
     'nsa_w2_k_2': 3.543,
     'dsa_kv_norm_2': 8.0,
     'diff_subln_2': 8.0}
    for name, (base, spread) in spreads.items():
        noise = np.random.default_rng([zlib.crc32(name.encode()), seed]).standard_normal(out[name].shape)
        drawn = base * np.exp(spread * noise) if base else spread * noise
        out[name] = __import__('jax').numpy.asarray(drawn.astype(out[name].dtype))
    for name, factor in factors.items():
        out[name] = (out[name] * factor).astype(out[name].dtype)
    return out
```

```python
import math
from contextlib import ExitStack

import concourse.bass as bass
from concourse import mybir

F32 = mybir.dt.float32
F32R = mybir.dt.float32r
ALU = mybir.AluOpType
ACT = mybir.ActivationFunctionType
AX = mybir.AxisListType

P = 128
S = 512
D = 1024
NC = D // P
NT = S // P
HD = 64
BLK = 1024
NEG = -1e30
NSTREAM = 3
NADA = 2
N_BUCKET = 32
NCMP = (S - 32) // 16 + 1
TOPK = min(256, S // 4)
DSCALE = HD ** -0.5
ALPHA = 4 ** 0.25
LAMBDA_INIT = 0.8 - 0.6 * math.exp(-0.3)
LRU_C = 8.0

ARENA = 16384
A_Q = 0
A_AK, A_BK, A_VA, A_VB, A_GT, A_BA = 4096, 4608, 6656, 7168, 9216, 13312
A_BC = 15360
A_XR, A_LG, A_XC = 0, 4224, 8320
XRW = S + 3
A_KS, A_KW, A_VN, A_CKT, A_CKN, A_IQ, A_IK, A_KC2 = 4096, 4608, 5120, 6144, 6656, 7168, 9216, 9728
A_GI, A_M2, A_HID, A_PEN, A_KCT, A_VCN = 11776, 11904, 13312, 13568, 14720, 14752
A_QL, A_OL = 7168, 8192
M2_K, M2_V, M2_UK, M2_UV, M2W = 0, 256, 384, 896, 1408
A_DK, A_DV = 4096, 8192
A_OHB, A_OHC, A_TAB = 0, 384, 1376
OHW = 1400
A_U = 9216
BAND, CBAND = 384, 992

COLS = {}
_n = 0
for _name, _w in (("c", 8), ("c2", 8), ("ng0", 8), ("ng1", 8), ("adab", 144), ("fg", 8), ("lng", 32), ("lnb", 32),
                  ("cw", 32), ("cb", 8), ("ba", 8), ("bx", 8), ("lam", 8), ("kvn", 1), ("sub", 1), ("bf", 1),
                  ("pek", 16), ("pev", 16), ("sink", 8), ("t31", 16), ("dlam", 4)):
    COLS[_name] = (_n, _n + _w)
    _n += _w
NCOL = _n
C_ID, C_ONE, C_TRI, C_MC = 0, 128, 256, 384
NCONST = 384 + NT * NCMP


def tile_plan():
    t = []
    t += [("p1", "T", ("q", i)) for i in range(4)] + [("p1", "T", ("ak", 0))]
    t += [("p1", "T", ("q", 4 + i)) for i in range(4)] + [("p1", "T", ("bk", i)) for i in range(4)]
    t += [("p1", "T", ("f", 0))]
    t += [("p1", "N", ("vb", b, 4)) for b in range(4)] + [("p1", "N", ("va", 0, 1))]
    t += [("p1", "T", ("gate", i)) for i in range(8)]
    t += [("o1", "T", ("out", i)) for i in range(8)]
    t += [("lin", "T", ("xr", i)) for i in range(8)] + [("lin", "T", ("lgate", i)) for i in range(8)]
    t += [("lcore", "G", ("wa", 0)), ("lcore", "G", ("wx", 0))]
    t += [("o2", "T", ("out", i)) for i in range(8)]
    t += [("ev1", "T", ("ik", 0))] + [("ev1", "T", ("iq", i)) for i in range(4)] + [("ev1", "N", ("gi", 0, 1))]
    t += [("ev2", "T", ("kvl", 0))]
    t += [("ev2", "T", ("q", i)) for i in range(8)] + [("ev2", "T", ("ks", 0)), ("ev2", "T", ("kw", 0))]
    t += [("ev2", "N", ("vn", b, 2)) for b in range(2)]
    t += [("ev2", "T", ("kc2", i)) for i in range(4)]
    t += [("ev3", "C", (kv, b)) for kv in range(2) for b in range(4)]
    t += [("o3", "T", ("out", i)) for i in range(8)]
    for q in range(4):
        t += [("m1", "T", ("up", i)) for i in range(8)] + [("m1", "T", ("down", i)) for i in range(8)]
    t += [("od", "T", ("q", i)) for i in range(8)] + [("od", "T", ("dk", i)) for i in range(8)]
    t += [("od", "N", ("dv0", b, 4)) for b in range(4)] + [("od", "N", ("dv1", b, 4)) for b in range(4)]
    t += [("o4", "T", ("out", i)) for i in range(8)]
    for q in range(4):
        t += [("m2", "T", ("up", i)) for i in range(8)] + [("m2", "T", ("down", i)) for i in range(8)]
    return t


TILES = tile_plan()
NTILE = len(TILES)
PHASE = {}
for _t, (_ph, _, _) in enumerate(TILES):
    PHASE.setdefault(_ph, []).append(_t)
T_INDEX = {t: n for n, t in enumerate(t for t in range(NTILE) if TILES[t][1] == "T")}
N_WIDTH = {"vb": 512, "va": 128, "gi": 128, "vn": 256, "dv0": 512, "dv1": 512}

EVAC = {}
_count = {"act": 0, "dve": 0}
for _t in T_INDEX:
    _e = "dve" if TILES[_t][2][0] in ("out", "down") else "act"
    _count[_e] += 1
    EVAC[_t] = (_e, _count[_e])
EVAC_ACT, EVAC_DVE = _count["act"], _count["dve"]

NGROUP = 18
ADA_FIRST = 16
ADA_AT = {}


def _plan_ada():
    n = ADA_FIRST
    for phase in ("p1", "o1", "lin", "o2", "ev1", "o3", "m1"):
        for m, t in enumerate(PHASE[phase]):
            k = min(2 if phase == "p1" and m % 3 == 2 and n < 48 else 1, 8 * NGROUP - n)
            if k > 0:
                ADA_AT[t] = list(range(n, n + k))
                n += k
    assert n == 144


_plan_ada()
STAT_AFTER = {t for ph in ("o1", "o2", "o3", "m1", "o4", "m2") for t in PHASE[ph][-7:]}
FIN_AT = {}
for _t, _ids in ADA_AT.items():
    for _i in _ids:
        if _i % 8 == 7:
            FIN_AT.setdefault(_t + 1, []).append(_i // 8)


def attention_plan():
    plan, i, j, m, g = {}, 0, 0, 0, 0
    for phase in ("swa", "fgt", "nsa", "dsa", "dif"):
        steps = []
        for u in range(8):
            kinds = {"nsa": ("cmp", "sel", "win")}.get(phase, (phase,))
            for n, kind in enumerate(kinds):
                for qb in range(NT):
                    for half in range(2 if kind == "dif" else 1):
                        if kind == "swa":
                            slots = (0, 2) if qb else (1, 2)
                            nk = 128 * (slots[1] - slots[0])
                        elif kind == "cmp":
                            slots, nk = (0, 1), NCMP
                        else:
                            slots, nk = (0, qb + 1), 128 * (qb + 1)
                        turned = kind != "dif" or half == 1
                        steps.append(dict(kind=kind, u=u, qb=qb, half=half, slots=slots, nk=nk, i=i,
                                          j=j if turned else None, tr_after=j + 1, m=m, g=g,
                                          first=(n == 0), last=(n == len(kinds) - 1),
                                          end=turned and qb == NT - 1))
                        i += 1
                        j += turned
                m += 1
            g += 1
        plan[phase] = steps
    return plan


ATT = attention_plan()
STEP = [s for phase in ("swa", "fgt", "nsa", "dsa", "dif") for s in ATT[phase]]
LAG_TR, LAG_PV, LAG_OUT = 3, 5, 9


def aux_plan():
    order = [("q", 0)]
    for n in range(32 + LAG_OUT + 2):
        if n < 32 and n % 4 == 1 and n // 4 < 7:
            order.append(("q", n // 4 + 1))
        m = n - LAG_OUT - 1
        if 0 <= m < 32 and m % 4 == 3:
            order.append(("o", m // 4))
    return order


AUX = aux_plan()


def dsa_pre(u):
    return AUX.index(("q", u)) + 1


def dsa_post(u):
    return AUX.index(("o", u)) + 1


def program(nc, W, WA, X, CV, CC, OH, M2, UB, UC, OUT):
    ctx = ExitStack()
    with ctx:
        def sb(name, shape, dt=F32):
            return ctx.enter_context(nc.sbuf_tensor(name, shape, dt))

        def sem(name):
            return ctx.enter_context(nc.semaphore(name))

        arena_at = (nc.sbuf_base + 31) // 32 * 32
        slab = sb("arena", [P, ARENA])
        x = sb("x", [P, NC, S])
        hH = sb("h_hi", [P, NC * S], F32R)
        hL = sb("h_lo", [P, NC * S], F32R)
        wraw = sb("w_raw", [P, NSTREAM, BLK])
        wH = sb("w_hi", [P, NSTREAM, BLK], F32R)
        wL = sb("w_lo", [P, NSTREAM, BLK], F32R)
        biasB = sb("bias_near", [P, 16, 256])
        PT = sb("probs_t", [P, 2, NT, S])
        E = sb("logits", [P, 4, S])
        adaw = sb("ada_w", [P, NADA, BLK])
        acc = sb("ada_acc", [P, BLK])
        cv = sb("vectors", [P, NCOL])
        cc = sb("constants", [P, NCONST])
        frow = sb("f_rows", [8, S])
        adac = sb("ada_cols", [P, NGROUP * 8])
        cact = sb("c_act", [P, 16])
        ncol = sb("norm_cols", [P, 4, 8])
        st = sb("stats", [P, 24])
        rst = sb("rstd", [P, 4])
        nmx = sb("neg_max", [P, 4])
        rsum = sb("row_sum", [P, 4])
        ftok = sb("f_tokens", [P, NT, 8])
        k8 = sb("lru_rate", [P, 6, 8])
        dlam = sb("diff_lam", [P, 8])

        bank = [ctx.enter_context(nc.psum_tensor(f"bank{i}", [P, S], F32)) for i in range(8)]
        LB, SB, TB, OB, AB = bank[0:2], bank[2:4], bank[4:6], (bank[6], bank[1]), bank[7]
        NB = bank[0:4]

        def score_bank(s):
            return (bank[2], bank[3], bank[7] if s["kind"] == "dsa" else bank[0])[s["i"] % 3]

        t8 = PT[:, :, :, :].rearrange("p a b s -> p (a b) s")
        ident, ones = cc[:, C_ID:C_ID + P], cc[:, C_ONE:C_ONE + P]
        tri = cc[:, C_TRI:C_TRI + P]
        maskc = cc[:, C_MC:C_MC + NT * NCMP].rearrange("p (q n) -> p q n", q=NT)

        def ar(at, *dims):
            n = 1
            for d in dims:
                n *= d
            v = slab[:, at:at + n]
            if len(dims) == 2:
                return v.rearrange("p (a b) -> p a b", a=dims[0])
            if len(dims) == 3:
                return v.rearrange("p (a b c) -> p a b c", a=dims[0], b=dims[1])
            return v

        def col(name, a=0, b=None):
            lo, hi = COLS[name]
            return cv[:, lo + a:lo + b if b is not None else hi]

        def cmp_in(kv):
            return t8[:, 4 + 2 * kv:6 + 2 * kv, :].rearrange("p a s -> p (a s)")[:, 0:16 * 2 * NCMP]

        Q = ar(A_Q, 8, S)
        biasC = ar(A_BC, 8, NT, NCMP)
        biasA = ar(A_BA, 8, 256)

        gH = nc.alloc_sbuf_tensor_at("g_hi", [P, NC * S], F32R, offset=arena_at)
        gL = nc.alloc_sbuf_tensor_at("g_lo", [P, NC * S], F32R, offset=arena_at + NC * S * 4)

        consts_in = sem("consts_in")
        x_in = sem("x_in")
        m2_in = sem("m2_in")
        raw_in = [sem(f"raw_in{i}") for i in range(NSTREAM)]
        ada_in = [sem(f"ada_in{i}") for i in range(NADA)]
        hi_done = sem("w_hi_done")
        lo_done = sem("w_lo_done")
        tile_done = sem("tile_done")
        evac_act = sem("evac_act")
        evac_dve = sem("evac_dve")
        evac_sem = {"act": evac_act, "dve": evac_dve}
        nat_evac = sem("nat_evac")
        ada_used = sem("ada_used")
        ada_sum = sem("ada_sum")
        ada_add = sem("ada_add")
        c_tanh = sem("c_silu")
        dve_chain = sem("dve_chain")
        act_chain = sem("act_chain")
        bias_mm = sem("bias_mm")
        bias_evac = sem("bias_evac")
        bias_out = sem("bias_stored")
        biasA_in, biasB_in, biasC_in = sem("bias_swa_in"), sem("bias_near_in"), sem("bias_cmp_in")
        x_set = sem("x_set")
        n_sq, n_stat, n_var, n_root = sem("norm_sq"), sem("norm_stat"), sem("norm_var"), sem("norm_root")
        n_diag, n_bcast, n_t = sem("norm_diag"), sem("norm_bcast"), sem("norm_t")
        h_hi, h_lo = sem("h_hi_done"), sem("h_lo_done")
        sq_done, g_hi_s, g_lo_s = sem("relu_sq"), sem("g_hi_done"), sem("g_lo_done")
        f_z, f_nz, f_e, f_row = sem("f_z"), sem("f_neg_abs"), sem("f_exp"), sem("f_row")
        f_tr, f_tok = sem("f_transposed"), sem("f_tokens_done")
        nf_diag, nf_mm, nf_copy = sem("nf_diag"), sem("nf_mm"), sem("nf_copy")
        at_sc, at_max, at_pr, at_nm = sem("scores"), sem("row_max"), sem("probs"), sem("probs_scaled")
        at_tr, at_pt, at_pv, at_oe = sem("probs_turned"), sem("pt_copied"), sem("pv_done"), sem("out_copied")
        aux_mm, aux_ev = sem("aux_mm"), sem("aux_evac")
        ix_s, ix_r, ix_a = sem("index_scores"), sem("index_relu"), sem("index_added")
        gi_done = sem("gates_done")
        lat_ev, lat_sq, lat_st, lat_v, lat_r = (sem("lat_copied"), sem("lat_sq"), sem("lat_stat"),
                                                sem("lat_var"), sem("lat_root"))
        lat_t, lat_n, lat_tt, lat_done = sem("lat_turned"), sem("lat_token"), sem("lat_back"), sem("lat_done")
        b_add, b_hi, b_lo = sem("cmp_in"), sem("cmp_hi"), sem("cmp_lo")
        hid_done, kc_mm, kc_done = sem("cmp_hidden"), sem("cmp_mm"), sem("cmp_done")
        l_conv, l_mm, l_sig, l_ixc, l_te, l_m, l_sq, l_y = (sem("lru_conv"), sem("lru_mm"), sem("lru_sig"),
                                                            sem("lru_ixc"), sem("lru_exp"), sem("lru_m"),
                                                            sem("lru_root"), sem("lru_y"))
        l_lam, l_lam2 = sem("lru_lam"), sem("lru_lam2")
        l_zero = sem("lru_zero")
        dl_p, dl_mm, dl_e, dl_done = sem("dlam_prod"), sem("dlam_sum"), sem("dlam_exp"), sem("dlam_done")
        d_sq, d_st, d_v, d_r, d_diag, d_bc, d_y = (sem("diff_sq"), sem("diff_stat"), sem("diff_var"),
                                                   sem("diff_root"), sem("diff_diag"), sem("diff_bcast"),
                                                   sem("diff_y"))
        out_s = sem("out_stored")

        X_SETS = {"o3": 1, "m1": 2, "o4": 3, "m2": 4}

        block = ctx.enter_context(nc.Block())

        H_ORDER = ["n0", "y1", "n1", "xc", "y2", "n2", "y3", "n3", "n4", "y4", "n5"]
        h_base = {name: 8 * n for n, name in enumerate(H_ORDER)}
        H_OF_PHASE = {"p1": "n0", "o1": "y1", "lin": "n1", "o2": "y2", "ev1": "n2", "o3": "y3", "m1": "n3",
                      "od": "n4", "o4": "y4", "m2": "n5"}

        @block.sync
        def _(sp):
            sp.dma_start(cv[:, :], CV).then_inc(consts_in, 16)
            sp.dma_start(cc[:, :], CC).then_inc(consts_in, 16)
            sp.dma_start(slab[0:34, 0:OHW], OH).then_inc(consts_in, 16)
            sp.dma_start(x[:, :, :], X.rearrange("p (c s) -> p c s", c=NC)).then_inc(x_in, 16)

            def ada_block(n):
                if n >= NADA:
                    sp.wait_ge(ada_used, n - NADA + 1)
                sp.dma_start(adaw[:, n % NADA, :], WA[n]).then_inc(ada_in[n % NADA], 16)

            def weight_block(t):
                if t >= NSTREAM:
                    sp.wait_ge(lo_done, t - NSTREAM + 1)
                sp.dma_start(wraw[:, t % NSTREAM, :], W[t]).then_inc(raw_in[t % NSTREAM], 16)

            def skew(U, at, step, pattern):
                return bass.AP(U.tensor, U.offset + at, [[step, 16]] + pattern)

            for n in range(4):
                ada_block(n)
            sp.wait_ge(bias_evac, 1)
            u = slab[0:24, A_U:A_U + BAND]
            sp.dma_start(UB, u.unsqueeze(1).to_broadcast([24, 16, BAND])).then_inc(bias_out, 16)
            sp.dma_start(UC, slab[0:24, A_U + BAND:A_U + BAND + CBAND]).then_inc(bias_out, 16)
            for n in range(4, ADA_FIRST):
                ada_block(n)
            for t in range(NTILE):
                weight_block(t)
                if 2 <= t < 10:
                    sp.wait_ge(bias_out, 32)
                    a = t - 2
                    at = slice(16 * a, 16 * a + 16)
                    band = 16 * BAND
                    sp.dma_start(biasA[at], skew(UB, P - 1 - 16 * a, BAND - 1,
                                                 [[band, 8], [1, 256]])).then_inc(biasA_in, 16)
                    sp.dma_start(biasB[at], skew(UB, 8 * band + P - 1 - 16 * a, BAND - 1,
                                                 [[band, 16], [1, 256]])).then_inc(biasB_in, 16)
                    for qb in range(NT):
                        sp.dma_start(biasC[at, :, qb, :], skew(UC, 8 * CBAND + 31 - 8 * qb - a, 62,
                                                               [[CBAND, 8], [1, NCMP]])).then_inc(biasC_in, 16)
                for n in ADA_AT.get(t, []):
                    ada_block(n)
                if t == PHASE["ev1"][1]:
                    sp.wait_ge(h_lo, h_base["n2"] + 8)
                    sp.dma_start(ar(A_M2, M2W), M2).then_inc(m2_in, 16)
            for c in range(NC):
                sp.wait_ge(h_hi, h_base["n5"] + 8 + c + 1)
                sp.dma_start(OUT[:, c, :], t8[:, c, :]).then_inc(out_s, 16)
            sp.wait_ge(out_s, 16 * NC)

        @block.gpsimd
        def _(pool):
            for t in range(NTILE):
                for name, phase in (("n3", "m1"), ("n4", "od"), ("n5", "m2")):
                    if t == min(PHASE[phase][0] + 2, NTILE):
                        for c in range(NC):
                            pool.wait_ge(h_hi, h_base[name] + c + 1)
                            nc.gpsimd.tensor_tensor(hL[:, c * S:(c + 1) * S], E[:, c % 4, :],
                                                    hH[:, c * S:(c + 1) * S].bitcast(F32),
                                                    ALU.subtract).then_inc(h_lo, 1)
                pool.wait_ge(hi_done, t + 1)
                s = t % NSTREAM
                nc.gpsimd.tensor_tensor(wL[:, s, :], wraw[:, s, :], wH[:, s, :].bitcast(F32),
                                        ALU.subtract).then_inc(lo_done, 1)

        @block.scalar
        def _(act):
            chain = [0]
            nexthi = [0]
            aux = [0]

            def link(ins):
                chain[0] += 1
                ins.then_inc(act_chain, 1)
                act.wait_ge(act_chain, chain[0])

            def ahead(upto):
                while nexthi[0] <= min(upto, NTILE - 1):
                    t = nexthi[0]
                    act.wait_ge(raw_in[t % NSTREAM], 16 * (t // NSTREAM + 1))
                    if t >= NSTREAM:
                        act.wait_ge(tile_done, t - NSTREAM + 1)
                    nc.scalar.activation(wH[:, t % NSTREAM, :], wraw[:, t % NSTREAM, :],
                                         ACT.Copy).then_inc(hi_done, 1)
                    nexthi[0] += 1

            def copy(out, in_, scale=1.0):
                return nc.scalar.activation(out, in_, ACT.Copy, scale=scale)

            def bias_build():
                act.wait_ge(bias_mm, 1)
                copy(slab[0:24, A_U:A_U + BAND], SB[0][0:24, 0:BAND])
                copy(slab[0:24, A_U + BAND:A_U + BAND + 496], SB[1][0:24, 0:496])
                copy(slab[0:24, A_U + BAND + 496:A_U + BAND + CBAND], TB[0][0:24, 0:496]).then_inc(bias_evac, 1)

            def norm(n, name, sets_x):
                if n == 0:
                    act.wait_ge(x_in, 16)
                    for c in range(NC):
                        square(c)
                else:
                    act.wait_ge(evac_dve, resid[0])
                    square(NC - 1)
                act.wait_ge(n_var, n + 1)
                nc.scalar.activation(rst[:, :], st[:, 0:4], ACT.Sqrt).then_inc(n_root, 1)
                for c in range(NC):
                    act.wait_ge(n_t, NC * n + c + 1)
                    if name is None:
                        nc.scalar.activation(t8[:, c, :], t8[:, c, :], ACT.Identity, bias=ncol[:, 1, c:c + 1],
                                             scale=ncol[:, 0, c:c + 1]).then_inc(h_hi, 1)
                        continue
                    if c >= 4:
                        act.wait_ge(h_lo, h_base[name] + c - 3)
                    link(nc.scalar.activation(E[:, c % 4, :], t8[:, c, :], ACT.Identity, bias=ncol[:, 1, c:c + 1],
                                              scale=ncol[:, 0, c:c + 1]))
                    copy(hH[:, c * S:(c + 1) * S], E[:, c % 4, :]).then_inc(h_hi, 1)
                if sets_x:
                    for c in range(NC):
                        ins = nc.scalar.activation(x[:, c, :], t8[:, c, :], ACT.Identity, bias=ncol[:, 3, c:c + 1],
                                                   scale=ncol[:, 2, c:c + 1])
                    sets[0] += 1
                    ins.then_inc(x_set, 1)
                    act.wait_ge(x_set, sets[0])

            sets = [0]

            def square(c):
                nc.scalar.activation(t8[:, c, :], x[:, c, :], ACT.Square).then_inc(n_sq, 1)

            resid = [0]

            def split_y():
                for c in range(NC):
                    copy(hH[:, c * S:(c + 1) * S], Q[:, c, :]).then_inc(h_hi, 1)

            up = [0]

            def up_hi():
                n = up[0]
                act.wait_ge(sq_done, n + 1)
                copy(gH[:, (n % 8) * S:(n % 8 + 1) * S], t8[:, 2 + n % 2, :]).then_inc(g_hi_s, 1)
                up[0] += 1

            ups = [0]

            def tiles(phase):
                for t in PHASE[phase]:
                    _, kind, what = TILES[t]
                    ahead(t + 2)
                    name = what[0]
                    if kind == "T" and EVAC[t][0] == "dve":
                        resid[0] = EVAC[t][1]
                        if name == "down" and what[1] == 0:
                            up_hi()
                        if t in STAT_AFTER:
                            act.wait_ge(evac_dve, EVAC[t][1] - 1)
                            square(what[1] - 1)
                        continue
                    if kind == "T":
                        act.wait_ge(tile_done, t + 1)
                        ps, i = LB[T_INDEX[t] % 2], what[1]
                        if name == "q":
                            ins = copy(Q[:, i, :], ps[:, :], DSCALE)
                        elif name == "ak":
                            ins = copy(ar(A_AK, S), ps[:, :])
                        elif name == "bk":
                            ins = copy(ar(A_BK, 4, S)[:, i, :], ps[:, :])
                        elif name == "f":
                            nc.scalar.activation(frow[:, :], ps[0:8, :], ACT.Identity,
                                                 bias=col("bf")[0:8, :]).then_inc(evac_act, 1)
                            continue
                        elif name == "gate":
                            ins = nc.scalar.activation(ar(A_GT, 8, S)[:, i, :], ps[:, :], ACT.Silu)
                        elif name == "xr":
                            ins = copy(ar(A_XR, 8, XRW)[:, i, 3:XRW], ps[:, :])
                        elif name == "lgate":
                            ins = nc.scalar.activation(ar(A_LG, 8, S)[:, i, :], ps[:, :], ACT.Silu)
                        elif name == "ik":
                            ins = copy(ar(A_IK, S), ps[:, :])
                        elif name == "iq":
                            ins = copy(ar(A_IQ, 4, S)[:, i, :], ps[:, :])
                        elif name == "kvl":
                            ins = nc.scalar.activation(t8[:, 0, :], ps[:, :], ACT.Copy, scale=1.0)
                        elif name == "ks":
                            ins = copy(ar(A_KS, S), ps[:, :])
                        elif name == "kw":
                            ins = copy(ar(A_KW, S), ps[:, :])
                        elif name == "kc2":
                            d = ar(A_KC2, 4, S)
                            copy(d[0:HD, i, :], ps[0:HD, :])
                            ins = copy(d[HD:P, i, 0:S - 1], ps[HD:P, 1:S])
                        elif name == "dk":
                            ins = copy(ar(A_DK, 8, S)[:, i, :], ps[:, :])
                        elif name == "up":
                            n = ups[0]
                            if n >= 2:
                                act.wait_ge(sq_done, n - 1)
                            nc.scalar.activation(t8[:, n % 2, :], ps[:, :], ACT.Relu).then_inc(evac_act, 1)
                            ups[0] += 1
                            if i > 0:
                                up_hi()
                            continue
                        ins.then_inc(evac_act, 1)
                    elif kind == "N" and what[1] == what[2] - 1:
                        act.wait_ge(tile_done, t + 1)
                        for tb in range(NT):
                            ps = NB[tb]
                            if name == "vb":
                                ins = copy(ar(A_VB, NT, S)[:, tb, :], ps[:, :])
                            elif name == "va":
                                ins = copy(ar(A_VA, NT, P)[:, tb, :], ps[:, 0:P])
                            elif name == "gi":
                                gi = ar(A_GI, NT, 32)
                                nc.scalar.activation(gi[:, tb, 0:24], ps[:, 0:24], ACT.Sigmoid)
                                ins = copy(gi[:, tb, 24:32], ps[:, 24:32], 8 ** -0.5 * 64 ** -0.5)
                            elif name == "vn":
                                ins = copy(ar(A_VN, NT, 256)[:, tb, :], ps[:, 0:256])
                            else:
                                k = int(name[2])
                                ins = copy(ar(A_DV, NT, 1024)[:, tb, 512 * k:512 * k + 512], ps[:, :])
                        ins.then_inc(nat_evac, 1)
                    if name == "kvl":
                        latent_act()

            def latent_act():
                act.wait_ge(evac_act, EVAC[PHASE["ev2"][0]][1])
                nc.scalar.activation(t8[:, 4, :], t8[:, 0, :], ACT.Square).then_inc(lat_sq, 1)
                link(nc.scalar.activation(t8[:, 5, :], t8[:, 0, :], ACT.Copy, scale=col("kvn")))
                act.wait_ge(lat_v, 1)
                nc.scalar.activation(rst[:, :], st[:, 0:4], ACT.Sqrt).then_inc(lat_r, 1)

            def latent_act2():
                act.wait_ge(lat_t, 1)
                act.wait_ge(lat_r, 1)
                for tb in range(NT):
                    ins = nc.scalar.activation(ar(A_CKN, NT, P)[:, tb, :], TB[0][:, tb * P:(tb + 1) * P],
                                               ACT.Copy, scale=rst[:, tb:tb + 1])
                ins.then_inc(lat_n, 1)
                act.wait_ge(lat_tt, 1)
                copy(ar(A_CKT, S), TB[1][:, :]).then_inc(lat_done, 1)

            def f_rows():
                act.wait_ge(f_nz, 1)
                nc.scalar.activation(E[0:8, 1, :], E[0:8, 0, :], ACT.Exp).then_inc(f_e, 1)
                act.wait_ge(f_tr, 1)
                copy(ftok[:, :, :], TB[0][:, 0:32].rearrange("p (t h) -> p t h", t=NT)).then_inc(f_tok, 1)

            def attend(phase):
                steps = ATT[phase]

                def exps(s):
                    act.wait_ge(at_max, s["i"] + 1)
                    i, n = s["i"] % 4, s["nk"] + (s["kind"] == "swa")
                    nc.scalar.activation(E[:, i, 0:n], E[:, i, 0:n], ACT.Exp, bias=nmx[:, i:i + 1],
                                         accum_out=rsum[:, i:i + 1]).then_inc(at_pr, 1)

                def turned_copy(s):
                    if s["j"] is None:
                        return
                    act.wait_ge(at_tr, s["j"] + 1)
                    if s["qb"] == 0 and s["m"] >= 2:
                        act.wait_ge(at_pv, s["m"] - 1)
                    a, b = s["slots"]
                    rows = NCMP if s["kind"] == "cmp" else P
                    dst = PT[0:rows, s["m"] % 2, a:b, s["qb"] * P:(s["qb"] + 1) * P]
                    src = TB[s["j"] % 2][0:rows, a * P:b * P].rearrange("p (k q) -> p k q", q=P)
                    copy(dst, src).then_inc(at_pt, 1)

                def nf(h):
                    act.wait_ge(nf_mm, h + 1)
                    if h >= 1:
                        act.wait_ge(at_max, ATT["fgt"][4 * (h - 1)]["i"])
                    copy(ar(A_BA + 1024 * (h % 2), S), AB[:, :]).then_inc(nf_copy, 1)

                def aux_evac(dst, src):
                    aux[0] += 1
                    act.wait_ge(aux_mm, aux[0])
                    copy(dst, src).then_inc(aux_ev, 1)

                if phase == "fgt":
                    nf(0)
                if phase == "dsa":
                    aux_evac(ar(A_QL, S), LB[0][:, :])
                for n in range(len(steps) + LAG_OUT + 2):
                    if n < len(steps):
                        s = steps[n]
                        if phase == "fgt" and s["qb"] == 0 and s["u"] < 7:
                            nf(s["u"] + 1)
                        if phase == "dsa" and s["qb"] == 1 and s["u"] < 7:
                            aux_evac(ar(A_QL + S * ((s["u"] + 1) % 2), S), LB[0][:, :])
                        exps(s)
                    if 0 <= n - LAG_TR < len(steps):
                        turned_copy(steps[n - LAG_TR])
                    m = n - LAG_OUT - 1
                    if phase == "dsa" and 0 <= m < len(steps) and steps[m]["end"]:
                        u = steps[m]["u"]
                        b = HD * (u % 2)
                        aux_evac(Q[b:b + HD, 4 + u // 2, :], LB[0][b:b + HD, :])

            act.wait_ge(consts_in, 48)
            nc.scalar.activation(cact[:, :], cv[:, 0:16], ACT.Silu).then_inc(c_tanh, 1)
            bias_build()
            ahead(1)
            norm(0, "n0", False)
            act.wait_ge(bias_out, 32)
            tiles("p1")
            f_rows()
            attend("swa")
            attend("fgt")
            act.wait_ge(at_oe, ATT["fgt"][-1]["g"] + 1)
            split_y()
            tiles("o1")
            norm(1, "n1", False)
            tiles("lin")
            act.wait_ge(l_lam, 1)
            nc.scalar.activation(k8[:, 1, :], k8[:, 0, :], ACT.Exp).then_inc(l_lam2, 1)
            t_g = PHASE["lcore"][0]
            ahead(t_g + 2)
            act.wait_ge(tile_done, t_g)
            for c in range(NC):
                act.wait_ge(l_conv, c + 1)
                copy(hH[:, c * S:(c + 1) * S], ar(A_XC, 8, S)[:, c, :]).then_inc(h_hi, 1)
            for c in range(NC):
                if c < NC - 1:
                    act.wait_ge(l_mm, 2 * c + 2)
                else:
                    act.wait_ge(tile_done, t_g + 2)
                nc.scalar.activation(t8[:, c, :], NB[2 * (c % 2)][:, :], ACT.Sigmoid, bias=col("ba", c, c + 1))
                if c >= 4:
                    act.wait_ge(l_ixc, c - 3)
                nc.scalar.activation(E[:, c % 4, :], NB[2 * (c % 2) + 1][:, :], ACT.Sigmoid,
                                     bias=col("bx", c, c + 1)).then_inc(l_sig, 1)
            ahead(t_g + 3)
            act.wait_ge(l_lam, 2)
            act.wait_ge(l_sig, NC)
            for c in range(NC):
                nc.scalar.activation(ar(A_XR, 8, S)[:, c, :], t8[:, c, :], ACT.Exp, scale=k8[:, 5, c:c + 1])
                nc.scalar.activation(t8[:, c, :], t8[:, c, :], ACT.Tanh,
                                     scale=k8[:, 4, c:c + 1]).then_inc(l_te, 1)
            for c in range(NC):
                act.wait_ge(l_m, c + 1)
                nc.scalar.activation(t8[:, c, :], t8[:, c, :], ACT.Sqrt).then_inc(l_sq, 1)
            for c in range(NC):
                act.wait_ge(l_y, c + 1)
                copy(hH[:, c * S:(c + 1) * S], ar(A_XC, 8, S)[:, c, :]).then_inc(h_hi, 1)
            tiles("o2")
            norm(2, "n2", True)
            tiles("ev1")
            n = 0
            for qb in range(1, NT):
                for j in range(8):
                    act.wait_ge(ix_s, n + 1)
                    if n >= 4:
                        act.wait_ge(ix_a, n - 3)
                    nc.scalar.activation(E[:, n % 4, 0:P * (qb + 1)], SB[n % 2][:, 0:P * (qb + 1)],
                                         ACT.Relu).then_inc(ix_r, 1)
                    n += 1
            tiles("ev2")
            latent_act2()
            act.wait_ge(tile_done, PHASE["ev2"][-1] + 1)
            for kv in range(2):
                act.wait_ge(b_add, kv + 1)
                copy(hH[:, 1024 * kv:1024 * kv + 992], cmp_in(kv)).then_inc(b_hi, 1)
            for kv in range(2):
                for b in range(4):
                    ahead(PHASE["ev3"][4 * kv + b] + 2)
                act.wait_ge(tile_done, PHASE["ev3"][4 * kv + 3] + 1)
                for hc in range(2):
                    ins = nc.scalar.activation(ar(A_HID, 4, 62)[:, 2 * kv + hc, :], LB[hc][:, 0:62],
                                               ACT.Gelu_apprx_tanh)
                ins.then_inc(hid_done, 1)
            act.wait_ge(kc_mm, 1)
            copy(ar(A_KCT, 32)[0:HD, 0:NCMP], SB[0][0:HD, 0:NCMP])
            copy(ar(A_KCT, 32)[HD:P, 0:NCMP], SB[0][HD:P, NCMP:2 * NCMP])
            copy(ar(A_VCN, P)[0:NCMP, :], SB[1][0:NCMP, 0:P]).then_inc(kc_done, 1)
            attend("nsa")
            attend("dsa")
            act.wait_ge(aux_ev, 16)
            split_y()
            tiles("o3")
            norm(3, "n3", True)
            tiles("m1")
            norm(4, "n4", True)
            tiles("od")
            act.wait_ge(dl_mm, 1)
            nc.scalar.activation(dlam[:, 4:6], AB[:, 0:2], ACT.Exp).then_inc(dl_e, 1)
            attend("dif")
            act.wait_ge(at_oe, ATT["dif"][-1]["g"] + 1)
            for h in range(8):
                nc.scalar.activation(t8[:, h, :], Q[:, h, :], ACT.Square).then_inc(d_sq, 1)
            act.wait_ge(d_v, 1)
            nc.scalar.activation(k8[:, 0:4, :].rearrange("p a b -> p (a b)"), k8[:, 0:4, :].rearrange("p a b -> p (a b)"),
                                 ACT.Sqrt).then_inc(d_r, 1)
            for c in range(NC):
                act.wait_ge(d_y, c + 1)
                copy(hH[:, c * S:(c + 1) * S], Q[:, c, :]).then_inc(h_hi, 1)
            tiles("o4")
            norm(5, "n5", True)
            tiles("m2")
            norm(6, None, False)

        @block.vector
        def _(dve):
            V = nc.vector
            chain = [0]
            pending = []

            def link(ins):
                chain[0] += 1
                ins.then_inc(dve_chain, 1)
                dve.wait_ge(dve_chain, chain[0])

            def ada_bias():
                g = pending.pop()
                dve.wait_ge(ada_sum, g + 1)
                V.tensor_tensor(adac[:, 8 * g:8 * g + 8], AB[:, 0:8], col("adab", 8 * g, 8 * g + 8),
                                ALU.add).then_inc(ada_add, 1)

            def ada_block(n):
                if n % 8 == 0 and pending:
                    ada_bias()
                dve.wait_ge(ada_in[n % NADA], 16 * (n // NADA + 1))
                c = (0 if n < 48 else 8) + n % 8
                if n:
                    dve.wait_ge(ada_used, n)
                if n % 8 == 0:
                    if n:
                        dve.wait_ge(ada_sum, n // 8)
                    ins = V.tensor_scalar(acc[:, :], adaw[:, n % NADA, :], cact[:, c:c + 1], None, ALU.mult)
                else:
                    ins = V.scalar_tensor_tensor(acc[:, :], adaw[:, n % NADA, :], cact[:, c:c + 1], acc[:, :],
                                                 ALU.mult, ALU.add)
                ins.then_inc(ada_used, 1)
                if n % 8 == 7:
                    pending.append(n // 8)

            def ada_slot(t):
                if pending and t in after_fin:
                    ada_bias()
                for n in ADA_AT.get(t, []):
                    ada_block(n)

            after_fin = {t + 1 for t in FIN_AT}

            def sub(out, a, b):
                return V.tensor_tensor(out, a, b, ALU.subtract)

            def low(c, src):
                return sub(hL[:, c * S:(c + 1) * S], src, hH[:, c * S:(c + 1) * S].bitcast(F32))

            def acol(g):
                return adac[:, 8 * g:8 * g + 8]

            def cols(shift, scale, g, b, fg, fb):
                dve.wait_ge(ada_add, max(shift, scale) + 1)
                dve.wait_ge(consts_in, 48)
                link(V.scalar_tensor_tensor(ncol[:, 0, :], acol(scale), 1.0, g, ALU.add, ALU.mult))
                if b is None:
                    link(V.tensor_copy(ncol[:, 1, :], acol(shift)))
                else:
                    link(V.scalar_tensor_tensor(ncol[:, 1, :], acol(scale), 1.0, b, ALU.add, ALU.mult))
                    link(V.tensor_tensor(ncol[:, 1, :], ncol[:, 1, :], acol(shift), ALU.add))
                if fg is not None:
                    link(V.tensor_scalar(ncol[:, 2, :], fg, ALPHA, None, ALU.mult))
                    if fb is None:
                        link(V.memset(ncol[:, 3, :], 0.0))
                    else:
                        link(V.tensor_scalar(ncol[:, 3, :], fb, ALPHA, None, ALU.mult))

            def norm(n, name, eps, centred):
                dve.wait_ge(n_stat, n + 1)
                if not centred:
                    link(V.tensor_scalar(st[:, 8:12], TB[0][:, 0:4], 1.0 / D, eps, ALU.mult, ALU.add))
                else:
                    link(V.tensor_scalar(st[:, 4:8], TB[0][:, 4:8], 1.0 / D, None, ALU.mult))
                    link(V.tensor_tensor(st[:, 12:16], st[:, 4:8], st[:, 4:8], ALU.mult))
                    link(V.scalar_tensor_tensor(st[:, 16:20], TB[0][:, 0:4], 1.0 / D, st[:, 12:16], ALU.mult,
                                                ALU.subtract))
                    link(V.tensor_scalar(st[:, 8:12], st[:, 16:20], eps, None, ALU.add))
                V.reciprocal(st[:, 0:4], st[:, 8:12]).then_inc(n_var, 1)
                dve.wait_ge(n_root, n + 1)
                if centred:
                    link(V.tensor_tensor(st[:, 20:24], st[:, 4:8], rst[:, :], ALU.mult))
                for tb in range(NT):
                    ins = V.tensor_scalar(E[:, 0, tb * P:(tb + 1) * P], ident, rst[:, tb:tb + 1], None, ALU.mult)
                    if centred:
                        ins = V.tensor_scalar(E[:, 1, tb * P:(tb + 1) * P], ident, st[:, 20 + tb:21 + tb], None,
                                              ALU.mult)
                ins.then_inc(n_diag, 1)
                dve.wait_ge(n_bcast, n + 1)
                for c in range(NC + 1):
                    if c < NC:
                        if centred:
                            link(V.tensor_tensor(t8[:, c, :], x[:, c, :], SB[0][:, :], ALU.mult))
                            V.tensor_tensor(t8[:, c, :], t8[:, c, :], SB[1][:, :], ALU.subtract).then_inc(n_t, 1)
                        else:
                            V.tensor_tensor(t8[:, c, :], x[:, c, :], SB[0][:, :], ALU.mult).then_inc(n_t, 1)
                    if c > 0 and name is not None and not centred:
                        dve.wait_ge(h_hi, h_base[name] + c)
                        low(c - 1, E[:, (c - 1) % 4, :]).then_inc(h_lo, 1)

            def split_y(name):
                for c in range(NC):
                    dve.wait_ge(h_hi, h_base[name] + c + 1)
                    low(c, Q[:, c, :]).then_inc(h_lo, 1)

            up = [0, 0]

            def up_lo():
                n = up[1]
                dve.wait_ge(g_hi_s, n + 1)
                sub(gL[:, (n % 8) * S:(n % 8 + 1) * S], t8[:, 2 + n % 2, :],
                    gH[:, (n % 8) * S:(n % 8 + 1) * S].bitcast(F32)).then_inc(g_lo_s, 1)
                up[1] += 1

            def tiles(phase, gate=None, hook=None):
                for t in PHASE[phase]:
                    _, kind, what = TILES[t]
                    if what[0] == "down" and what[1] == 0:
                        up_lo()
                    ada_slot(t)
                    if kind == "T" and EVAC[t][0] == "dve":
                        c = what[1]
                        dve.wait_ge(tile_done, t + 1)
                        if phase in X_SETS:
                            dve.wait_ge(x_set, X_SETS[phase])
                        if EVAC[t][1] > 1:
                            dve.wait_ge(evac_dve, EVAC[t][1] - 1)
                        V.scalar_tensor_tensor(x[:, c, :], LB[T_INDEX[t] % 2][:, :], gate[:, c:c + 1], x[:, c, :],
                                               ALU.mult, ALU.add).then_inc(evac_dve, 1)
                    elif what[0] == "up":
                        n = up[0]
                        dve.wait_ge(evac_act, EVAC[t][1])
                        if n >= 2:
                            dve.wait_ge(g_lo_s, n - 1)
                        V.tensor_tensor(t8[:, 2 + n % 2, :], t8[:, n % 2, :], t8[:, n % 2, :],
                                        ALU.mult).then_inc(sq_done, 1)
                        up[0] += 1
                        if what[1] > 0:
                            up_lo()
                    elif hook:
                        hook(t, what)
                if pending and 8 * pending[0] + 7 in ADA_AT.get(t - 1, []):
                    ada_bias()

            def log1p_series(e, s, s2, p):
                link(V.tensor_scalar(s, e, 2.0, None, ALU.add))
                link(V.reciprocal(s2, s))
                link(V.tensor_tensor(s, s2, e, ALU.mult))
                link(V.tensor_tensor(s2, s, s, ALU.mult))
                link(V.tensor_scalar(p, s2, 1.0 / 15, None, ALU.mult))
                for k in (13, 11, 9, 7, 5, 3):
                    link(V.scalar_tensor_tensor(p, p, 1.0 / k, s2, ALU.add, ALU.mult))
                link(V.scalar_tensor_tensor(s, p, 1.0, s, ALU.add, ALU.mult))

            def f_rows():
                dve.wait_ge(evac_act, EVAC[[t for t in PHASE["p1"] if TILES[t][2][0] == "f"][0]][1])
                V.scalar_tensor_tensor(E[0:8, 0, :], frow[:, :], -1.0, frow[:, :], ALU.mult, ALU.min).then_inc(f_nz, 1)
                dve.wait_ge(f_e, 1)
                s, s2, p = E[0:8, 0, :], E[0:8, 2, :], E[0:8, 3, :]
                log1p_series(E[0:8, 1, :], s, s2, p)
                link(V.tensor_scalar(frow[:, :], frow[:, :], 0.0, None, ALU.min))
                link(V.scalar_tensor_tensor(s2, s, -2.0, frow[:, :], ALU.mult, ALU.add))
                link(V.memset(p, 1.0))
                V.tensor_tensor_scan(frow[:, :], p, s2, 0.0, ALU.mult, ALU.add).then_inc(f_row, 1)
                dve.wait_ge(f_row, 1)
                dve.wait_ge(f_tok, 1)

            def attend(phase):
                steps = ATT[phase]

                def nf_diag_rows(h):
                    if h:
                        dve.wait_ge(nf_mm, h)
                    V.tensor_scalar(ar(A_AK, S)[0:8, :], frow[:, :], ident[0:8, h:h + 1], -1.0, ALU.mult,
                                    ALU.mult).then_inc(nf_diag, 1)

                def nf_masked(h):
                    dve.wait_ge(nf_copy, h + 1)
                    a = ar(A_BA + 1024 * (h % 2), NT, P)
                    b = ar(A_BA + 1024 * (h % 2) + S, NT, P)
                    link(V.tensor_tensor(b, a, tri.unsqueeze(1).to_broadcast([P, NT, P]), ALU.add))

                def logits(s):
                    i, nk, qb, kind, u = s["i"], s["nk"], s["qb"], s["kind"], s["u"]
                    if i >= 4:
                        dve.wait_ge(at_tr, STEP[i - 4]["tr_after"])
                    dve.wait_ge(at_sc, i + 1)
                    e, ps = E[:, i % 4, :], score_bank(s)
                    near = max(0, nk - 256)
                    if kind == "swa":
                        h = u // 2 + 4 * (u % 2)
                        V.tensor_tensor(e[:, 0:nk], ps[:, 0:nk], biasA[:, h, 256 - nk:256], ALU.add)
                        link(V.tensor_copy(e[:, nk:nk + 1], col("sink", h, h + 1)))
                        nk += 1
                    elif kind == "fgt":
                        a, b = ar(A_BA + 1024 * (u % 2), S), ar(A_BA + 1024 * (u % 2) + S, S)
                        d = nk - P
                        if d:
                            V.scalar_tensor_tensor(e[:, 0:d], ps[:, 0:d], ftok[:, qb, u:u + 1], a[:, 0:d], ALU.add,
                                                   ALU.add)
                        link(V.scalar_tensor_tensor(e[:, d:nk], ps[:, d:nk], ftok[:, qb, u:u + 1], b[:, d:nk],
                                                    ALU.add, ALU.add))
                    elif kind == "cmp":
                        h = u // 2 + 4 * (u % 2)
                        link(V.tensor_tensor(e[:, 0:nk], ps[:, 0:nk], biasC[:, h, qb, :], ALU.add))
                    else:
                        h = {"sel": u // 2 + 4 * (u % 2), "win": u // 2 + 4 * (u % 2), "dsa": 8 + u,
                             "dif": 2 * u + s["half"]}[kind]
                        if kind == "dsa" and qb:
                            pen = ar(A_PEN + (0, 0, 256, 640)[qb], nk)
                            if near:
                                V.scalar_tensor_tensor(e[:, 0:near], ps[:, 0:near], col("t31", h, h + 1),
                                                       pen[:, 0:near], ALU.add, ALU.add)
                            link(V.tensor_tensor(e[:, near:nk], ps[:, near:nk], pen[:, near:nk], ALU.add))
                            link(V.tensor_tensor(e[:, near:nk], e[:, near:nk], biasB[:, h, 0:256], ALU.add))
                        else:
                            if near:
                                V.tensor_scalar(e[:, 0:near], ps[:, 0:near], col("t31", h, h + 1), None, ALU.add)
                            link(V.tensor_tensor(e[:, near:nk], ps[:, near:nk], biasB[:, h, 256 - (nk - near):256],
                                                 ALU.add))
                    V.tensor_reduce(nmx[:, i % 4:i % 4 + 1], e[:, 0:nk], AX.X, ALU.max, negate=True).then_inc(at_max, 1)

                def scale(s):
                    i, nk, kind = s["i"] % 4, s["nk"], s["kind"]
                    e, r = E[:, i, 0:nk], rsum[:, i:i + 1]
                    dve.wait_ge(at_pr, s["i"] + 1)
                    link(V.tensor_scalar(r, r, 1e-30, None, ALU.max))
                    link(V.reciprocal(r, r))
                    if kind in ("cmp", "sel", "win"):
                        h = s["u"] // 2 + 4 * (s["u"] % 2)
                        b = ("cmp", "sel", "win").index(kind)
                        gate = ar(A_GI, NT, 32)[:, s["qb"], 3 * h + b:3 * h + b + 1]
                        if kind == "cmp":
                            link(V.tensor_tensor(r, r, gate, ALU.mult))
                            ins = V.scalar_tensor_tensor(e, e, r, maskc[:, s["qb"], :], ALU.mult, ALU.mult)
                        else:
                            ins = V.tensor_scalar(e, e, r, gate, ALU.mult, ALU.mult)
                    elif kind == "dif" and s["half"]:
                        link(V.tensor_tensor(r, r, dlam[:, 7:8], ALU.mult))
                        dve.wait_ge(at_nm, s["i"])
                        ins = V.scalar_tensor_tensor(e, e, r, E[:, (s["i"] - 1) % 4, 0:nk], ALU.mult, ALU.add)
                    else:
                        ins = V.tensor_scalar(e, e, r, None, ALU.mult)
                    ins.then_inc(at_nm, 1)

                def out(s):
                    g, u, kind = s["g"], s["u"], s["kind"]
                    dve.wait_ge(at_pv, s["m"] + 1)
                    ps, b = OB[g % 2], HD * (u % 2)
                    if kind in ("swa", "fgt"):
                        c = u // 2 + 4 * (kind == "fgt")
                        ins = V.tensor_tensor(Q[b:b + HD, c, :], ps[b:b + HD, :], ar(A_GT, 8, S)[b:b + HD, c, :],
                                              ALU.mult)
                    elif kind == "win":
                        ins = V.tensor_copy(Q[b:b + HD, u // 2, :], ps[b:b + HD, :])
                    elif kind == "dsa":
                        if u >= 2:
                            dve.wait_ge(aux_mm, dsa_post(u - 2))
                        ins = V.tensor_copy(ar(A_OL + S * (u % 2), S), ps[:, :])
                    else:
                        ins = V.tensor_copy(Q[:, u, :], ps[:, :])
                    ins.then_inc(at_oe, 1)

                if phase == "fgt":
                    nf_diag_rows(0)
                    nf_masked(0)
                lag_out = LAG_OUT + (3 if phase == "dif" else 0)
                for n in range(len(steps) + lag_out):
                    if n < len(steps):
                        s = steps[n]
                        if phase == "fgt" and s["qb"] == 0 and s["u"] < 7:
                            nf_diag_rows(s["u"] + 1)
                        if phase == "fgt" and s["qb"] == 2 and s["u"] < 7:
                            nf_masked(s["u"] + 1)
                        logits(s)
                    if 0 <= n - 1 < len(steps):
                        scale(steps[n - 1])
                    m = n - lag_out
                    if m >= 0 and steps[m]["end"] and steps[m]["last"]:
                        out(steps[m])

            dve.wait_ge(c_tanh, 1)
            for n in range(ADA_FIRST):
                ada_block(n)
            ada_bias()
            cols(0, 1, col("ng0"), None, None, None)
            norm(0, "n0", 1e-6, False)
            tiles("p1")
            f_rows()
            dve.wait_ge(biasA_in, 16 * 8)
            attend("swa")
            attend("fgt")
            split_y("y1")
            tiles("o1", acol(2))
            cols(3, 4, col("ng1"), None, None, None)
            norm(1, "n1", 1e-6, False)
            link(V.memset(ar(A_XR, 8, XRW)[:, :, 0:3], 0.0))
            xr, xc = ar(A_XR, 8, XRW), ar(A_XC, 8, S)

            def conv(t, what):
                if what[0] != "xr":
                    return
                c = what[1]
                dve.wait_ge(evac_act, EVAC[t][1])
                link(V.tensor_scalar(xc[:, c, :], xr[:, c, 0:S], col("cw", c, c + 1), col("cb", c, c + 1), ALU.mult,
                                     ALU.add))
                for j in range(1, 4):
                    ins = V.scalar_tensor_tensor(xc[:, c, :], xr[:, c, j:j + S], col("cw", 8 * j + c, 8 * j + c + 1),
                                                 xc[:, c, :], ALU.mult, ALU.add)
                    if j < 3:
                        link(ins)
                ins.then_inc(l_conv, 1)

            tiles("lin", None, conv)
            V.scalar_tensor_tensor(k8[:, 0, :], col("lam"), -1.0, col("lam"), ALU.mult, ALU.min).then_inc(l_lam, 1)
            dve.wait_ge(l_lam2, 1)
            log1p_series(k8[:, 1, :], k8[:, 0, :], k8[:, 2, :], k8[:, 3, :])
            link(V.tensor_scalar(k8[:, 2, :], col("lam"), -1.0, 0.0, ALU.mult, ALU.max))
            link(V.scalar_tensor_tensor(k8[:, 3, :], k8[:, 0, :], 2.0, k8[:, 2, :], ALU.mult, ALU.add))
            link(V.tensor_scalar(k8[:, 4, :], k8[:, 3, :], LRU_C, None, ALU.mult))
            V.tensor_scalar(k8[:, 5, :], k8[:, 3, :], -LRU_C, None, ALU.mult).then_inc(l_lam, 1)
            for c in range(NC):
                dve.wait_ge(h_hi, h_base["xc"] + c + 1)
                low(c, xc[:, c, :]).then_inc(h_lo, 1)
            for c in range(NC):
                dve.wait_ge(l_sig, c + 1)
                V.tensor_tensor(xc[:, c, :], E[:, c % 4, :], xc[:, c, :], ALU.mult).then_inc(l_ixc, 1)
            a_ = ar(A_XR, 8, S)
            dve.wait_ge(l_ixc, NC)
            for c in range(NC):
                dve.wait_ge(l_te, c + 1)
                link(V.tensor_tensor(E[:, c % 4, :], a_[:, c, :], a_[:, c, :], ALU.mult))
                V.scalar_tensor_tensor(t8[:, c, :], E[:, c % 4, :], 1.0, t8[:, c, :], ALU.add, ALU.mult).then_inc(l_m, 1)
            for c in range(NC + 1):
                if c < NC:
                    dve.wait_ge(l_sq, c + 1)
                    link(V.tensor_tensor(t8[:, c, :], t8[:, c, :], xc[:, c, :], ALU.mult))
                    link(V.tensor_tensor_scan(xc[:, c, :], a_[:, c, :], t8[:, c, :], 0.0, ALU.mult, ALU.add))
                    V.tensor_tensor(xc[:, c, :], xc[:, c, :], ar(A_LG, 8, S)[:, c, :], ALU.mult).then_inc(l_y, 1)
                if c > 0:
                    dve.wait_ge(h_hi, h_base["y2"] + c)
                    low(c - 1, xc[:, c - 1, :]).then_inc(h_lo, 1)
            tiles("o2", acol(5))
            cols(6, 7, col("fg"), None, col("fg"), None)
            norm(2, "n2", 1e-6, False)
            link(V.tensor_scalar(acol(8), acol(8), 1.0, None, ALU.add))
            tiles("ev1")
            n = 0
            gi = ar(A_GI, NT, 32)
            dve.wait_ge(nat_evac, 3)
            for qb in range(1, NT):
                nk = P * (qb + 1)
                w = t8[:, qb, 0:nk]
                for j in range(8):
                    dve.wait_ge(ix_r, n + 1)
                    iw = gi[:, qb, 24 + j:25 + j]
                    if n:
                        dve.wait_ge(ix_a, n)
                    if j == 0:
                        ins = V.tensor_scalar(w, E[:, n % 4, 0:nk], iw, None, ALU.mult)
                    else:
                        ins = V.scalar_tensor_tensor(w, E[:, n % 4, 0:nk], iw, w, ALU.mult, ALU.add)
                    ins.then_inc(ix_a, 1)
                    n += 1
            dve.wait_ge(ix_a, n)

            def topk():
                for qb in range(1, NT):
                    nk = P * (qb + 1)
                    w = t8[:, qb, 0:nk]
                    link(V.tensor_tensor(w[:, nk - P:nk], w[:, nk - P:nk], tri, ALU.add))
                    for _ in range(TOPK // 8):
                        link(V.max(st[:, 8:16], w))
                        link(V.match_replace(w, st[:, 8:16], w, -3e38))
                    link(V.tensor_scalar(ar(A_PEN + (0, 0, 256, 640)[qb], nk), w, -2e38, NEG, ALU.is_gt, ALU.mult))

            def latent():
                dve.wait_ge(lat_st, 1)
                link(V.tensor_scalar(st[:, 16:20], TB[0][:, 0:4], 1.0 / P, 1e-5, ALU.mult, ALU.add))
                V.reciprocal(st[:, 0:4], st[:, 16:20]).then_inc(lat_v, 1)

            latent()
            topk()
            kc2 = ar(A_KC2, 4, S)
            dve.wait_ge(evac_act, EVAC[[t for t in PHASE["ev2"] if TILES[t][1] == "T"][-1]][1])
            dve.wait_ge(lat_t, 1)
            for kv in range(2):
                pe = col("pek") if kv == 0 else col("pev")
                for g in range(2):
                    v = kc2[:, 2 * kv + g, :].rearrange("p (n l r) -> p l n r", l=8, r=2)
                    for half in range(2):
                        o = cmp_in(kv).rearrange("p (l g n) -> p l g n", l=16, g=2)[:, 8 * half:8 * half + 8, g, :]
                        i0 = v[:, :, half:half + NCMP, 0]
                        i1 = pe[:, 8 * half:8 * half + 8].unsqueeze(2).to_broadcast([P, 8, NCMP])
                        ins = V.tensor_tensor(o, i0, i1, ALU.add)
                ins.then_inc(b_add, 1)
            for kv in range(2):
                dve.wait_ge(b_hi, kv + 1)
                sub(hL[:, 1024 * kv:1024 * kv + 992], cmp_in(kv),
                    hH[:, 1024 * kv:1024 * kv + 992].bitcast(F32)).then_inc(b_lo, 1)
            dve.wait_ge(b_lo, 2)
            for t in PHASE["ev3"]:
                ada_slot(t)
            dve.wait_ge(biasB_in, 16 * 8)
            dve.wait_ge(biasC_in, 16 * 8 * NT)
            attend("nsa")
            attend("dsa")
            dve.wait_ge(aux_ev, 16)
            split_y("y3")
            tiles("o3", acol(8))
            cols(9, 10, col("lng", 0, 8), col("lnb", 0, 8), col("lng", 0, 8), col("lnb", 0, 8))
            norm(3, "n3", 1e-5, True)
            link(V.tensor_scalar(acol(11), acol(11), 1.0, None, ALU.add))
            tiles("m1", acol(11))
            if pending:
                ada_bias()
            cols(12, 13, col("lng", 8, 16), col("lnb", 8, 16), col("lng", 8, 16), col("lnb", 8, 16))
            norm(4, "n4", 1e-5, True)
            for g in (14, 17):
                link(V.tensor_scalar(acol(g), acol(g), 1.0, None, ALU.add))
            lo, _ = COLS["dlam"]
            lv = cv[0:HD, lo:lo + 4].rearrange("p (a b) -> p a b", b=2)
            V.tensor_tensor(dlam[0:HD, 0:2], lv[:, :, 0], lv[:, :, 1], ALU.mult).then_inc(dl_p, 1)
            tiles("od")
            dve.wait_ge(dl_e, 1)
            link(sub(dlam[:, 6:7], dlam[:, 4:5], dlam[:, 5:6]))
            link(V.tensor_scalar(dlam[:, 7:8], dlam[:, 6:7], LAMBDA_INIT, -1.0, ALU.add, ALU.mult))
            attend("dif")
            dve.wait_ge(d_st, 1)
            v32 = k8[:, 0:4, :].rearrange("p a b -> p (a b)")
            link(V.tensor_scalar(v32, TB[0][:, 0:32], 1.0 / P, 1e-5, ALU.mult, ALU.add))
            V.reciprocal(v32, v32).then_inc(d_v, 1)
            link(V.tensor_scalar(dlam[:, 0:1], col("sub"), 1.0 - LAMBDA_INIT, None, ALU.mult))
            dve.wait_ge(d_r, 1)
            for h in range(9):
                if h < 8:
                    if h >= 2:
                        dve.wait_ge(d_bc, h - 1)
                    for tb in range(NT):
                        ins = V.tensor_scalar(E[:, h % 2, tb * P:(tb + 1) * P], ident, v32[:, 4 * h + tb:4 * h + tb + 1],
                                              None, ALU.mult)
                    ins.then_inc(d_diag, 1)
                if h > 0:
                    k = h - 1
                    dve.wait_ge(d_bc, k + 1)
                    V.scalar_tensor_tensor(Q[:, k, :], Q[:, k, :], dlam[:, 0:1], SB[k % 2][:, :], ALU.mult,
                                           ALU.mult).then_inc(d_y, 1)
            split_y("y4")
            tiles("o4", acol(14))
            cols(15, 16, col("lng", 16, 24), col("lnb", 16, 24), col("lng", 16, 24), col("lnb", 16, 24))
            norm(5, "n5", 1e-5, True)
            tiles("m2", acol(17))
            link(V.tensor_copy(ncol[:, 0, :], col("lng", 24, 32)))
            link(V.tensor_copy(ncol[:, 1, :], col("lnb", 24, 32)))
            norm(6, None, 1e-5, True)

        @block.tensor
        def _(pe):
            mm = nc.tensor.matmul
            aux = [0]
            nat = [0]

            def mm3(out, a, b, start, stop):
                mm(out, a[0], b[0], start=start, stop=False, skip_group_check=True)
                mm(out, a[0], b[1], start=False, stop=False, skip_group_check=True)
                return mm(out, a[1], b[0], start=False, stop=stop, skip_group_check=True)

            def weights(t, at, n):
                s = t % NSTREAM
                return wH[:, s, at:at + n], wL[:, s, at:at + n]

            def h(at, n):
                return hH[:, at:at + n], hL[:, at:at + n]

            def g(at, n):
                return gH[:, at:at + n], gL[:, at:at + n]

            def finish_ada(grp):
                pe.wait_ge(ada_used, 8 * grp + 8)
                if grp:
                    pe.wait_ge(ada_add, grp)
                for m in range(8):
                    ins = mm(AB[:, m:m + 1], acc[:, m * P:(m + 1) * P], ones[:, 0:1], start=True, stop=True)
                ins.then_inc(ada_sum, 1)

            def bank_free(t):
                n = T_INDEX[t]
                if n >= 2:
                    prev = TL[n - 2]
                    pe.wait_ge(evac_sem[EVAC[prev][0]], EVAC[prev][1])

            TL = list(T_INDEX)
            downs = [0]

            def tiles(phase):
                base = h_base.get(H_OF_PHASE.get(phase))
                first = True
                for t in PHASE[phase]:
                    _, kind, what = TILES[t]
                    pe.wait_ge(lo_done, t + 1)
                    if kind == "T":
                        bank_free(t)
                        if nat[0]:
                            pe.wait_ge(nat_evac, nat[0])
                        if what[0] == "down" and what[1] == 0:
                            downs[0] += 1
                        for k in range(NC):
                            if first and base is not None:
                                pe.wait_ge(h_lo, base + k + 1)
                            if what[0] == "down" and what[1] == 0:
                                pe.wait_ge(g_lo_s, 8 * (downs[0] - 1) + k + 1)
                            rhs = g(k * S, S) if what[0] == "down" else h(k * S, S)
                            ins = mm3(LB[T_INDEX[t] % 2][:, :], weights(t, k * P, P), rhs, k == 0, k == NC - 1)
                        ins.then_inc(tile_done, 1)
                    elif kind == "N":
                        name, b, nb = what
                        w = N_WIDTH[name]
                        n = 32 if name == "gi" else w
                        if b == 0:
                            for d in (1, 2):
                                prev = TL[max(i for i, tt in enumerate(TL) if tt < t) + 1 - d]
                                pe.wait_ge(evac_sem[EVAC[prev][0]], EVAC[prev][1])
                            if nat[0]:
                                pe.wait_ge(nat_evac, nat[0])
                        per = BLK // w
                        for kk in range(per):
                            k = b * per + kk
                            for tb in range(NT):
                                ins = mm3(NB[tb][:, 0:n], h(k * S + tb * P, P), weights(t, kk * w, n), k == 0,
                                          k == NC - 1)
                        ins.then_inc(tile_done, 1)
                        if b == nb - 1:
                            nat[0] += 1
                    first = False
                    if t in STAT_AFTER:
                        stats(phase not in ("o1", "o2"))
                    for grp in FIN_AT.get(t, []):
                        finish_ada(grp)
                    if kind == "T" and what[0] == "kvl":
                        pe.wait_ge(lat_sq, 1)
                        for tb in range(NT):
                            ins = mm(TB[0][:, tb:tb + 1], t8[:, 4, tb * P:(tb + 1) * P], ones[:, 0:1], start=True,
                                     stop=True)
                        ins.then_inc(lat_st, 1)

            stats_done = [0]

            def stats(centred):
                c = stats_done[0] % NC
                stats_done[0] += 1
                pe.wait_ge(n_sq, stats_done[0])
                for tb in range(NT):
                    ins = mm(TB[0][:, tb:tb + 1], t8[:, c, tb * P:(tb + 1) * P], ones[:, 0:1],
                             start=(c == 0 and tb == 0), stop=False, skip_group_check=True)
                    if centred:
                        ins = mm(TB[0][:, 4 + tb:5 + tb], x[:, c, tb * P:(tb + 1) * P], ones[:, 0:1], start=False,
                                 stop=False, skip_group_check=True)
                return ins

            def norm(n, centred):
                for c in range(NC if n == 0 else 1):
                    ins = stats(centred)
                ins.then_inc(n_stat, 1)
                pe.wait_ge(n_diag, n + 1)
                ins = mm(SB[0][:, :], ones, E[:, 0, :], start=True, stop=True)
                if centred:
                    ins = mm(SB[1][:, :], ones, E[:, 1, :], start=True, stop=True)
                ins.then_inc(n_bcast, 1)

            def attend(phase):
                steps = ATT[phase]

                def scores(s):
                    i, u, qb, nk, kind = s["i"], s["u"], s["qb"], s["nk"], s["kind"]
                    if i >= 3:
                        pe.wait_ge(at_max, i - 2)
                    b = HD * (u % 2)
                    q = slice(qb * P, (qb + 1) * P)
                    if kind == "swa":
                        a, k = Q[b:b + HD, u // 2, q], ar(A_AK, S)[b:b + HD, (qb + 1) * P - nk:(qb + 1) * P]
                    elif kind == "fgt":
                        a, k = Q[b:b + HD, 4 + u // 2, q], ar(A_BK, 4, S)[b:b + HD, u // 2, 0:nk]
                    elif kind == "cmp":
                        a, k = Q[b:b + HD, u // 2, q], ar(A_KCT, 32)[b:b + HD, 0:nk]
                    elif kind in ("sel", "win"):
                        a = Q[b:b + HD, u // 2, q]
                        k = ar(A_KS if kind == "sel" else A_KW, S)[b:b + HD, 0:nk]
                    elif kind == "dsa":
                        if qb == 0:
                            pe.wait_ge(aux_ev, dsa_pre(u))
                        a, k = ar(A_QL + S * (u % 2), S)[:, q], ar(A_CKT, S)[:, 0:nk]
                    else:
                        b = HD * s["half"]
                        a, k = Q[b:b + HD, u, q], ar(A_DK, 8, S)[b:b + HD, u, 0:nk]
                    mm(score_bank(s)[:, 0:nk], a, k, start=True, stop=True).then_inc(at_sc, 1)

                def turn(s):
                    j = s["j"]
                    if j is None:
                        return
                    pe.wait_ge(at_nm, s["i"] + 1)
                    if j >= 2:
                        pe.wait_ge(at_pt, j - 1)
                    a, b = s["slots"]
                    for n in range(a, b):
                        w = min(P, s["nk"])
                        ins = nc.tensor.transpose(TB[j % 2][0:w, n * P:(n + 1) * P],
                                                  E[:, s["i"] % 4, (n - a) * P:(n - a) * P + w], ident)
                    ins.then_inc(at_tr, 1)

                def values(s, part):
                    kind, u, m, g_ = s["kind"], s["u"], s["m"], s["g"]
                    if part == 0:
                        pe.wait_ge(at_pt, s["j"] + 1)
                        if s["first"] and g_ >= 2:
                            pe.wait_ge(at_oe, g_ - 1)
                    o, pt = OB[g_ % 2], PT[:, m % 2, :, :]
                    if kind == "swa":
                        va = ar(A_VA, NT, P)
                        q = slice(part * P, (part + 1) * P)
                        ins = mm(o[:, q], va[:, part, :], pt[:, 1, q], start=True, stop=(part == 0),
                                 skip_group_check=True)
                        if part:
                            ins = mm(o[:, q], va[:, part - 1, :], pt[:, 0, q], start=False, stop=True,
                                     skip_group_check=True)
                    elif kind == "cmp":
                        if part == 3:
                            ins = mm(o[:, :], ar(A_VCN, P)[0:NCMP, :], pt[0:NCMP, 0, :], start=True, stop=False,
                                     skip_group_check=True)
                    else:
                        kb = part
                        if kind == "fgt":
                            v = ar(A_VB, NT, S)[:, kb, (u // 2) * P:(u // 2 + 1) * P]
                        elif kind == "dsa":
                            v = ar(A_CKN, NT, P)[:, kb, :]
                        elif kind == "dif":
                            v = ar(A_DV, NT, 1024)[:, kb, u * P:(u + 1) * P]
                        else:
                            v = ar(A_VN, NT, 256)[:, kb, P * (kind == "win"):P * (kind == "win") + P]
                        ins = mm(o[:, kb * P:S], v, pt[:, kb, kb * P:S], start=(kb == 0 and s["first"]),
                                 stop=(kb == NT - 1), skip_group_check=True)
                    if part == 3:
                        ins.then_inc(at_pv, 1)

                def nf(hd):
                    pe.wait_ge(nf_diag, hd + 1)
                    if hd:
                        pe.wait_ge(nf_copy, hd)
                    mm(AB[:, :], ones[0:8, :], ar(A_AK, S)[0:8, :], start=True, stop=True).then_inc(nf_mm, 1)

                def aux_mm_(lhsT, rhs):
                    if aux[0]:
                        pe.wait_ge(aux_ev, aux[0])
                    aux[0] += 1
                    mm(LB[0][:, :], lhsT, rhs, start=True, stop=True).then_inc(aux_mm, 1)

                def q_latent(u):
                    b = HD * (u % 2)
                    aux_mm_(ar(A_M2, M2W)[b:b + HD, M2_UK + P * (u // 2):M2_UK + P * (u // 2) + P],
                            Q[b:b + HD, 4 + u // 2, :])

                def o_latent(u):
                    pe.wait_ge(at_oe, ATT["dsa"][4 * u]["g"] + 1)
                    aux_mm_(ar(A_M2, M2W)[:, M2_UV + P * (u // 2):M2_UV + P * (u // 2) + P],
                            ar(A_OL + S * (u % 2), S))

                if phase == "fgt":
                    pe.wait_ge(ada_add, len([k for k in FIN_AT if k <= PHASE["p1"][-1]]) + 2)
                    nf(0)
                if phase == "dsa":
                    q_latent(0)
                for n in range(len(steps) + LAG_OUT + 4):
                    if n < len(steps):
                        s = steps[n]
                        if phase == "fgt" and s["qb"] == 0 and s["u"] < 7:
                            nf(s["u"] + 1)
                        if phase == "dsa" and s["qb"] == 1 and s["u"] < 7:
                            q_latent(s["u"] + 1)
                        scores(s)
                    if 0 <= n - LAG_TR < len(steps):
                        turn(steps[n - LAG_TR])
                    for part in range(4):
                        k = n - LAG_PV - part * (2 if phase == "dif" else 1)
                        if 0 <= k < len(steps) and steps[k]["end"]:
                            values(steps[k], part)
                    m = n - LAG_OUT - 1
                    if phase == "dsa" and 0 <= m < len(steps) and steps[m]["end"]:
                        o_latent(steps[m]["u"])

            pe.wait_ge(consts_in, 48)
            tab = ar(A_TAB, 24)[0:34, :]
            mm(SB[0][0:24, 0:BAND], tab, ar(A_OHB, BAND)[0:34, :], start=True, stop=True)
            mm(SB[1][0:24, 0:496], tab, ar(A_OHC, CBAND)[0:34, 0:496], start=True, stop=True)
            mm(TB[0][0:24, 0:496], tab, ar(A_OHC, CBAND)[0:34, 496:CBAND], start=True, stop=True).then_inc(bias_mm, 1)
            finish_ada(0)
            finish_ada(1)
            pe.wait_ge(bias_evac, 1)
            norm(0, False)
            tiles("p1")
            pe.wait_ge(f_row, 1)
            for tb in range(NT):
                ins = nc.tensor.transpose(TB[0][:, 8 * tb:8 * tb + 8], frow[:, tb * P:(tb + 1) * P], ident[0:8, 0:8])
            ins.then_inc(f_tr, 1)
            pe.wait_ge(f_tok, 1)
            pe.wait_ge(evac_act, EVAC[PHASE["p1"][-1]][1])
            attend("swa")
            attend("fgt")
            pe.wait_ge(at_oe, ATT["fgt"][-1]["g"] + 1)
            tiles("o1")
            norm(1, False)
            tiles("lin")
            ta, tx = PHASE["lcore"]
            pe.wait_ge(lo_done, tx + 1)
            pe.wait_ge(evac_act, EVAC[PHASE["lin"][-1]][1])
            pe.wait_ge(n_t, 16)
            for c in range(NC):
                pe.wait_ge(h_lo, h_base["xc"] + c + 1)
                if c >= 2:
                    pe.wait_ge(l_sig, c - 1)
                for k, t in enumerate((ta, tx)):
                    ins = mm3(NB[2 * (c % 2) + k][:, :], weights(t, c * P, P), h(c * S, S), True, True)
                    ins.then_inc(l_mm if c < NC - 1 else tile_done, 1)
            pe.wait_ge(l_sig, NC)
            tiles("o2")
            norm(2, False)
            tiles("ev1")
            n = 0
            pe.wait_ge(nat_evac, nat[0])
            for qb in range(1, NT):
                for j in range(8):
                    b = HD * (j % 2)
                    if n >= 2:
                        pe.wait_ge(ix_r, n - 1)
                    mm(SB[n % 2][:, 0:P * (qb + 1)], ar(A_IQ, 4, S)[b:b + HD, j // 2, qb * P:(qb + 1) * P],
                       ar(A_IK, S)[b:b + HD, 0:P * (qb + 1)], start=True, stop=True).then_inc(ix_s, 1)
                    n += 1
            pe.wait_ge(ix_r, n)
            tiles("ev2")
            pe.wait_ge(lat_r, 1)
            for tb in range(NT):
                ins = nc.tensor.transpose(TB[0][:, tb * P:(tb + 1) * P], t8[:, 5, tb * P:(tb + 1) * P], ident)
            ins.then_inc(lat_t, 1)
            pe.wait_ge(lat_n, 1)
            for tb in range(NT):
                ins = nc.tensor.transpose(TB[1][:, tb * P:(tb + 1) * P], ar(A_CKN, NT, P)[:, tb, :], ident)
            ins.then_inc(lat_tt, 1)
            pe.wait_ge(evac_act, EVAC[PHASE["ev2"][-1]][1])
            for kv in range(2):
                pe.wait_ge(b_lo, kv + 1)
                if kv:
                    pe.wait_ge(hid_done, 1)
                for b in range(4):
                    t = PHASE["ev3"][4 * kv + b]
                    pe.wait_ge(lo_done, t + 1)
                    for lp in range(4):
                        for hc in range(2):
                            ins = mm3(LB[hc][:, 0:62], weights(t, lp * 256 + hc * P, P),
                                      h(1024 * kv + (4 * b + lp) * 62, 62), b == 0 and lp == 0, b == 3 and lp == 3)
                    ins.then_inc(tile_done, 1)
            pe.wait_ge(hid_done, 2)
            pe.wait_ge(m2_in, 16)
            hid, m2 = ar(A_HID, 4, 62), ar(A_M2, M2W)
            for hc in range(2):
                mm(SB[0][:, 0:62], m2[:, M2_K + P * hc:M2_K + P * hc + P], hid[:, hc, :], start=(hc == 0),
                   stop=(hc == 1))
            for gg in range(2):
                for hc in range(2):
                    ins = mm(SB[1][0:NCMP, HD * gg:HD * gg + HD], hid[:, 2 + hc, NCMP * gg:NCMP * gg + NCMP],
                             m2[:, M2_V + HD * hc:M2_V + HD * hc + HD], start=(hc == 0), stop=(hc == 1),
                             skip_group_check=True)
            ins.then_inc(kc_mm, 1)
            pe.wait_ge(kc_done, 1)
            pe.wait_ge(lat_done, 1)
            attend("nsa")
            pe.wait_ge(at_oe, ATT["nsa"][-1]["g"] + 1)
            attend("dsa")
            pe.wait_ge(aux_ev, 16)
            tiles("o3")
            norm(3, True)
            tiles("m1")
            norm(4, True)
            pe.wait_ge(dl_p, 1)
            mm(AB[:, 0:2], ones[0:HD, :], dlam[0:HD, 0:2], start=True, stop=True).then_inc(dl_mm, 1)
            tiles("od")
            pe.wait_ge(nat_evac, nat[0])
            attend("dif")
            for hh in range(8):
                pe.wait_ge(d_sq, hh + 1)
                for tb in range(NT):
                    ins = mm(TB[0][:, 4 * hh + tb:4 * hh + tb + 1], t8[:, hh, tb * P:(tb + 1) * P], ones[:, 0:1],
                             start=True, stop=True)
            ins.then_inc(d_st, 1)
            for hh in range(8):
                pe.wait_ge(d_diag, hh + 1)
                if hh >= 2:
                    pe.wait_ge(d_y, hh - 1)
                mm(SB[hh % 2][:, :], ones, E[:, hh % 2, :], start=True, stop=True).then_inc(d_bc, 1)
            pe.wait_ge(at_oe, ATT["dif"][-1]["g"] + 1)
            tiles("o4")
            norm(5, True)
            tiles("m2")
            norm(6, True)


def bucket(dist):
    import numpy as np
    n = np.maximum(dist, 0)
    nf = np.maximum(n, 1).astype(np.float32)
    large = 16 + (np.log(nf / 16) / math.log(128 / 16) * 16).astype(np.int32)
    return np.where(n < 16, n, np.minimum(large, N_BUCKET - 1))


def constants():
    import numpy as np

    def onehot(dist):
        o = np.zeros((34, dist.size), np.float32)
        o[bucket(dist), np.arange(dist.size)] = 1
        o[32] = dist < 0
        o[33] = dist >= 128
        return o

    cc = np.zeros((P, NCONST), np.float32)
    cc[:, C_ID:C_ID + P] = np.eye(P)
    cc[:, C_ONE:C_ONE + P] = 1
    r = np.arange(P)
    cc[:, C_TRI:C_TRI + P] = np.where(r[None, :] > r[:, None], NEG, 0)
    t = np.arange(NT)[None, :, None] * P + r[:, None, None]
    cc[:, C_MC:] = (t >= 16 * np.arange(NCMP)[None, None, :] + 31).reshape(P, -1)
    z = 16 * np.arange(61, -1, -1)[None, :] + np.arange(16)[:, None]
    return cc, onehot(np.arange(255, 255 - BAND, -1)), onehot(z.reshape(-1) - 480 - 31)


def layout(i):
    import numpy as np
    r = np.arange
    pair = np.concatenate([np.concatenate([r(64 * c, 64 * c + 64), r(256 + 64 * c, 320 + 64 * c)]) for c in range(4)])
    rows = np.concatenate([pair, r(512, 1024)])
    w_in, e_in, o_in = i["attn_w_in"][0], i["ev_w_in_2"][0], i["od_w_in_2"][0]
    l_in = i["lru_w_in"][0]
    outs = {"o1": i["attn_w_out"][0][rows], "o2": i["lru_w_out"][0], "o3": i["ev_w_out_2"][0][rows],
            "o4": i["od_w_out_2"][0]}
    stacked = {"wa": i["lru_w_a"][0].reshape(D, P), "wx": i["lru_w_x"][0].reshape(D, P)}

    def block(mat, cols, k0=0):
        w = mat[:, cols]
        if w.shape[1] < P:
            w = np.concatenate([w, np.zeros((w.shape[0], P - w.shape[1]), w.dtype)], 1)
        n = BLK // w.shape[1]
        return w[k0 * P:(k0 + n) * P].reshape(n, P, -1).transpose(1, 0, 2).reshape(P, BLK)

    blocks, quarter = [], {"m1": -1, "m2": -1}
    for phase, kind, what in TILES:
        name, n = what[0], what[1]
        c = r(P * n, P * n + P)
        if phase == "p1":
            cols = {"q": (pair if n < 4 else 768 - 512 + r(1024))[c] if name == "q" else None, "ak": r(512, 640),
                    "bk": 1280 + c, "f": r(2304, 2312),
                    "gate": 2312 + rows[c] if name == "gate" else None, "vb": r(1792, 2304), "va": r(640, 768)}[name]
            b = block(w_in, cols, n * 2 if name == "vb" else 0)
        elif phase in outs:
            b = block(outs[phase], c)
        elif phase == "lin":
            b = block(l_in, c + (D if name == "lgate" else 0))
        elif phase == "lcore":
            b = block(stacked[name], r(P))
        elif phase in ("ev1", "ev2"):
            if name == "q":
                cols = pair[c] if n < 4 else 1304 + c - 512
            elif name == "kc2":
                k = 512 + 128 * (n // 2) + 64 * (n % 2)
                cols = np.concatenate([r(k, k + 64)] * 2)
            else:
                cols = {"ik": np.concatenate([r(2456, 2520)] * 2), "iq": 1944 + c,
                        "gi": np.concatenate([r(1280, 1304), r(2520, 2528)]), "kvl": r(1816, 1944),
                        "ks": r(768, 896), "kw": r(1024, 1152),
                        "vn": np.concatenate([r(896, 1024), r(1152, 1280)])}[name]
            b = block(e_in, cols, 4 * n if name == "vn" else 0)
        elif phase == "ev3":
            b = block(i["nsa_w1_k_2" if what[0] == 0 else "nsa_w1_v_2"][0], r(256), 4 * n)
        elif phase in ("m1", "m2"):
            layer = int(phase[1]) - 1
            if name == "up":
                quarter[phase] += n == 0
                b = block(i["mlp_w1_2"][layer], quarter[phase] * D + c)
            else:
                b = block(i["mlp_w2_2"][layer][quarter[phase] * D:(quarter[phase] + 1) * D], c)
        else:
            cols = {"q": c, "dk": D + c, "dv0": 2 * D + r(512), "dv1": 2 * D + 512 + r(512)}[name]
            b = block(o_in, cols, 2 * n if name[:2] == "dv" else 0)
        blocks.append(b)
    W = np.stack(blocks)

    ada = []
    for w, n in ((i["ada_w"], 3), (i["ada_w_2"], 6)):
        ada.append(w.reshape(2, NC, P, n, D).transpose(0, 3, 1, 2, 4).reshape(-1, P, D))
    WA = np.concatenate(ada)

    def feat(v):
        return v.reshape(-1, P).T

    vec = {
        "c": feat(i["c"]), "c2": feat(i["c_2"]), "ng0": feat(i["norm_g"][0]), "ng1": feat(i["norm_g"][1]),
        "adab": feat(np.concatenate([i["ada_b"].reshape(-1), i["ada_b_2"].reshape(-1)])), "fg": feat(i["final_g"]),
        "lng": feat(i["ln_g_2"]), "lnb": feat(i["ln_b_2"]), "cw": feat(i["lru_conv_w"]), "cb": feat(i["lru_conv_b"]),
        "ba": feat(i["lru_b_a"]), "bx": feat(i["lru_b_x"]), "lam": feat(i["lru_lambda"]),
        "kvn": feat(i["dsa_kv_norm_2"]), "sub": feat(i["diff_subln_2"]), "bf": i["attn_b_f"].T,
        "pek": feat(i["nsa_pe_k_2"]), "pev": feat(i["nsa_pe_v_2"]),
        "sink": np.broadcast_to(i["attn_sinks"], (P, 8)), "t31": np.broadcast_to(i["rel_bias_2"][31:32], (P, 16)),
        "dlam": i["diff_lam_2"][0].T,
    }
    CV = np.zeros((P, NCOL), np.float32)
    for name, v in vec.items():
        lo, hi = COLS[name]
        CV[:v.shape[0], lo:hi] = v
    CC, oh_band, oh_cmp = constants()
    tab = np.zeros((34, 24), np.float32)
    tab[:32, :8], tab[:32, 8:] = i["rel_bias"], i["rel_bias_2"]
    tab[32], tab[33, :8] = NEG, NEG
    OH = np.concatenate([oh_band, oh_cmp, tab], 1)
    w2k = i["nsa_w2_k_2"][0].reshape(2, P, HD).transpose(1, 0, 2)
    w2v = i["nsa_w2_v_2"][0].reshape(2, P, HD).transpose(1, 0, 2)
    uk = i["dsa_w_uk_2"][0].transpose(1, 2, 0).reshape(4, P, P).transpose(1, 0, 2)
    M2 = np.concatenate([np.concatenate([w2k, w2k], 2).reshape(P, -1), w2v.reshape(P, -1), uk.reshape(P, -1),
                         i["dsa_w_uv_2"][0].reshape(P, -1)], 1)
    X = i["x"][0].T.reshape(NC, P, S).transpose(1, 0, 2).reshape(P, -1)
    return [np.ascontiguousarray(a) for a in (W, WA, X, CV, CC, OH, M2)]


def kernel(**inputs):
    import numpy as np
    import concourse.bacc as bacc
    from concourse.bass_utils import run_bass_kernel_spmd as run

    nc = bacc.Bacc("TRN2", target_bir_lowering=False, num_devices=1)
    arrays, args = {}, []
    for name, a in zip(("W", "WA", "X", "CV", "CC", "OH", "M2"), layout({k: np.asarray(v) for k, v in inputs.items()})):
        arrays[f"in_{name}"] = a
        args.append(nc.dram_tensor(f"in_{name}", a.shape, mybir.dt.from_np(a.dtype), kind="ExternalInput").ap())
    args.append(nc.dram_tensor("bias_by_distance", (24, 16, BAND), F32, kind="Internal").ap())
    args.append(nc.dram_tensor("bias_of_compressed", (24, CBAND), F32, kind="Internal").ap())
    args.append(nc.dram_tensor("out", (P, NC, S), F32, kind="ExternalOutput").ap())
    program(nc, *args)
    r = run(nc, [arrays], core_ids=[0])
    out = r.results[0]["out"]
    return out.transpose(2, 1, 0).reshape(1, S, D)
```

```python
import math
from contextlib import ExitStack

import concourse.bass as bass
from concourse import mybir

F32 = mybir.dt.float32
F32R = mybir.dt.float32r
ALU = mybir.AluOpType
ACT = mybir.ActivationFunctionType
AX = mybir.AxisListType

P = 128
S = 512
D = 1024
NC = D // P
NT = S // P
HD = 64
BLK = 1024
NEG = -1e30
NSTREAM = 3
NADA = 2
N_BUCKET = 32
NCMP = (S - 32) // 16 + 1
TOPK = min(256, S // 4)
DSCALE = HD ** -0.5
ALPHA = 4 ** 0.25
LAMBDA_INIT = 0.8 - 0.6 * math.exp(-0.3)
LRU_C = 8.0

ARENA = 16384
A_Q = 0
A_AK, A_BK, A_VA, A_VB, A_GT, A_BA = 4096, 4608, 6656, 7168, 9216, 13312
A_BC = 15360
A_XR, A_LG, A_XC = 0, 4224, 8320
XRW = S + 3
A_KS, A_KW, A_VN, A_CKT, A_CKN, A_IQ, A_IK, A_KC2 = 4096, 4608, 5120, 6144, 6656, 7168, 9216, 9728
A_GI, A_M2, A_HID, A_PEN, A_KCT, A_VCN = 11776, 11904, 13312, 13568, 14720, 14752
A_OL = 8192
M2_K, M2_V, M2_UK, M2_UV, M2W = 0, 256, 384, 896, 1408
A_DK, A_DV = 4096, 8192
A_OHB, A_OHC, A_TAB = 0, 384, 1376
OHW = 1400
A_ADA = (1408, 5504, 11104)
A_U = 9664
BAND, CBAND = 384, 992

COLS = {}
_n = 0
for _name, _w in (("c", 8), ("c2", 8), ("ng0", 8), ("ng1", 8), ("adab", 144), ("fg", 8), ("lng", 32), ("lnb", 32),
                  ("cw", 32), ("cb", 8), ("ba", 8), ("bx", 8), ("lam", 8), ("kvn", 1), ("sub", 1), ("bf", 1),
                  ("pek", 16), ("pev", 16), ("sink", 8), ("t31", 16), ("dlam", 4)):
    COLS[_name] = (_n, _n + _w)
    _n += _w
NCOL = _n
C_ID, C_ONE, C_TRI, C_MC = 0, 128, 256, 384
NCONST = 384 + NT * NCMP


def tile_plan():
    t = []
    t += [("p1", "T", ("q", i)) for i in range(4)] + [("p1", "T", ("va", 0)), ("p1", "T", ("ak", 0))]
    t += [("p1", "T", ("q", 4 + i)) for i in range(4)] + [("p1", "T", ("bk", i)) for i in range(4)]
    t += [("p1", "T", ("f", 0))]
    t += [("p1", "N", ("vb", b, 4)) for b in range(4)]
    t += [("p1", "T", ("gate", i)) for i in range(8)]
    t += [("o1", "T", ("out", i)) for i in range(8)]
    t += [("lin", "T", ("xr", i)) for i in range(8)] + [("lin", "T", ("lgate", i)) for i in range(8)]
    t += [("lcore", "G", ("wa", 0)), ("lcore", "G", ("wx", 0))]
    t += [("o2", "T", ("out", i)) for i in range(8)]
    t += [("ev1", "T", ("gi", 0)), ("ev1", "T", ("ik", 0))] + [("ev1", "T", ("iq", i)) for i in range(4)]
    t += [("ev2", "T", ("kvl", 0))]
    t += [("ev2", "T", ("q", i)) for i in range(8)] + [("ev2", "T", ("ks", 0)), ("ev2", "T", ("kw", 0))]
    t += [("ev2", "T", ("vn", i)) for i in range(2)]
    t += [("ev2", "T", ("kc2", i)) for i in range(2)]
    t += [("o3", "T", ("out", i)) for i in range(8)]
    for q in range(4):
        t += [("m1", "T", ("up", i)) for i in range(8)] + [("m1", "T", ("down", i)) for i in range(8)]
    t += [("od", "T", ("q", i)) for i in range(8)] + [("od", "T", ("dk", i)) for i in range(8)]
    t += [("od", "N", ("dv0", b, 4)) for b in range(4)] + [("od", "N", ("dv1", b, 4)) for b in range(4)]
    t += [("o4", "T", ("out", i)) for i in range(8)]
    for q in range(4):
        t += [("m2", "T", ("up", i)) for i in range(8)] + [("m2", "T", ("down", i)) for i in range(8)]
    return t


TILES = tile_plan()
NTILE = len(TILES)
PHASE = {}
for _t, (_ph, _, _) in enumerate(TILES):
    PHASE.setdefault(_ph, []).append(_t)
T_INDEX = {t: n for n, t in enumerate(t for t in range(NTILE) if TILES[t][1] == "T")}
N_WIDTH = {"vb": 512, "dv0": 512, "dv1": 512}
TURNED = ("va", "gi", "vn")

EVAC = {}
_count = {"act": 0, "dve": 0}
for _t in T_INDEX:
    _e = "dve" if TILES[_t][2][0] in ("out", "down") else "act"
    _count[_e] += 1
    EVAC[_t] = (_e, _count[_e])
EVAC_ACT, EVAC_DVE = _count["act"], _count["dve"]

NGROUP = 18
ADA_FIRST = 16
ADA_EARLY = 12
ADA_AT = {}


def _plan_ada():
    n = ADA_FIRST
    for phase in ("p1", "o1", "lin", "o2", "ev1", "o3", "m1"):
        for m, t in enumerate(PHASE[phase]):
            if TILES[t][2] in (("up", 7), ("down", 0)):
                continue
            k = min(2 if phase == "p1" and m % 3 == 2 and n < 48 else 1, 8 * NGROUP - n)
            if k > 0:
                ADA_AT[t] = list(range(n, n + k))
                n += k
    assert n == 144


_plan_ada()
STAT_AFTER = {t for ph in ("o1", "o2", "o3", "m1", "o4", "m2") for t in PHASE[ph][-7:]}
FIN_AT = {}
for _t, _ids in ADA_AT.items():
    for _i in _ids:
        if _i % 8 == 7:
            FIN_AT.setdefault(_t + 1, []).append(_i // 8)


def attention_plan():
    plan, i, j, m, g = {}, 0, 0, 0, 0
    for phase in ("swa", "fgt", "nsa", "dsa", "dif"):
        steps = []
        for u in range(8):
            kinds = {"nsa": ("cmp", "sel", "win")}.get(phase, (phase,))
            for n, kind in enumerate(kinds):
                for qb in range(1 if kind == "cmp" else NT):
                    for half in range(2 if kind == "dif" else 1):
                        if kind == "swa":
                            slots = (0, 2) if qb else (1, 2)
                            nk = 128 * (slots[1] - slots[0])
                        elif kind == "cmp":
                            slots, nk = (0, NT), NT * NCMP
                        else:
                            slots, nk = (0, qb + 1), 128 * (qb + 1)
                        turned = kind != "dif" or half == 1
                        steps.append(dict(kind=kind, u=u, qb=qb, half=half, slots=slots, nk=nk, i=i,
                                          j=j if turned else None, tr_after=j + 1, m=m, g=g,
                                          first=(n == 0), last=(n == len(kinds) - 1),
                                          end=turned and (qb == NT - 1 or kind == "cmp")))
                        i += 1
                        j += turned
                m += 1
            g += 1
        plan[phase] = steps
    return plan


ATT = attention_plan()
STEP = [s for phase in ("swa", "fgt", "nsa", "dsa", "dif") for s in ATT[phase]]
LAG_TR, LAG_PV, LAG_OUT = 3, 5, 9


LAG_SUM = LAG_OUT + 8
LAG_POST = LAG_OUT + 4


def program(nc, W, WC, WA, X, CV, CC, OH, M2, UB, UC, OUT):
    ctx = ExitStack()
    with ctx:
        def sb(name, shape, dt=F32):
            return ctx.enter_context(nc.sbuf_tensor(name, shape, dt))

        def sem(name):
            return ctx.enter_context(nc.semaphore(name))

        arena_at = (nc.sbuf_base + 31) // 32 * 32
        slab = sb("arena", [P, ARENA])
        x = sb("x", [P, NC, S])
        h_hi_at = (nc.sbuf_base + 31) // 32 * 32
        hH = sb("h_hi", [P, NC * S], F32R)
        h_lo_at = (nc.sbuf_base + 31) // 32 * 32
        hL = sb("h_lo", [P, NC * S], F32R)
        wraw = sb("w_raw", [P, NSTREAM, BLK])
        wH = sb("w_hi", [P, NSTREAM, BLK], F32R)
        wL = sb("w_lo", [P, NSTREAM, BLK], F32R)
        biasB = sb("bias_near", [P, 16, 256])
        PT = sb("probs_t", [P, 2, NT, S])
        E = sb("logits", [P, 4, S])
        adaw = sb("ada_w", [P, NADA, BLK])
        acc = sb("ada_acc", [P, BLK])
        cv = sb("vectors", [P, NCOL])
        cc = sb("constants", [P, NCONST])
        frow = sb("f_rows", [8, S])
        adac = sb("ada_cols", [P, NGROUP * 8])
        cact = sb("c_act", [P, 16])
        ncol = sb("norm_cols", [P, 4, 8])
        st = sb("stats", [P, 24])
        rst = sb("rstd", [P, 4])
        nmx = sb("neg_max", [P, 4])
        rsum = sb("row_sum", [P, 4])
        ftok = sb("f_tokens", [P, NT, 8])
        k8 = sb("lru_rate", [P, 6, 8])
        dlam = sb("diff_lam", [P, 8])

        bank = [ctx.enter_context(nc.psum_tensor(f"bank{i}", [P, S], F32)) for i in range(8)]
        LB, SB, TB, OB, AB = bank[0:2], bank[2:4], bank[4:6], (bank[6], bank[1]), bank[7]
        NB = bank[0:4]

        def score_bank(s):
            return (bank[2], bank[3], bank[7] if s["kind"] in ("cmp", "sel", "win", "dsa") else bank[0])[s["i"] % 3]

        t8 = PT[:, :, :, :].rearrange("p a b s -> p (a b) s")
        ident, ones = cc[:, C_ID:C_ID + P], cc[:, C_ONE:C_ONE + P]
        tri = cc[:, C_TRI:C_TRI + P]
        maskc = cc[:, C_MC:C_MC + NT * NCMP].rearrange("p (q n) -> p q n", q=NT)

        def ar(at, *dims):
            n = 1
            for d in dims:
                n *= d
            v = slab[:, at:at + n]
            if len(dims) == 2:
                return v.rearrange("p (a b) -> p a b", a=dims[0])
            if len(dims) == 3:
                return v.rearrange("p (a b c) -> p a b c", a=dims[0], b=dims[1])
            return v

        def col(name, a=0, b=None):
            lo, hi = COLS[name]
            return cv[:, lo + a:lo + b if b is not None else hi]

        def cmp_in(kv):
            return t8[:, 4 + 2 * kv:6 + 2 * kv, :].rearrange("p a s -> p (a s)")[:, 0:16 * 2 * NCMP]

        def turned_at(s):
            if s["kind"] == "cmp":
                return ar(A_KC2, 1, S), s["m"] - 3
            if s["kind"] in ("sel", "win"):
                return PT[:, int(s["kind"] == "win"), :, :], s["m"] - 3
            return PT[:, s["m"] % 2, :, :], s["m"] - 2

        def cmp_weights(kv, k):
            if kv:
                return cmp_w2[:, 256 * k:256 * k + 256]
            if k < 8:
                return ar(A_IQ, 8, 256)[:, k, :]
            return E[:, :, :].rearrange("p a s -> p (a s)")[:, 256 * (k - 8):256 * (k - 8) + 256]

        def stage_rows(what):
            return 32 if what[0] == "gi" else P

        def stage(what):
            at = {"va": A_GT + 7 * S, "gi": A_CKN, "vn": A_KC2 + (2 + what[1]) * S}[what[0]]
            return ar(at, S)[0:stage_rows(what), :]

        Q = ar(A_Q, 8, S)
        biasC = ar(A_BC, 8, NT, NCMP)
        biasA = ar(A_BA, 8, 256)

        gH = nc.alloc_sbuf_tensor_at("g_hi", [P, NC * S], F32R, offset=arena_at)
        gL = nc.alloc_sbuf_tensor_at("g_lo", [P, NC * S], F32R, offset=arena_at + NC * S * 4)

        head_sq = nc.alloc_sbuf_tensor_at("head_sq", [P, NC * S], F32, offset=h_hi_at)
        cmp_w2 = nc.alloc_sbuf_tensor_at("cmp_w2", [P, NC * S], F32, offset=h_hi_at)
        qlat = nc.alloc_sbuf_tensor_at("q_latent", [P, NC * S], F32, offset=h_lo_at)

        consts_in = sem("consts_in")
        x_in = sem("x_in")
        m2_in = sem("m2_in")
        raw_in = [sem(f"raw_in{i}") for i in range(NSTREAM)]
        ada_in = [sem(f"ada_in{i}") for i in range(NADA)]
        ada_first = [sem(f"ada_first{i}") for i in range(3)]
        hi_done = sem("w_hi_done")
        lo_done = sem("w_lo_done")
        tile_done = sem("tile_done")
        evac_act = sem("evac_act")
        evac_dve = sem("evac_dve")
        evac_sem = {"act": evac_act, "dve": evac_dve}
        nat_evac = sem("nat_evac")
        vt_mm, vt_ev = sem("values_turned"), sem("values_copied")
        ada_used = sem("ada_used")
        ada_sum = sem("ada_sum")
        ada_add = sem("ada_add")
        c_tanh = sem("c_silu")
        dve_chain = sem("dve_chain")
        act_chain = sem("act_chain")
        bias_mm = sem("bias_mm")
        bias_evac = sem("bias_evac")
        bias_out = sem("bias_stored")
        biasA_in, biasB_in, biasC_in = sem("bias_swa_in"), sem("bias_near_in"), sem("bias_cmp_in")
        x_set = sem("x_set")
        n_sq, n_stat, n_var, n_root = sem("norm_sq"), sem("norm_stat"), sem("norm_var"), sem("norm_root")
        n_diag, n_bcast, n_t = sem("norm_diag"), sem("norm_bcast"), sem("norm_t")
        n_mean, n_diag2, n_bcast2 = sem("norm_mean"), sem("norm_mean_diag"), sem("norm_mean_bcast")
        h_hi, h_lo = sem("h_hi_done"), sem("h_lo_done")
        sq_done, g_hi_s, g_lo_s = sem("relu_sq"), sem("g_hi_done"), sem("g_lo_done")
        f_nz, f_e, f_log, f_row = sem("f_neg_abs"), sem("f_exp"), sem("f_log"), sem("f_row")
        f_tr, f_tok = sem("f_transposed"), sem("f_tokens_done")
        nf_diag, nf_mm, nf_copy = sem("nf_diag"), sem("nf_mm"), sem("nf_copy")
        at_sc, at_max, at_pr, at_nm = sem("scores"), sem("row_max"), sem("probs"), sem("probs_scaled")
        at_tr, at_pt, at_pv, at_oe = sem("probs_turned"), sem("pt_copied"), sem("pv_done"), sem("out_copied")
        aux_mm, aux_ev = sem("aux_mm"), sem("aux_evac")
        ix_s, ix_r, ix_a = sem("index_scores"), sem("index_relu"), sem("index_added")
        gi_done = sem("gates_done")
        lat_ev, lat_sq, lat_st, lat_v, lat_r = (sem("lat_copied"), sem("lat_sq"), sem("lat_stat"),
                                                sem("lat_var"), sem("lat_root"))
        lat_t, lat_n, lat_tt, lat_done = sem("lat_turned"), sem("lat_token"), sem("lat_back"), sem("lat_done")
        b_add, c_mm = sem("cmp_in"), sem("cmp_mm_hidden")
        wk_in, wv_in = sem("cmp_wk_in"), sem("cmp_wv_in")
        hid_done, kc_mm, kc_done = sem("cmp_hidden"), sem("cmp_mm"), sem("cmp_done")
        l_conv, l_mm, l_sig, l_ixc, l_te, l_m, l_sq, l_y = (sem("lru_conv"), sem("lru_mm"), sem("lru_sig"),
                                                            sem("lru_ixc"), sem("lru_exp"), sem("lru_m"),
                                                            sem("lru_root"), sem("lru_y"))
        l_lam, l_lam2 = sem("lru_lam"), sem("lru_lam2")
        l_in, l_scan = sem("lru_input"), sem("lru_scanned")
        dl_p, dl_mm, dl_e, dl_done = sem("dlam_prod"), sem("dlam_sum"), sem("dlam_exp"), sem("dlam_done")
        d_sq, d_st, d_v, d_r, d_diag, d_bc, d_y = (sem("diff_sq"), sem("diff_stat"), sem("diff_var"),
                                                   sem("diff_root"), sem("diff_diag"), sem("diff_bcast"),
                                                   sem("diff_y"))
        out_s = sem("out_stored")

        X_SETS = {"o3": 1, "m1": 2, "o4": 3, "m2": 4}

        block = ctx.enter_context(nc.Block())

        H_ORDER = ["n0", "y1", "n1", "xc", "y2", "n2", "y3", "n3", "n4", "y4", "n5"]
        h_base = {name: 8 * n for n, name in enumerate(H_ORDER)}
        H_OF_PHASE = {"p1": "n0", "o1": "y1", "lin": "n1", "o2": "y2", "ev1": "n2", "o3": "y3", "m1": "n3",
                      "od": "n4", "o4": "y4", "m2": "n5"}

        @block.sync
        def _(sp):
            sp.dma_start(cv[:, :], CV).then_inc(consts_in, 16)
            sp.dma_start(cc[:, :], CC).then_inc(consts_in, 16)
            sp.dma_start(slab[0:34, 0:OHW], OH).then_inc(consts_in, 16)

            def ada_batch(k):
                sp.dma_start(ar(A_ADA[k], 4, BLK), WA[4 * k:4 * k + 4].rearrange("n p w -> p n w")).then_inc(
                    ada_first[k], 16)

            ada_batch(0)
            ada_batch(1)
            sp.dma_start(x[:, :, :], X.rearrange("p (c s) -> p c s", c=NC)).then_inc(x_in, 16)
            ada_batch(2)

            def ada_block(n):
                if n >= ADA_EARLY + NADA:
                    sp.wait_ge(ada_used, n - NADA + 1)
                sp.dma_start(adaw[:, n % NADA, :], WA[n]).then_inc(ada_in[n % NADA], 16)

            def weight_block(t):
                if t >= NSTREAM:
                    sp.wait_ge(lo_done, t - NSTREAM + 1)
                sp.dma_start(wraw[:, t % NSTREAM, :], W[t]).then_inc(raw_in[t % NSTREAM], 16)

            def skew(U, at, step, pattern):
                return bass.AP(U.tensor, U.offset + at, [[step, 16]] + pattern)

            sp.wait_ge(bias_evac, 1)
            u = slab[0:24, A_U:A_U + BAND]
            sp.dma_start(UB, u.unsqueeze(1).to_broadcast([24, 16, BAND])).then_inc(bias_out, 16)
            sp.dma_start(UC, slab[0:24, A_U + BAND:A_U + BAND + CBAND]).then_inc(bias_out, 16)
            for n in range(ADA_EARLY, ADA_FIRST):
                ada_block(n)
            for t in range(NTILE):
                weight_block(t)
                if 2 <= t < 10:
                    sp.wait_ge(bias_out, 32)
                    a = t - 2
                    at = slice(16 * a, 16 * a + 16)
                    band = 16 * BAND
                    sp.dma_start(biasA[at], skew(UB, P - 1 - 16 * a, BAND - 1,
                                                 [[band, 8], [1, 256]])).then_inc(biasA_in, 16)
                    sp.dma_start(biasB[at], skew(UB, 8 * band + P - 1 - 16 * a, BAND - 1,
                                                 [[band, 16], [1, 256]])).then_inc(biasB_in, 16)
                    for qb in range(NT):
                        sp.dma_start(biasC[at, :, qb, :], skew(UC, 8 * CBAND + 31 - 8 * qb - a, 62,
                                                               [[CBAND, 8], [1, NCMP]])).then_inc(biasC_in, 16)
                for n in ADA_AT.get(t, []):
                    ada_block(n)
                if t == PHASE["ev2"][6]:
                    sp.wait_ge(ix_a, 24)
                    sp.dma_start(ar(A_IQ, 2048), WC[0][:, 0:2048]).then_inc(wk_in, 16)
                    sp.dma_start(E[:, :, :].rearrange("p a s -> p (a s)"), WC[0][:, 2048:4096]).then_inc(wk_in, 16)
                if t == PHASE["o3"][1]:
                    sp.wait_ge(tile_done, PHASE["o3"][0])
                    sp.dma_start(cmp_w2[:, :], WC[1]).then_inc(wv_in, 16)
                if t == PHASE["ev1"][1]:
                    sp.wait_ge(h_lo, h_base["n2"] + 8)
                    sp.dma_start(ar(A_M2, M2W), M2).then_inc(m2_in, 16)
            for c in range(NC):
                sp.wait_ge(h_hi, h_base["n5"] + 8 + c + 1)
                sp.dma_start(OUT[:, c, :], t8[:, c, :]).then_inc(out_s, 16)
            sp.wait_ge(out_s, 16 * NC)

        @block.gpsimd
        def _(pool):
            for t in range(NTILE):
                if t == PHASE["o2"][0] + 2:
                    for c in range(NC):
                        pool.wait_ge(h_hi, h_base["y2"] + c + 1)
                        nc.gpsimd.tensor_tensor(hL[:, c * S:(c + 1) * S], ar(A_XC, 8, S)[:, c, :],
                                                hH[:, c * S:(c + 1) * S].bitcast(F32),
                                                ALU.subtract).then_inc(h_lo, 1)
                for name, phase in (("n3", "m1"), ("n4", "od"), ("n5", "m2")):
                    if t == min(PHASE[phase][0] + 2, NTILE):
                        for c in range(NC):
                            pool.wait_ge(h_hi, h_base[name] + c + 1)
                            nc.gpsimd.tensor_tensor(hL[:, c * S:(c + 1) * S], E[:, c % 4, :],
                                                    hH[:, c * S:(c + 1) * S].bitcast(F32),
                                                    ALU.subtract).then_inc(h_lo, 1)
                pool.wait_ge(hi_done, t + 1)
                s = t % NSTREAM
                nc.gpsimd.tensor_tensor(wL[:, s, :], wraw[:, s, :], wH[:, s, :].bitcast(F32),
                                        ALU.subtract).then_inc(lo_done, 1)

        @block.scalar
        def _(act):
            chain = [0]
            nexthi = [0]
            aux = [0]

            def link(ins):
                chain[0] += 1
                ins.then_inc(act_chain, 1)
                act.wait_ge(act_chain, chain[0])

            def ahead(upto):
                while nexthi[0] <= min(upto, NTILE - 1):
                    t = nexthi[0]
                    act.wait_ge(raw_in[t % NSTREAM], 16 * (t // NSTREAM + 1))
                    if t >= NSTREAM:
                        act.wait_ge(tile_done, t - NSTREAM + 1)
                    nc.scalar.activation(wH[:, t % NSTREAM, :], wraw[:, t % NSTREAM, :],
                                         ACT.Copy).then_inc(hi_done, 1)
                    nexthi[0] += 1

            def copy(out, in_, scale=1.0):
                return nc.scalar.activation(out, in_, ACT.Copy, scale=scale)

            def bias_build():
                act.wait_ge(bias_mm, 1)
                copy(slab[0:24, A_U:A_U + BAND], SB[0][0:24, 0:BAND])
                copy(slab[0:24, A_U + BAND:A_U + BAND + 496], SB[1][0:24, 0:496])
                copy(slab[0:24, A_U + BAND + 496:A_U + BAND + CBAND], TB[0][0:24, 0:496]).then_inc(bias_evac, 1)

            def norm(n, name, sets_x):
                if n == 0:
                    act.wait_ge(x_in, 16)
                    for c in range(NC):
                        square(c)
                    ahead(1)
                else:
                    act.wait_ge(evac_dve, resid[0])
                    square(NC - 1)
                act.wait_ge(n_var, n + 1)
                nc.scalar.activation(rst[:, :], st[:, 0:4], ACT.Sqrt).then_inc(n_root, 1)
                for c in range(NC):
                    act.wait_ge(n_t, NC * n + c + 1)
                    if name is None:
                        nc.scalar.activation(t8[:, c, :], t8[:, c, :], ACT.Identity, bias=ncol[:, 1, c:c + 1],
                                             scale=ncol[:, 0, c:c + 1]).then_inc(h_hi, 1)
                        continue
                    if c >= 4:
                        act.wait_ge(h_lo, h_base[name] + c - 3)
                    link(nc.scalar.activation(E[:, c % 4, :], t8[:, c, :], ACT.Identity, bias=ncol[:, 1, c:c + 1],
                                              scale=ncol[:, 0, c:c + 1]))
                    copy(hH[:, c * S:(c + 1) * S], E[:, c % 4, :]).then_inc(h_hi, 1)
                if sets_x:
                    for c in range(NC):
                        ins = nc.scalar.activation(x[:, c, :], t8[:, c, :], ACT.Identity, bias=ncol[:, 3, c:c + 1],
                                                   scale=ncol[:, 2, c:c + 1])
                    sets[0] += 1
                    ins.then_inc(x_set, 1)
                    act.wait_ge(x_set, sets[0])

            sets = [0]

            def square(c):
                nc.scalar.activation(t8[:, c, :], x[:, c, :], ACT.Square).then_inc(n_sq, 1)

            resid = [0]

            def split_y():
                for c in range(NC):
                    copy(hH[:, c * S:(c + 1) * S], Q[:, c, :]).then_inc(h_hi, 1)

            up = [0]

            def up_hi():
                n = up[0]
                act.wait_ge(sq_done, n + 1)
                copy(gH[:, (n % 8) * S:(n % 8 + 1) * S], t8[:, 2 + n % 2, :]).then_inc(g_hi_s, 1)
                up[0] += 1

            ups = [0]

            def tiles(phase):
                for t in PHASE[phase]:
                    _, kind, what = TILES[t]
                    ahead(t + 2)
                    name = what[0]
                    turned_last = [TILES[t - 1][2]] if t and TILES[t - 1][2][0] in TURNED else []
                    if kind == "T" and EVAC[t][0] == "dve":
                        resid[0] = EVAC[t][1]
                        if name == "down" and what[1] == 0:
                            up_hi()
                        if t in STAT_AFTER:
                            act.wait_ge(evac_dve, EVAC[t][1] - 1)
                            square(what[1] - 1)
                        continue
                    if kind == "T":
                        act.wait_ge(tile_done, t + 1)
                        ps, i = LB[T_INDEX[t] % 2], what[1]
                        if name == "q":
                            ins = copy(Q[:, i, :], ps[:, :], DSCALE)
                        elif name == "ak":
                            ins = copy(ar(A_AK, S), ps[:, :])
                        elif name in TURNED:
                            ins = copy(stage(what), ps[0:stage_rows(what), :])
                        elif name == "bk":
                            ins = copy(ar(A_BK, 4, S)[:, i, :], ps[:, :])
                        elif name == "f":
                            nc.scalar.activation(frow[:, :], ps[0:8, :], ACT.Identity,
                                                 bias=col("bf")[0:8, :]).then_inc(evac_act, 1)
                            continue
                        elif name == "gate":
                            if i == 0:
                                act.wait_ge(f_nz, 1)
                                nc.scalar.activation(E[:, 0, 32:64], E[:, 0, 32:64], ACT.Exp).then_inc(f_e, 1)
                            ins = nc.scalar.activation(ar(A_GT, 8, S)[:, i, :], ps[:, :], ACT.Silu)
                        elif name == "xr":
                            ins = copy(ar(A_XR, 8, XRW)[:, i, 3:XRW], ps[:, :])
                        elif name == "lgate":
                            ins = nc.scalar.activation(ar(A_LG, 8, S)[:, i, :], ps[:, :], ACT.Silu)
                        elif name == "ik":
                            ins = copy(ar(A_IK, S), ps[:, :])
                        elif name == "iq":
                            ins = copy(ar(A_IQ, 4, S)[:, i, :], ps[:, :])
                        elif name == "kvl":
                            ins = nc.scalar.activation(t8[:, 0, :], ps[:, :], ACT.Copy, scale=1.0)
                        elif name == "ks":
                            ins = copy(ar(A_KS, S), ps[:, :])
                        elif name == "kw":
                            ins = copy(ar(A_KW, S), ps[:, :])
                        elif name == "kc2":
                            d = ar(A_KC2, 4, S)
                            for gg in range(2):
                                src = ps[HD * gg:HD * gg + HD, :]
                                copy(d[0:HD, 2 * i + gg, :], src)
                                ins = copy(d[HD:P, 2 * i + gg, 0:S - 1], src[:, 1:S])
                        elif name == "dk":
                            ins = copy(ar(A_DK, 8, S)[:, i, :], ps[:, :])
                        elif name == "up":
                            n = ups[0]
                            if n >= 2:
                                act.wait_ge(sq_done, n - 1)
                            nc.scalar.activation(t8[:, n % 2, :], ps[:, :], ACT.Relu).then_inc(evac_act, 1)
                            ups[0] += 1
                            if i > 0:
                                up_hi()
                            continue
                        ins.then_inc(evac_act, 1)
                    elif kind == "N" and what[1] == what[2] - 1:
                        act.wait_ge(tile_done, t + 1)
                        for tb in range(NT):
                            ps = NB[tb]
                            if name == "vb":
                                ins = copy(ar(A_VB, NT, S)[:, tb, :], ps[:, :])
                            else:
                                k = int(name[2])
                                ins = copy(ar(A_DV, NT, 1024)[:, tb, 512 * k:512 * k + 512], ps[:, :])
                        ins.then_inc(nat_evac, 1)
                    for last in turned_last:
                        turned_evac(last)
                    if name == "kvl":
                        latent_act()

            turns = [0]

            def turned_evac(what):
                name, i = what
                turns[0] += 1
                act.wait_ge(vt_mm, turns[0])
                if name == "gi":
                    v = TB[1][:, 0:NT * 32].rearrange("p (t n) -> p t n", t=NT)
                    gi = ar(A_GI, NT, 32)
                    nc.scalar.activation(gi[:, :, 0:24], v[:, :, 0:24], ACT.Sigmoid)
                    ins = copy(gi[:, :, 24:32], v[:, :, 24:32], 8 ** -0.5 * 64 ** -0.5)
                else:
                    v = TB[1][:, :].rearrange("p (t n) -> p t n", t=NT)
                    dst = ar(A_VA, NT, P) if name == "va" else ar(A_VN, NT, 256)[:, :, P * i:P * i + P]
                    ins = copy(dst, v)
                ins.then_inc(vt_ev, 1)

            def latent_act():
                act.wait_ge(evac_act, EVAC[PHASE["ev2"][0]][1])
                nc.scalar.activation(t8[:, 4, :], t8[:, 0, :], ACT.Square).then_inc(lat_sq, 1)
                link(nc.scalar.activation(t8[:, 5, :], t8[:, 0, :], ACT.Copy, scale=col("kvn")))
                act.wait_ge(lat_v, 1)
                nc.scalar.activation(rst[:, :], st[:, 0:4], ACT.Sqrt).then_inc(lat_r, 1)

            def latent_act2():
                act.wait_ge(lat_t, 1)
                act.wait_ge(lat_r, 1)
                for tb in range(NT):
                    ins = nc.scalar.activation(ar(A_CKN, NT, P)[:, tb, :], TB[0][:, tb * P:(tb + 1) * P],
                                               ACT.Copy, scale=rst[:, tb:tb + 1])
                ins.then_inc(lat_n, 1)
                act.wait_ge(lat_tt, 1)
                copy(ar(A_CKT, S), TB[1][:, :]).then_inc(lat_done, 1)

            def f_rows():
                act.wait_ge(f_tr, 3)
                copy(ftok[:, :, :], TB[0][:, 0:32].rearrange("p (t h) -> p t h", t=NT)).then_inc(f_tok, 1)

            def attend(phase):
                steps = ATT[phase]

                def exps(s):
                    act.wait_ge(at_max, s["i"] + 1)
                    if s["kind"] == "cmp":
                        e = E[:, s["i"] % 4, 0:s["nk"]]
                        nc.scalar.activation(e, e, ACT.Exp).then_inc(at_pr, 1)
                        return
                    i, n = s["i"] % 4, s["nk"] + (s["kind"] == "swa")
                    nc.scalar.activation(E[:, i, 0:n], E[:, i, 0:n], ACT.Exp, bias=nmx[:, i:i + 1],
                                         accum_out=rsum[:, i:i + 1]).then_inc(at_pr, 1)

                def turned_copy(s):
                    if s["j"] is None:
                        return
                    act.wait_ge(at_tr, s["j"] + 1)
                    at, before = turned_at(s)
                    if s["qb"] == 0 and before >= 0:
                        act.wait_ge(at_pv, before + 1)
                    a, b = s["slots"]
                    if s["kind"] == "cmp":
                        dst, src = at[0:NCMP, 0, :], TB[s["j"] % 2][0:NCMP, :]
                    else:
                        dst = at[:, a:b, s["qb"] * P:(s["qb"] + 1) * P]
                        src = TB[s["j"] % 2][:, a * P:b * P].rearrange("p (k q) -> p k q", q=P)
                    copy(dst, src).then_inc(at_pt, 1)

                def nf(h):
                    act.wait_ge(nf_mm, h + 1)
                    if h >= 1:
                        act.wait_ge(at_max, ATT["fgt"][4 * (h - 1)]["i"])
                    copy(ar(A_BA + 1024 * (h % 2), S), AB[:, :]).then_inc(nf_copy, 1)

                def aux_evac(dst, src):
                    aux[0] += 1
                    act.wait_ge(aux_mm, aux[0])
                    copy(dst, src).then_inc(aux_ev, 1)

                if phase == "fgt":
                    nf(0)
                for n in range(len(steps) + LAG_POST + 1):
                    if n < len(steps):
                        s = steps[n]
                        if phase == "fgt" and s["qb"] == NT - 1 and s["u"] < 7:
                            nf(s["u"] + 1)
                        if s["kind"] == "sel" and s["qb"] == 0:
                            aux_evac(qlat[:, s["u"] * S:(s["u"] + 1) * S], LB[0][:, :])
                        exps(s)
                    if 0 <= n - LAG_TR < len(steps):
                        turned_copy(steps[n - LAG_TR])
                    m = n - LAG_POST
                    if phase == "dsa" and 0 <= m < len(steps) and steps[m]["end"]:
                        u = steps[m]["u"]
                        b = HD * (u % 2)
                        aux_evac(Q[b:b + HD, 4 + u // 2, :], LB[0][b:b + HD, :])
                    if phase == "dif" and 0 <= m < len(steps) and steps[m]["end"]:
                        u = steps[m]["u"]
                        act.wait_ge(at_oe, steps[m]["g"] + 1)
                        nc.scalar.activation(head_sq[:, u * S:(u + 1) * S], Q[:, u, :], ACT.Square).then_inc(d_sq, 1)

            act.wait_ge(consts_in, 48)
            nc.scalar.activation(cact[:, :], cv[:, 0:16], ACT.Silu).then_inc(c_tanh, 1)
            bias_build()
            norm(0, "n0", False)
            act.wait_ge(bias_out, 32)
            tiles("p1")
            f_rows()
            attend("swa")
            attend("fgt")
            act.wait_ge(at_oe, ATT["fgt"][-1]["g"] + 1)
            split_y()
            tiles("o1")
            norm(1, "n1", False)
            tiles("lin")
            act.wait_ge(l_lam, 1)
            nc.scalar.activation(k8[:, 1, :], k8[:, 0, :], ACT.Exp).then_inc(l_lam2, 1)
            t_g = PHASE["lcore"][0]
            ahead(t_g + 2)
            act.wait_ge(tile_done, t_g)
            for c in range(NC):
                act.wait_ge(l_conv, c + 1)
                copy(hH[:, c * S:(c + 1) * S], ar(A_XC, 8, S)[:, c, :]).then_inc(h_hi, 1)
            for c in range(NC):
                if c < NC - 1:
                    act.wait_ge(l_mm, 2 * c + 2)
                else:
                    act.wait_ge(tile_done, t_g + 2)
                nc.scalar.activation(t8[:, c, :], NB[2 * (c % 2)][:, :], ACT.Sigmoid, bias=col("ba", c, c + 1))
                if c >= 4:
                    act.wait_ge(l_ixc, c - 3)
                nc.scalar.activation(E[:, c % 4, :], NB[2 * (c % 2) + 1][:, :], ACT.Sigmoid,
                                     bias=col("bx", c, c + 1)).then_inc(l_sig, 1)
            ahead(t_g + 3)
            act.wait_ge(l_lam, 2)
            act.wait_ge(l_sig, NC)
            for c in range(NC):
                nc.scalar.activation(ar(A_XR, 8, S)[:, c, :], t8[:, c, :], ACT.Exp, scale=k8[:, 5, c:c + 1])
                nc.scalar.activation(t8[:, c, :], t8[:, c, :], ACT.Tanh,
                                     scale=k8[:, 4, c:c + 1]).then_inc(l_te, 1)
            for c in range(NC):
                act.wait_ge(l_m, c + 1)
                nc.scalar.activation(t8[:, c, :], t8[:, c, :], ACT.Sqrt).then_inc(l_sq, 1)
            for c in range(NC):
                act.wait_ge(l_y, c + 1)
                copy(hH[:, c * S:(c + 1) * S], ar(A_XC, 8, S)[:, c, :]).then_inc(h_hi, 1)
            tiles("o2")
            norm(2, "n2", True)
            tiles("ev1")
            n = 0
            for qb in range(1, NT):
                for j in range(8):
                    act.wait_ge(ix_s, n + 1)
                    if n >= 4:
                        act.wait_ge(ix_a, n - 3)
                    nc.scalar.activation(E[:, n % 4, 0:P * (qb + 1)], SB[n % 2][:, 0:P * (qb + 1)],
                                         ACT.Relu).then_inc(ix_r, 1)
                    n += 1
            tiles("ev2")
            latent_act2()
            ahead(PHASE["o3"][0] + 1)
            for kv in range(2):
                act.wait_ge(c_mm, kv + 1)
                for hc in range(2):
                    ins = nc.scalar.activation(ar(A_HID, 4, 62)[:, 2 * kv + hc, :], LB[hc][:, 0:62],
                                               ACT.Gelu_apprx_tanh)
                ins.then_inc(hid_done, 1)
            act.wait_ge(kc_mm, 1)
            copy(ar(A_KCT, 32)[0:HD, 0:NCMP], SB[0][0:HD, 0:NCMP])
            copy(ar(A_KCT, 32)[HD:P, 0:NCMP], SB[0][HD:P, NCMP:2 * NCMP])
            copy(ar(A_VCN, P)[0:NCMP, :], SB[1][0:NCMP, 0:P]).then_inc(kc_done, 1)
            attend("nsa")
            attend("dsa")
            act.wait_ge(aux_ev, 16)
            split_y()
            tiles("o3")
            norm(3, "n3", True)
            tiles("m1")
            norm(4, "n4", True)
            tiles("od")
            act.wait_ge(dl_mm, 1)
            nc.scalar.activation(dlam[:, 4:6], AB[:, 0:2], ACT.Exp).then_inc(dl_e, 1)
            attend("dif")
            act.wait_ge(at_oe, ATT["dif"][-1]["g"] + 1)
            act.wait_ge(d_v, 1)
            nc.scalar.activation(k8[:, 0:4, :].rearrange("p a b -> p (a b)"), k8[:, 0:4, :].rearrange("p a b -> p (a b)"),
                                 ACT.Sqrt).then_inc(d_r, 1)
            for c in range(NC):
                act.wait_ge(d_y, c + 1)
                copy(hH[:, c * S:(c + 1) * S], Q[:, c, :]).then_inc(h_hi, 1)
            tiles("o4")
            norm(5, "n5", True)
            tiles("m2")
            norm(6, None, False)

        @block.vector
        def _(dve):
            V = nc.vector
            chain = [0]
            pending = []

            def link(ins):
                chain[0] += 1
                ins.then_inc(dve_chain, 1)
                dve.wait_ge(dve_chain, chain[0])

            def ada_bias():
                g = pending.pop()
                dve.wait_ge(ada_sum, g + 1)
                V.tensor_tensor(adac[:, 8 * g:8 * g + 8], AB[:, 0:8], col("adab", 8 * g, 8 * g + 8),
                                ALU.add).then_inc(ada_add, 1)

            def ada_block(n):
                if n % 8 == 0 and pending:
                    ada_bias()
                if n < ADA_EARLY:
                    dve.wait_ge(ada_first[n // 4], 16)
                    w = ar(A_ADA[n // 4], 4, BLK)[:, n % 4, :]
                else:
                    dve.wait_ge(ada_in[n % NADA], 16 * ((n - ADA_EARLY) // NADA + 1))
                    w = adaw[:, n % NADA, :]
                c = (0 if n < 48 else 8) + n % 8
                if n:
                    dve.wait_ge(ada_used, n)
                if n % 8 == 0:
                    if n:
                        dve.wait_ge(ada_sum, n // 8)
                    ins = V.tensor_scalar(acc[:, :], w, cact[:, c:c + 1], None, ALU.mult)
                else:
                    ins = V.scalar_tensor_tensor(acc[:, :], w, cact[:, c:c + 1], acc[:, :],
                                                 ALU.mult, ALU.add)
                ins.then_inc(ada_used, 1)
                if n % 8 == 7:
                    pending.append(n // 8)

            def ada_slot(t):
                if pending and t in after_fin:
                    ada_bias()
                for n in ADA_AT.get(t, []):
                    ada_block(n)

            after_fin = {t + 1 for t in FIN_AT}

            def sub(out, a, b):
                return V.tensor_tensor(out, a, b, ALU.subtract)

            def low(c, src):
                return sub(hL[:, c * S:(c + 1) * S], src, hH[:, c * S:(c + 1) * S].bitcast(F32))

            def acol(g):
                return adac[:, 8 * g:8 * g + 8]

            def cols(shift, scale, g, b, fg, fb):
                dve.wait_ge(ada_add, max(shift, scale) + 1)
                dve.wait_ge(consts_in, 48)
                link(V.scalar_tensor_tensor(ncol[:, 0, :], acol(scale), 1.0, g, ALU.add, ALU.mult))
                if b is None:
                    link(V.tensor_copy(ncol[:, 1, :], acol(shift)))
                else:
                    link(V.scalar_tensor_tensor(ncol[:, 1, :], acol(scale), 1.0, b, ALU.add, ALU.mult))
                    link(V.tensor_tensor(ncol[:, 1, :], ncol[:, 1, :], acol(shift), ALU.add))
                if fg is not None:
                    link(V.tensor_scalar(ncol[:, 2, :], fg, ALPHA, None, ALU.mult))
                    if fb is None:
                        link(V.memset(ncol[:, 3, :], 0.0))
                    else:
                        link(V.tensor_scalar(ncol[:, 3, :], fb, ALPHA, None, ALU.mult))

            means = [0]

            def norm(n, name, eps, centred):
                dve.wait_ge(n_stat, n + 1)
                if not centred:
                    link(V.tensor_scalar(st[:, 8:12], TB[0][:, 0:4], 1.0 / D, eps, ALU.mult, ALU.add))
                else:
                    link(V.tensor_scalar(st[:, 4:8], TB[0][:, 4:8], 1.0 / D, None, ALU.mult))
                    link(V.tensor_tensor(st[:, 12:16], st[:, 4:8], st[:, 4:8], ALU.mult))
                    link(V.scalar_tensor_tensor(st[:, 16:20], TB[0][:, 0:4], 1.0 / D, st[:, 12:16], ALU.mult,
                                                ALU.subtract))
                    link(V.tensor_scalar(st[:, 8:12], st[:, 16:20], eps, None, ALU.add))
                V.reciprocal(st[:, 0:4], st[:, 8:12]).then_inc(n_var, 1)
                dve.wait_ge(n_root, n + 1)
                if centred:
                    V.tensor_tensor(st[:, 20:24], st[:, 4:8], rst[:, :], ALU.mult).then_inc(n_mean, 1)
                for tb in range(NT):
                    ins = V.tensor_scalar(E[:, 0, tb * P:(tb + 1) * P], ident, rst[:, tb:tb + 1], None, ALU.mult)
                ins.then_inc(n_diag, 1)
                if centred:
                    means[0] += 1
                    dve.wait_ge(n_mean, means[0])
                    for tb in range(NT):
                        ins = V.tensor_scalar(E[:, 1, tb * P:(tb + 1) * P], ident, st[:, 20 + tb:21 + tb], None,
                                              ALU.mult)
                    ins.then_inc(n_diag2, 1)
                dve.wait_ge(n_bcast, n + 1)
                for c in range(NC + 1):
                    if c < NC:
                        if centred:
                            link(V.tensor_tensor(t8[:, c, :], x[:, c, :], SB[0][:, :], ALU.mult))
                            if c == 0:
                                dve.wait_ge(n_bcast2, means[0])
                            V.tensor_tensor(t8[:, c, :], t8[:, c, :], SB[1][:, :], ALU.subtract).then_inc(n_t, 1)
                        else:
                            V.tensor_tensor(t8[:, c, :], x[:, c, :], SB[0][:, :], ALU.mult).then_inc(n_t, 1)
                    if c > 0 and name is not None and not centred:
                        dve.wait_ge(h_hi, h_base[name] + c)
                        low(c - 1, E[:, (c - 1) % 4, :]).then_inc(h_lo, 1)

            def split_y(name):
                for c in range(NC):
                    dve.wait_ge(h_hi, h_base[name] + c + 1)
                    low(c, Q[:, c, :]).then_inc(h_lo, 1)

            up = [0, 0]

            def up_lo():
                n = up[1]
                dve.wait_ge(g_hi_s, n + 1)
                sub(gL[:, (n % 8) * S:(n % 8 + 1) * S], t8[:, 2 + n % 2, :],
                    gH[:, (n % 8) * S:(n % 8 + 1) * S].bitcast(F32)).then_inc(g_lo_s, 1)
                up[1] += 1

            def tiles(phase, gate=None, hook=None):
                for t in PHASE[phase]:
                    _, kind, what = TILES[t]
                    if what[0] == "down" and what[1] == 0:
                        up_lo()
                    ada_slot(t)
                    if kind == "T" and EVAC[t][0] == "dve":
                        c = what[1]
                        dve.wait_ge(tile_done, t + 1)
                        if phase in X_SETS:
                            dve.wait_ge(x_set, X_SETS[phase])
                        if EVAC[t][1] > 1:
                            dve.wait_ge(evac_dve, EVAC[t][1] - 1)
                        V.scalar_tensor_tensor(x[:, c, :], LB[T_INDEX[t] % 2][:, :], gate[:, c:c + 1], x[:, c, :],
                                               ALU.mult, ALU.add).then_inc(evac_dve, 1)
                    elif what[0] == "up":
                        n = up[0]
                        dve.wait_ge(evac_act, EVAC[t][1])
                        if n >= 2:
                            dve.wait_ge(g_lo_s, n - 1)
                        V.tensor_tensor(t8[:, 2 + n % 2, :], t8[:, n % 2, :], t8[:, n % 2, :],
                                        ALU.mult).then_inc(sq_done, 1)
                        up[0] += 1
                        if what[1] > 0:
                            up_lo()
                    elif hook:
                        hook(t, what)
                if pending and 8 * pending[0] + 7 in ADA_AT.get(t - 1, []):
                    ada_bias()

            def log1p_series(e, s, s2, p):
                link(V.tensor_scalar(s, e, 2.0, None, ALU.add))
                link(V.reciprocal(s2, s))
                link(V.tensor_tensor(s, s2, e, ALU.mult))
                link(V.tensor_tensor(s2, s, s, ALU.mult))
                link(V.tensor_scalar(p, s2, 1.0 / 15, None, ALU.mult))
                for k in (13, 11, 9, 7, 5, 3):
                    link(V.scalar_tensor_tensor(p, p, 1.0 / k, s2, ALU.add, ALU.mult))
                link(V.scalar_tensor_tensor(s, p, 1.0, s, ALU.add, ALU.mult))

            fz, fe = E[:, 0, 0:32], E[:, 0, 32:64]
            fs, fs2, fp = E[:, 1, 0:32], E[:, 2, 0:32], E[:, 3, 0:32]

            def f_rows(t, what):
                if what == ("vb", 2, 4):
                    dve.wait_ge(f_tr, 1)
                    link(V.tensor_copy(fz, TB[0][:, 0:32]))
                    V.scalar_tensor_tensor(fe, fz, -1.0, fz, ALU.mult, ALU.min).then_inc(f_nz, 1)
                elif what == ("gate", 1):
                    dve.wait_ge(f_e, 1)
                    log1p_series(fe, fs, fs2, fp)
                    link(V.tensor_scalar(fz, fz, 0.0, None, ALU.min))
                    V.scalar_tensor_tensor(fs2, fs, -2.0, fz, ALU.mult, ALU.add).then_inc(f_log, 1)
                elif what == ("gate", 5):
                    dve.wait_ge(f_tr, 2)
                    link(V.memset(E[0:8, 3, :], 1.0))
                    V.tensor_tensor_scan(frow[:, :], E[0:8, 3, :], TB[0][0:8, :], 0.0, ALU.mult,
                                         ALU.add).then_inc(f_row, 1)

            def attend(phase):
                steps = ATT[phase]

                def nf_diag_rows(h):
                    if h:
                        dve.wait_ge(nf_mm, h)
                    V.tensor_scalar(ar(A_AK, S)[0:8, :], frow[:, :], ident[0:8, h:h + 1], -1.0, ALU.mult,
                                    ALU.mult).then_inc(nf_diag, 1)

                def nf_masked(h):
                    dve.wait_ge(nf_copy, h + 1)
                    a = ar(A_BA + 1024 * (h % 2), NT, P)
                    b = ar(A_BA + 1024 * (h % 2) + S, NT, P)
                    link(V.tensor_tensor(b, a, tri.unsqueeze(1).to_broadcast([P, NT, P]), ALU.add))

                def mark(ins):
                    chain[0] += 1
                    ins.then_inc(dve_chain, 1)
                    return chain[0]

                def by_block(s):
                    return E[:, s["i"] % 4, 0:NT * NCMP].rearrange("p (q n) -> p q n", q=NT)

                def each(v):
                    return v.unsqueeze(2).to_broadcast([P, NT, NCMP])

                def logits(s):
                    i, nk, qb, kind, u = s["i"], s["nk"], s["qb"], s["kind"], s["u"]
                    if i >= 4:
                        dve.wait_ge(at_tr, STEP[i - 4]["tr_after"])
                    dve.wait_ge(at_sc, i + 1)
                    e, ps = E[:, i % 4, :], score_bank(s)
                    near = max(0, nk - 256)
                    if kind == "swa":
                        h = u // 2 + 4 * (u % 2)
                        V.tensor_tensor(e[:, 0:nk], ps[:, 0:nk], biasA[:, h, 256 - nk:256], ALU.add)
                        return mark(V.tensor_copy(e[:, nk:nk + 1], col("sink", h, h + 1)))
                    if kind == "fgt":
                        a, b = ar(A_BA + 1024 * (u % 2), S), ar(A_BA + 1024 * (u % 2) + S, S)
                        d = nk - P
                        if d:
                            V.scalar_tensor_tensor(e[:, 0:d], ps[:, 0:d], ftok[:, qb, u:u + 1], a[:, 0:d], ALU.add,
                                                   ALU.add)
                        return mark(V.scalar_tensor_tensor(e[:, d:nk], ps[:, d:nk], ftok[:, qb, u:u + 1], b[:, d:nk],
                                                           ALU.add, ALU.add))
                    if kind == "cmp":
                        h = u // 2 + 4 * (u % 2)
                        link(V.tensor_tensor(e[:, 0:nk], ps[:, 0:nk], biasC[:, h, :, :].rearrange("p q n -> p (q n)"),
                                             ALU.add))
                        link(V.tensor_reduce(st[:, 0:4], by_block(s), AX.X, ALU.max))
                        return None
                    h = {"sel": u // 2 + 4 * (u % 2), "win": u // 2 + 4 * (u % 2), "dsa": 8 + u,
                         "dif": 2 * u + s["half"]}[kind]
                    if kind == "dsa" and qb:
                        pen = ar(A_PEN + (0, 0, 256, 640)[qb], nk)
                        link(V.tensor_tensor(e[:, near:nk], ps[:, near:nk], pen[:, near:nk], ALU.add))
                        if near:
                            V.scalar_tensor_tensor(e[:, 0:near], ps[:, 0:near], col("t31", h, h + 1),
                                                   pen[:, 0:near], ALU.add, ALU.add)
                        return mark(V.tensor_tensor(e[:, near:nk], e[:, near:nk], biasB[:, h, 0:256], ALU.add))
                    if near:
                        V.tensor_scalar(e[:, 0:near], ps[:, 0:near], col("t31", h, h + 1), None, ALU.add)
                    return mark(V.tensor_tensor(e[:, near:nk], ps[:, near:nk], biasB[:, h, 256 - (nk - near):256],
                                                ALU.add))

                def row_max(s, added):
                    i, nk = s["i"], s["nk"] + (s["kind"] == "swa")
                    if s["kind"] == "cmp":
                        V.tensor_tensor(by_block(s), by_block(s), each(st[:, 0:4]), ALU.subtract).then_inc(at_max, 1)
                        return
                    dve.wait_ge(dve_chain, added)
                    V.tensor_reduce(nmx[:, i % 4:i % 4 + 1], E[:, i % 4, 0:nk], AX.X, ALU.max,
                                    negate=True).then_inc(at_max, 1)

                def guard(s):
                    dve.wait_ge(at_pr, s["i"] + 1)
                    r = rsum[:, s["i"] % 4:s["i"] % 4 + 1]
                    if s["kind"] == "cmp":
                        link(V.tensor_reduce(st[:, 4:8], by_block(s), AX.X, ALU.add))
                        r = st[:, 4:8]
                    return mark(V.tensor_scalar(r, r, 1e-30, None, ALU.max))

                def scale(s, guarded):
                    i, nk, kind = s["i"] % 4, s["nk"], s["kind"]
                    e, r = E[:, i, 0:nk], rsum[:, i:i + 1]
                    dve.wait_ge(dve_chain, guarded)
                    link(V.reciprocal(st[:, 4:8], st[:, 4:8]) if kind == "cmp" else V.reciprocal(r, r))
                    if kind in ("cmp", "sel", "win"):
                        h = s["u"] // 2 + 4 * (s["u"] % 2)
                        b = 3 * h + ("cmp", "sel", "win").index(kind)
                        if kind == "cmp":
                            link(V.tensor_tensor(st[:, 4:8], st[:, 4:8], ar(A_GI, NT, 32)[:, :, b], ALU.mult))
                            link(V.tensor_tensor(by_block(s), by_block(s), each(st[:, 4:8]), ALU.mult))
                            ins = V.tensor_tensor(by_block(s), by_block(s), maskc, ALU.mult)
                        else:
                            gate = ar(A_GI, NT, 32)[:, s["qb"], b:b + 1]
                            ins = V.tensor_scalar(e, e, r, gate, ALU.mult, ALU.mult)
                    elif kind == "dif" and s["half"]:
                        link(V.tensor_tensor(r, r, dlam[:, 7:8], ALU.mult))
                        dve.wait_ge(at_nm, s["i"])
                        ins = V.scalar_tensor_tensor(e, e, r, E[:, (s["i"] - 1) % 4, 0:nk], ALU.mult, ALU.add)
                    else:
                        ins = V.tensor_scalar(e, e, r, None, ALU.mult)
                    ins.then_inc(at_nm, 1)

                def out(s):
                    g, u, kind = s["g"], s["u"], s["kind"]
                    dve.wait_ge(at_pv, s["m"] + 1)
                    ps, b = OB[g % 2], HD * (u % 2)
                    if kind in ("swa", "fgt"):
                        c = u // 2 + 4 * (kind == "fgt")
                        ins = V.tensor_tensor(Q[b:b + HD, c, :], ps[b:b + HD, :], ar(A_GT, 8, S)[b:b + HD, c, :],
                                              ALU.mult)
                    elif kind == "win":
                        ins = V.tensor_copy(Q[b:b + HD, u // 2, :], ps[b:b + HD, :])
                    elif kind == "dsa":
                        if u >= 2:
                            dve.wait_ge(aux_mm, 8 + u - 1)
                        ins = V.tensor_copy(ar(A_OL + S * (u % 2), S), ps[:, :])
                    else:
                        ins = V.tensor_copy(Q[:, u, :], ps[:, :])
                    ins.then_inc(at_oe, 1)

                if phase == "fgt":
                    nf_diag_rows(0)
                    nf_masked(0)
                lag_out = LAG_OUT + (3 if phase == "dif" else 0)
                for n in range(len(steps) + lag_out):
                    if n < len(steps):
                        s = steps[n]
                        if phase == "fgt" and s["qb"] == 0 and s["u"] < 7:
                            nf_diag_rows(s["u"] + 1)
                        if phase == "fgt" and s["qb"] == 0 and s["u"] > 0:
                            nf_masked(s["u"])
                        added = logits(s)
                    if 0 <= n - 1 < len(steps):
                        guarded = guard(steps[n - 1])
                    if n < len(steps):
                        row_max(s, added)
                    if 0 <= n - 1 < len(steps):
                        scale(steps[n - 1], guarded)
                    m = n - lag_out
                    if m >= 0 and steps[m]["end"] and steps[m]["last"]:
                        out(steps[m])

            dve.wait_ge(c_tanh, 1)
            for n in range(ADA_FIRST):
                ada_block(n)
            ada_bias()
            cols(0, 1, col("ng0"), None, None, None)
            norm(0, "n0", 1e-6, False)
            tiles("p1", None, f_rows)
            dve.wait_ge(f_row, 1)
            dve.wait_ge(f_tok, 1)
            dve.wait_ge(biasA_in, 16 * 8)
            attend("swa")
            attend("fgt")
            split_y("y1")
            tiles("o1", acol(2))
            cols(3, 4, col("ng1"), None, None, None)
            norm(1, "n1", 1e-6, False)
            link(V.memset(ar(A_XR, 8, XRW)[:, :, 0:3], 0.0))
            xr, xc = ar(A_XR, 8, XRW), ar(A_XC, 8, S)

            def conv(t, what):
                if what[0] != "xr":
                    return
                c = what[1]
                dve.wait_ge(evac_act, EVAC[t][1])
                link(V.tensor_scalar(xc[:, c, :], xr[:, c, 0:S], col("cw", c, c + 1), col("cb", c, c + 1), ALU.mult,
                                     ALU.add))
                for j in range(1, 4):
                    ins = V.scalar_tensor_tensor(xc[:, c, :], xr[:, c, j:j + S], col("cw", 8 * j + c, 8 * j + c + 1),
                                                 xc[:, c, :], ALU.mult, ALU.add)
                    if j < 3:
                        link(ins)
                ins.then_inc(l_conv, 1)

            tiles("lin", None, conv)
            V.scalar_tensor_tensor(k8[:, 0, :], col("lam"), -1.0, col("lam"), ALU.mult, ALU.min).then_inc(l_lam, 1)
            dve.wait_ge(l_lam2, 1)
            log1p_series(k8[:, 1, :], k8[:, 0, :], k8[:, 2, :], k8[:, 3, :])
            link(V.tensor_scalar(k8[:, 2, :], col("lam"), -1.0, 0.0, ALU.mult, ALU.max))
            link(V.scalar_tensor_tensor(k8[:, 3, :], k8[:, 0, :], 2.0, k8[:, 2, :], ALU.mult, ALU.add))
            link(V.tensor_scalar(k8[:, 4, :], k8[:, 3, :], LRU_C, None, ALU.mult))
            V.tensor_scalar(k8[:, 5, :], k8[:, 3, :], -LRU_C, None, ALU.mult).then_inc(l_lam, 1)
            for c in range(NC):
                dve.wait_ge(h_hi, h_base["xc"] + c + 1)
                low(c, xc[:, c, :]).then_inc(h_lo, 1)
            for c in range(NC):
                dve.wait_ge(l_sig, c + 1)
                V.tensor_tensor(xc[:, c, :], E[:, c % 4, :], xc[:, c, :], ALU.mult).then_inc(l_ixc, 1)
            a_ = ar(A_XR, 8, S)
            dve.wait_ge(l_ixc, NC)
            for c in range(NC):
                dve.wait_ge(l_te, c + 1)
                link(V.tensor_tensor(E[:, c % 4, :], a_[:, c, :], a_[:, c, :], ALU.mult))
                V.scalar_tensor_tensor(t8[:, c, :], E[:, c % 4, :], 1.0, t8[:, c, :], ALU.add, ALU.mult).then_inc(l_m, 1)
            for c in range(NC + 1):
                if c < NC:
                    dve.wait_ge(l_sq, c + 1)
                    V.tensor_tensor(t8[:, c, :], t8[:, c, :], xc[:, c, :], ALU.mult).then_inc(l_in, 1)
                if c > 0:
                    dve.wait_ge(l_scan, c)
                    V.tensor_tensor(xc[:, c - 1, :], xc[:, c - 1, :], ar(A_LG, 8, S)[:, c - 1, :],
                                    ALU.mult).then_inc(l_y, 1)
                if c < NC:
                    dve.wait_ge(l_in, c + 1)
                    V.tensor_tensor_scan(xc[:, c, :], a_[:, c, :], t8[:, c, :], 0.0, ALU.mult,
                                         ALU.add).then_inc(l_scan, 1)
            tiles("o2", acol(5))
            cols(6, 7, col("fg"), None, col("fg"), None)
            norm(2, "n2", 1e-6, False)
            link(V.tensor_scalar(acol(8), acol(8), 1.0, None, ALU.add))
            tiles("ev1")
            n = 0
            gi = ar(A_GI, NT, 32)
            dve.wait_ge(vt_ev, 2)
            for qb in range(1, NT):
                nk = P * (qb + 1)
                w = t8[:, qb, 0:nk]
                for j in range(8):
                    dve.wait_ge(ix_r, n + 1)
                    iw = gi[:, qb, 24 + j:25 + j]
                    if n:
                        dve.wait_ge(ix_a, n)
                    if j == 0:
                        ins = V.tensor_scalar(w, E[:, n % 4, 0:nk], iw, None, ALU.mult)
                    else:
                        ins = V.scalar_tensor_tensor(w, E[:, n % 4, 0:nk], iw, w, ALU.mult, ALU.add)
                    ins.then_inc(ix_a, 1)
                    n += 1
            dve.wait_ge(ix_a, n)

            def topk():
                for qb in range(1, NT):
                    nk = P * (qb + 1)
                    w = t8[:, qb, 0:nk]
                    link(V.tensor_tensor(w[:, nk - P:nk], w[:, nk - P:nk], tri, ALU.add))
                    for _ in range(TOPK // 8):
                        link(V.max(st[:, 8:16], w))
                        link(V.match_replace(w, st[:, 8:16], w, -3e38))
                    link(V.tensor_scalar(ar(A_PEN + (0, 0, 256, 640)[qb], nk), w, -2e38, NEG, ALU.is_gt, ALU.mult))

            def latent():
                dve.wait_ge(lat_st, 1)
                link(V.tensor_scalar(st[:, 16:20], TB[0][:, 0:4], 1.0 / P, 1e-5, ALU.mult, ALU.add))
                V.reciprocal(st[:, 0:4], st[:, 16:20]).then_inc(lat_v, 1)

            latent()
            topk()
            kc2 = ar(A_KC2, 4, S)
            dve.wait_ge(evac_act, EVAC[[t for t in PHASE["ev2"] if TILES[t][1] == "T"][-1]][1])
            dve.wait_ge(lat_t, 1)
            for kv in range(2):
                pe = col("pek") if kv == 0 else col("pev")
                for g in range(2):
                    v = kc2[:, 2 * kv + g, :].rearrange("p (n l r) -> p l n r", l=8, r=2)
                    for half in range(2):
                        o = cmp_in(kv).rearrange("p (l g n) -> p l g n", l=16, g=2)[:, 8 * half:8 * half + 8, g, :]
                        i0 = v[:, :, half:half + NCMP, 0]
                        i1 = pe[:, 8 * half:8 * half + 8].unsqueeze(2).to_broadcast([P, 8, NCMP])
                        ins = V.tensor_tensor(o, i0, i1, ALU.add)
                ins.then_inc(b_add, 1)
            dve.wait_ge(biasB_in, 16 * 8)
            dve.wait_ge(biasC_in, 16 * 8 * NT)
            attend("nsa")
            attend("dsa")
            dve.wait_ge(aux_ev, 16)
            split_y("y3")
            tiles("o3", acol(8))
            cols(9, 10, col("lng", 0, 8), col("lnb", 0, 8), col("lng", 0, 8), col("lnb", 0, 8))
            norm(3, "n3", 1e-5, True)
            link(V.tensor_scalar(acol(11), acol(11), 1.0, None, ALU.add))
            tiles("m1", acol(11))
            if pending:
                ada_bias()
            cols(12, 13, col("lng", 8, 16), col("lnb", 8, 16), col("lng", 8, 16), col("lnb", 8, 16))
            norm(4, "n4", 1e-5, True)
            for g in (14, 17):
                link(V.tensor_scalar(acol(g), acol(g), 1.0, None, ALU.add))
            lo, _ = COLS["dlam"]
            lv = cv[0:HD, lo:lo + 4].rearrange("p (a b) -> p a b", b=2)
            V.tensor_tensor(dlam[0:HD, 0:2], lv[:, :, 0], lv[:, :, 1], ALU.mult).then_inc(dl_p, 1)
            tiles("od")
            dve.wait_ge(dl_e, 1)
            link(sub(dlam[:, 6:7], dlam[:, 4:5], dlam[:, 5:6]))
            link(V.tensor_scalar(dlam[:, 7:8], dlam[:, 6:7], LAMBDA_INIT, -1.0, ALU.add, ALU.mult))
            attend("dif")
            dve.wait_ge(d_st, 8)
            v32 = k8[:, 0:4, :].rearrange("p a b -> p (a b)")
            link(V.tensor_scalar(v32, AB[:, 0:32], 1.0 / P, 1e-5, ALU.mult, ALU.add))
            V.reciprocal(v32, v32).then_inc(d_v, 1)
            link(V.tensor_scalar(dlam[:, 0:1], col("sub"), 1.0 - LAMBDA_INIT, None, ALU.mult))
            dve.wait_ge(d_r, 1)
            for h in range(9):
                if h < 8:
                    if h >= 2:
                        dve.wait_ge(d_bc, h - 1)
                    for tb in range(NT):
                        ins = V.tensor_scalar(E[:, h % 2, tb * P:(tb + 1) * P], ident, v32[:, 4 * h + tb:4 * h + tb + 1],
                                              None, ALU.mult)
                    ins.then_inc(d_diag, 1)
                if h > 0:
                    k = h - 1
                    dve.wait_ge(d_bc, k + 1)
                    V.scalar_tensor_tensor(Q[:, k, :], Q[:, k, :], dlam[:, 0:1], SB[k % 2][:, :], ALU.mult,
                                           ALU.mult).then_inc(d_y, 1)
            split_y("y4")
            tiles("o4", acol(14))
            cols(15, 16, col("lng", 16, 24), col("lnb", 16, 24), col("lng", 16, 24), col("lnb", 16, 24))
            norm(5, "n5", 1e-5, True)
            tiles("m2", acol(17))
            link(V.tensor_copy(ncol[:, 0, :], col("lng", 24, 32)))
            link(V.tensor_copy(ncol[:, 1, :], col("lnb", 24, 32)))
            norm(6, None, 1e-5, True)

        @block.tensor
        def _(pe):
            mm = nc.tensor.matmul
            aux = [0]
            nat = [0]

            def mm3(out, a, b, start, stop):
                mm(out, a[0], b[0], start=start, stop=False, skip_group_check=True)
                mm(out, a[0], b[1], start=False, stop=False, skip_group_check=True)
                return mm(out, a[1], b[0], start=False, stop=stop, skip_group_check=True)

            def weights(t, at, n):
                s = t % NSTREAM
                return wH[:, s, at:at + n], wL[:, s, at:at + n]

            def h(at, n):
                return hH[:, at:at + n], hL[:, at:at + n]

            def g(at, n):
                return gH[:, at:at + n], gL[:, at:at + n]

            def finish_ada(grp):
                pe.wait_ge(ada_used, 8 * grp + 8)
                if grp:
                    pe.wait_ge(ada_add, grp)
                for m in range(8):
                    ins = mm(AB[:, m:m + 1], acc[:, m * P:(m + 1) * P], ones[:, 0:1], start=True, stop=True)
                ins.then_inc(ada_sum, 1)

            def bank_free(t):
                n = T_INDEX[t]
                if n >= 2:
                    prev = TL[n - 2]
                    pe.wait_ge(evac_sem[EVAC[prev][0]], EVAC[prev][1])

            TL = list(T_INDEX)
            downs = [0]
            turns = [0]

            def tiles(phase):
                base = h_base.get(H_OF_PHASE.get(phase))
                first = True
                for t in PHASE[phase]:
                    _, kind, what = TILES[t]
                    pe.wait_ge(lo_done, t + 1)
                    if kind == "T":
                        bank_free(t)
                        if nat[0]:
                            pe.wait_ge(nat_evac, nat[0])
                        if what[0] == "down" and what[1] == 0:
                            downs[0] += 1
                        for k in range(NC):
                            if first and base is not None:
                                pe.wait_ge(h_lo, base + k + 1)
                            if what[0] == "down" and what[1] == 0:
                                pe.wait_ge(g_lo_s, 8 * (downs[0] - 1) + k + 1)
                            rhs = g(k * S, S) if what[0] == "down" else h(k * S, S)
                            ins = mm3(LB[T_INDEX[t] % 2][:, :], weights(t, k * P, P), rhs, k == 0, k == NC - 1)
                        ins.then_inc(tile_done, 1)
                    elif kind == "N":
                        name, b, nb = what
                        w = N_WIDTH[name]
                        n = w
                        if b == 0:
                            for d in (1, 2):
                                prev = TL[max(i for i, tt in enumerate(TL) if tt < t) + 1 - d]
                                pe.wait_ge(evac_sem[EVAC[prev][0]], EVAC[prev][1])
                            if nat[0]:
                                pe.wait_ge(nat_evac, nat[0])
                        per = BLK // w
                        for kk in range(per):
                            k = b * per + kk
                            for tb in range(NT):
                                ins = mm3(NB[tb][:, 0:n], h(k * S + tb * P, P), weights(t, kk * w, n), k == 0,
                                          k == NC - 1)
                        ins.then_inc(tile_done, 1)
                        if b == nb - 1:
                            nat[0] += 1
                    first = False
                    if what == ("vb", 1, 4):
                        pe.wait_ge(evac_act, EVAC[[k for k in PHASE["p1"] if TILES[k][2][0] == "f"][0]][1])
                        for tb in range(NT):
                            ins = nc.tensor.transpose(TB[0][:, 8 * tb:8 * tb + 8], frow[:, tb * P:(tb + 1) * P],
                                                      ident[0:8, 0:8])
                        ins.then_inc(f_tr, 1)
                    if what == ("gate", 3):
                        pe.wait_ge(f_log, 1)
                        for tb in range(NT):
                            ins = nc.tensor.transpose(TB[0][0:8, P * tb:P * tb + P], E[:, 2, 8 * tb:8 * tb + 8], ident)
                        ins.then_inc(f_tr, 1)
                    if t and TILES[t - 1][2][0] in TURNED:
                        what1 = TILES[t - 1][2]
                        r = stage_rows(what1)
                        pe.wait_ge(evac_act, EVAC[t - 1][1])
                        if turns[0]:
                            pe.wait_ge(vt_ev, turns[0])
                        turns[0] += 1
                        for tb in range(NT):
                            ins = nc.tensor.transpose(TB[1][:, r * tb:r * tb + r],
                                                      stage(what1)[:, tb * P:(tb + 1) * P], ident[0:r, 0:r])
                        ins.then_inc(vt_mm, 1)
                    if t in STAT_AFTER:
                        stats(phase not in ("o1", "o2"))
                    for grp in FIN_AT.get(t, []):
                        finish_ada(grp)
                    if kind == "T" and what[0] == "kvl":
                        pe.wait_ge(lat_sq, 1)
                        for tb in range(NT):
                            ins = mm(TB[0][:, tb:tb + 1], t8[:, 4, tb * P:(tb + 1) * P], ones[:, 0:1], start=True,
                                     stop=True)
                        ins.then_inc(lat_st, 1)

            stats_done = [0]
            means = [0]

            def stats(centred):
                c = stats_done[0] % NC
                stats_done[0] += 1
                pe.wait_ge(n_sq, stats_done[0])
                for tb in range(NT):
                    ins = mm(TB[0][:, tb:tb + 1], t8[:, c, tb * P:(tb + 1) * P], ones[:, 0:1],
                             start=(c == 0 and tb == 0), stop=False, skip_group_check=True)
                    if centred:
                        ins = mm(TB[0][:, 4 + tb:5 + tb], x[:, c, tb * P:(tb + 1) * P], ones[:, 0:1], start=False,
                                 stop=False, skip_group_check=True)
                return ins

            def norm(n, centred):
                for c in range(NC if n == 0 else 1):
                    ins = stats(centred)
                ins.then_inc(n_stat, 1)
                pe.wait_ge(n_diag, n + 1)
                mm(SB[0][:, :], ones, E[:, 0, :], start=True, stop=True).then_inc(n_bcast, 1)
                if centred:
                    means[0] += 1
                    pe.wait_ge(n_diag2, means[0])
                    mm(SB[1][:, :], ones, E[:, 1, :], start=True, stop=True).then_inc(n_bcast2, 1)

            def attend(phase):
                steps = ATT[phase]

                def scores(s):
                    i, u, qb, nk, kind = s["i"], s["u"], s["qb"], s["nk"], s["kind"]
                    if i >= 3:
                        pe.wait_ge(at_max, i - 2)
                    b = HD * (u % 2)
                    q = slice(qb * P, (qb + 1) * P)
                    if kind == "cmp":
                        for qq in range(NT):
                            ins = mm(score_bank(s)[:, NCMP * qq:NCMP * qq + NCMP], Q[b:b + HD, u // 2, qq * P:qq * P + P],
                                     ar(A_KCT, 32)[b:b + HD, 0:NCMP], start=True, stop=True)
                        ins.then_inc(at_sc, 1)
                        return
                    if kind == "swa":
                        a, k = Q[b:b + HD, u // 2, q], ar(A_AK, S)[b:b + HD, (qb + 1) * P - nk:(qb + 1) * P]
                    elif kind == "fgt":
                        a, k = Q[b:b + HD, 4 + u // 2, q], ar(A_BK, 4, S)[b:b + HD, u // 2, 0:nk]
                    elif kind in ("sel", "win"):
                        a = Q[b:b + HD, u // 2, q]
                        k = ar(A_KS if kind == "sel" else A_KW, S)[b:b + HD, 0:nk]
                    elif kind == "dsa":
                        if qb == 0:
                            pe.wait_ge(aux_ev, u + 1)
                        a, k = qlat[:, u * S + qb * P:u * S + qb * P + P], ar(A_CKT, S)[:, 0:nk]
                    else:
                        b = HD * s["half"]
                        a, k = Q[b:b + HD, u, q], ar(A_DK, 8, S)[b:b + HD, u, 0:nk]
                    mm(score_bank(s)[:, 0:nk], a, k, start=True, stop=True).then_inc(at_sc, 1)

                def turn(s):
                    j = s["j"]
                    if j is None:
                        return
                    pe.wait_ge(at_nm, s["i"] + 1)
                    if j >= 2:
                        pe.wait_ge(at_pt, j - 1)
                    a, b = s["slots"]
                    w = NCMP if s["kind"] == "cmp" else P
                    for n in range(a, b):
                        ins = nc.tensor.transpose(TB[j % 2][0:w, n * P:(n + 1) * P],
                                                  E[:, s["i"] % 4, (n - a) * w:(n - a) * w + w], ident)
                    ins.then_inc(at_tr, 1)

                def values(s, part):
                    kind, u, m, g_ = s["kind"], s["u"], s["m"], s["g"]
                    if part == 0:
                        pe.wait_ge(at_pt, s["j"] + 1)
                        if s["first"] and g_ >= 2:
                            pe.wait_ge(at_oe, g_ - 1)
                    o, pt = OB[g_ % 2], turned_at(s)[0]
                    if kind == "swa":
                        va = ar(A_VA, NT, P)
                        q = slice(part * P, (part + 1) * P)
                        ins = mm(o[:, q], va[:, part, :], pt[:, 1, q], start=True, stop=(part == 0),
                                 skip_group_check=True)
                        if part:
                            ins = mm(o[:, q], va[:, part - 1, :], pt[:, 0, q], start=False, stop=True,
                                     skip_group_check=True)
                    elif kind == "cmp":
                        if part == 3:
                            ins = mm(o[:, :], ar(A_VCN, P)[0:NCMP, :], pt[0:NCMP, 0, :], start=True, stop=False,
                                     skip_group_check=True)
                    else:
                        kb = part
                        if kind == "fgt":
                            v = ar(A_VB, NT, S)[:, kb, (u // 2) * P:(u // 2 + 1) * P]
                        elif kind == "dsa":
                            v = ar(A_CKN, NT, P)[:, kb, :]
                        elif kind == "dif":
                            v = ar(A_DV, NT, 1024)[:, kb, u * P:(u + 1) * P]
                        else:
                            v = ar(A_VN, NT, 256)[:, kb, P * (kind == "win"):P * (kind == "win") + P]
                        ins = mm(o[:, kb * P:S], v, pt[:, kb, kb * P:S], start=(kb == 0 and s["first"]),
                                 stop=(kb == NT - 1), skip_group_check=True)
                    if part == 3:
                        ins.then_inc(at_pv, 1)

                def nf(hd):
                    pe.wait_ge(nf_diag, hd + 1)
                    if hd:
                        pe.wait_ge(nf_copy, hd)
                    mm(AB[:, :], ones[0:8, :], ar(A_AK, S)[0:8, :], start=True, stop=True).then_inc(nf_mm, 1)

                def aux_mm_(lhsT, rhs):
                    if aux[0]:
                        pe.wait_ge(aux_ev, aux[0])
                    aux[0] += 1
                    mm(LB[0][:, :], lhsT, rhs, start=True, stop=True).then_inc(aux_mm, 1)

                def q_latent(u):
                    b = HD * (u % 2)
                    aux_mm_(ar(A_M2, M2W)[b:b + HD, M2_UK + P * (u // 2):M2_UK + P * (u // 2) + P],
                            Q[b:b + HD, 4 + u // 2, :])

                def o_latent(u):
                    pe.wait_ge(at_oe, ATT["dsa"][4 * u]["g"] + 1)
                    aux_mm_(ar(A_M2, M2W)[:, M2_UV + P * (u // 2):M2_UV + P * (u // 2) + P],
                            ar(A_OL + S * (u % 2), S))

                if phase == "fgt":
                    pe.wait_ge(ada_add, len([k for k in FIN_AT if k <= PHASE["p1"][-1]]) + 2)
                    nf(0)
                for n in range(len(steps) + LAG_SUM + 1):
                    if n < len(steps):
                        s = steps[n]
                        if phase == "fgt" and s["qb"] == NT - 1 and s["u"] < 7:
                            nf(s["u"] + 1)
                        if s["kind"] == "sel" and s["qb"] == 0:
                            q_latent(s["u"])
                        scores(s)
                    if 0 <= n - LAG_TR < len(steps):
                        turn(steps[n - LAG_TR])
                    for part in range(4):
                        k = n - LAG_PV - part * (2 if phase == "dif" else 1)
                        if 0 <= k < len(steps) and steps[k]["end"]:
                            values(steps[k], part)
                    m = n - LAG_POST
                    if phase == "dsa" and 0 <= m < len(steps) and steps[m]["end"]:
                        o_latent(steps[m]["u"])
                    m = n - LAG_SUM
                    if phase == "dif" and 0 <= m < len(steps) and steps[m]["end"]:
                        u = steps[m]["u"]
                        pe.wait_ge(d_sq, u + 1)
                        for tb in range(NT):
                            at = u * S + tb * P
                            ins = mm(AB[:, 4 * u + tb:4 * u + tb + 1], head_sq[:, at:at + P], ones[:, 0:1],
                                     start=True, stop=True)
                        ins.then_inc(d_st, 1)

            pe.wait_ge(consts_in, 48)
            tab = ar(A_TAB, 24)[0:34, :]
            mm(SB[0][0:24, 0:BAND], tab, ar(A_OHB, BAND)[0:34, :], start=True, stop=True)
            mm(SB[1][0:24, 0:496], tab, ar(A_OHC, CBAND)[0:34, 0:496], start=True, stop=True)
            mm(TB[0][0:24, 0:496], tab, ar(A_OHC, CBAND)[0:34, 496:CBAND], start=True, stop=True).then_inc(bias_mm, 1)
            finish_ada(0)
            finish_ada(1)
            pe.wait_ge(bias_evac, 1)
            norm(0, False)
            tiles("p1")
            pe.wait_ge(f_row, 1)
            for tb in range(NT):
                ins = nc.tensor.transpose(TB[0][:, 8 * tb:8 * tb + 8], frow[:, tb * P:(tb + 1) * P], ident[0:8, 0:8])
            ins.then_inc(f_tr, 1)
            pe.wait_ge(f_tok, 1)
            pe.wait_ge(evac_act, EVAC[PHASE["p1"][-1]][1])
            pe.wait_ge(vt_ev, 1)
            pe.wait_ge(nat_evac, nat[0])
            attend("swa")
            attend("fgt")
            pe.wait_ge(at_oe, ATT["fgt"][-1]["g"] + 1)
            tiles("o1")
            norm(1, False)
            tiles("lin")
            ta, tx = PHASE["lcore"]
            pe.wait_ge(lo_done, tx + 1)
            pe.wait_ge(evac_act, EVAC[PHASE["lin"][-1]][1])
            pe.wait_ge(n_t, 16)
            for c in range(NC):
                pe.wait_ge(h_lo, h_base["xc"] + c + 1)
                if c >= 2:
                    pe.wait_ge(l_sig, c - 1)
                for k, t in enumerate((ta, tx)):
                    ins = mm3(NB[2 * (c % 2) + k][:, :], weights(t, c * P, P), h(c * S, S), True, True)
                    ins.then_inc(l_mm if c < NC - 1 else tile_done, 1)
            pe.wait_ge(l_sig, NC)
            tiles("o2")
            norm(2, False)
            tiles("ev1")
            n = 0
            pe.wait_ge(nat_evac, nat[0])
            for qb in range(1, NT):
                for j in range(8):
                    b = HD * (j % 2)
                    if n >= 2:
                        pe.wait_ge(ix_r, n - 1)
                    mm(SB[n % 2][:, 0:P * (qb + 1)], ar(A_IQ, 4, S)[b:b + HD, j // 2, qb * P:(qb + 1) * P],
                       ar(A_IK, S)[b:b + HD, 0:P * (qb + 1)], start=True, stop=True).then_inc(ix_s, 1)
                    n += 1
            pe.wait_ge(ix_r, n)
            tiles("ev2")
            pe.wait_ge(lat_r, 1)
            for tb in range(NT):
                ins = nc.tensor.transpose(TB[0][:, tb * P:(tb + 1) * P], t8[:, 5, tb * P:(tb + 1) * P], ident)
            ins.then_inc(lat_t, 1)
            pe.wait_ge(lat_n, 1)
            pe.wait_ge(vt_ev, 4)
            for tb in range(NT):
                ins = nc.tensor.transpose(TB[1][:, tb * P:(tb + 1) * P], ar(A_CKN, NT, P)[:, tb, :], ident)
            ins.then_inc(lat_tt, 1)
            pe.wait_ge(evac_act, EVAC[PHASE["ev2"][-1]][1])
            for kv in range(2):
                pe.wait_ge(b_add, kv + 1)
                if kv:
                    pe.wait_ge(wv_in, 16)
                    pe.wait_ge(hid_done, 1)
                else:
                    pe.wait_ge(wk_in, 32)
                for hc in range(2):
                    for k in range(16):
                        ins = mm(LB[hc][:, 0:62], cmp_weights(kv, k)[:, hc * P:hc * P + P],
                                 cmp_in(kv)[:, 62 * k:62 * k + 62], start=(k == 0), stop=(k == 15))
                ins.then_inc(c_mm, 1)
            pe.wait_ge(hid_done, 2)
            pe.wait_ge(m2_in, 16)
            hid, m2 = ar(A_HID, 4, 62), ar(A_M2, M2W)
            for hc in range(2):
                mm(SB[0][:, 0:62], m2[:, M2_K + P * hc:M2_K + P * hc + P], hid[:, hc, :], start=(hc == 0),
                   stop=(hc == 1))
            for gg in range(2):
                for hc in range(2):
                    ins = mm(SB[1][0:NCMP, HD * gg:HD * gg + HD], hid[:, 2 + hc, NCMP * gg:NCMP * gg + NCMP],
                             m2[:, M2_V + HD * hc:M2_V + HD * hc + HD], start=(hc == 0), stop=(hc == 1),
                             skip_group_check=True)
            ins.then_inc(kc_mm, 1)
            pe.wait_ge(kc_done, 1)
            pe.wait_ge(lat_done, 1)
            attend("nsa")
            attend("dsa")
            pe.wait_ge(aux_ev, 16)
            tiles("o3")
            norm(3, True)
            tiles("m1")
            norm(4, True)
            tiles("od")
            pe.wait_ge(dl_p, 1)
            mm(AB[:, 0:2], ones[0:HD, :], dlam[0:HD, 0:2], start=True, stop=True).then_inc(dl_mm, 1)
            pe.wait_ge(nat_evac, nat[0])
            attend("dif")
            for hh in range(8):
                pe.wait_ge(d_diag, hh + 1)
                if hh >= 2:
                    pe.wait_ge(d_y, hh - 1)
                mm(SB[hh % 2][:, :], ones, E[:, hh % 2, :], start=True, stop=True).then_inc(d_bc, 1)
            pe.wait_ge(at_oe, ATT["dif"][-1]["g"] + 1)
            tiles("o4")
            norm(5, True)
            tiles("m2")
            norm(6, True)


def bucket(dist):
    import numpy as np
    n = np.maximum(dist, 0)
    nf = np.maximum(n, 1).astype(np.float32)
    large = 16 + (np.log(nf / 16) / math.log(128 / 16) * 16).astype(np.int32)
    return np.where(n < 16, n, np.minimum(large, N_BUCKET - 1))


def constants():
    import numpy as np

    def onehot(dist):
        o = np.zeros((34, dist.size), np.float32)
        o[bucket(dist), np.arange(dist.size)] = 1
        o[32] = dist < 0
        o[33] = dist >= 128
        return o

    cc = np.zeros((P, NCONST), np.float32)
    cc[:, C_ID:C_ID + P] = np.eye(P)
    cc[:, C_ONE:C_ONE + P] = 1
    r = np.arange(P)
    cc[:, C_TRI:C_TRI + P] = np.where(r[None, :] > r[:, None], NEG, 0)
    t = np.arange(NT)[None, :, None] * P + r[:, None, None]
    cc[:, C_MC:] = (t >= 16 * np.arange(NCMP)[None, None, :] + 31).reshape(P, -1)
    z = 16 * np.arange(61, -1, -1)[None, :] + np.arange(16)[:, None]
    return cc, onehot(np.arange(255, 255 - BAND, -1)), onehot(z.reshape(-1) - 480 - 31)


def layout(i):
    import numpy as np
    r = np.arange
    pair = np.concatenate([np.concatenate([r(64 * c, 64 * c + 64), r(256 + 64 * c, 320 + 64 * c)]) for c in range(4)])
    rows = np.concatenate([pair, r(512, 1024)])
    w_in, e_in, o_in = i["attn_w_in"][0], i["ev_w_in_2"][0], i["od_w_in_2"][0]
    l_in = i["lru_w_in"][0]
    outs = {"o1": i["attn_w_out"][0][rows], "o2": i["lru_w_out"][0], "o3": i["ev_w_out_2"][0][rows],
            "o4": i["od_w_out_2"][0]}
    stacked = {"wa": i["lru_w_a"][0].reshape(D, P), "wx": i["lru_w_x"][0].reshape(D, P)}

    def block(mat, cols, k0=0):
        w = mat[:, cols]
        if w.shape[1] < P:
            w = np.concatenate([w, np.zeros((w.shape[0], P - w.shape[1]), w.dtype)], 1)
        n = BLK // w.shape[1]
        return w[k0 * P:(k0 + n) * P].reshape(n, P, -1).transpose(1, 0, 2).reshape(P, BLK)

    blocks, quarter = [], {"m1": -1, "m2": -1}
    for phase, kind, what in TILES:
        name, n = what[0], what[1]
        c = r(P * n, P * n + P)
        if phase == "p1":
            cols = {"q": (pair if n < 4 else 768 - 512 + r(1024))[c] if name == "q" else None, "ak": r(512, 640),
                    "bk": 1280 + c, "f": r(2304, 2312),
                    "gate": 2312 + rows[c] if name == "gate" else None, "vb": r(1792, 2304), "va": r(640, 768)}[name]
            b = block(w_in, cols, n * 2 if name == "vb" else 0)
        elif phase in outs:
            b = block(outs[phase], c)
        elif phase == "lin":
            b = block(l_in, c + (D if name == "lgate" else 0))
        elif phase == "lcore":
            b = block(stacked[name], r(P))
        elif phase in ("ev1", "ev2"):
            if name == "q":
                cols = pair[c] if n < 4 else 1304 + c - 512
            elif name == "kc2":
                cols = 512 + c
            else:
                cols = {"ik": np.concatenate([r(2456, 2520)] * 2), "iq": 1944 + c,
                        "gi": np.concatenate([r(1280, 1304), r(2520, 2528)]), "kvl": r(1816, 1944),
                        "ks": r(768, 896), "kw": r(1024, 1152),
                        "vn": r(1152, 1280) if n else r(896, 1024)}[name]
            b = block(e_in, cols)
        elif phase in ("m1", "m2"):
            layer = int(phase[1]) - 1
            if name == "up":
                quarter[phase] += n == 0
                b = block(i["mlp_w1_2"][layer], quarter[phase] * D + c)
            else:
                b = block(i["mlp_w2_2"][layer][quarter[phase] * D:(quarter[phase] + 1) * D], c)
        else:
            cols = {"q": c, "dk": D + c, "dv0": 2 * D + r(512), "dv1": 2 * D + 512 + r(512)}[name]
            b = block(o_in, cols, 2 * n if name[:2] == "dv" else 0)
        blocks.append(b)
    W = np.stack(blocks)
    WC = np.stack([np.concatenate([block(i[name][0], r(256), 4 * n) for n in range(4)], 1)
                   for name in ("nsa_w1_k_2", "nsa_w1_v_2")])

    ada = []
    for w, n in ((i["ada_w"], 3), (i["ada_w_2"], 6)):
        ada.append(w.reshape(2, NC, P, n, D).transpose(0, 3, 1, 2, 4).reshape(-1, P, D))
    WA = np.concatenate(ada)

    def feat(v):
        return v.reshape(-1, P).T

    vec = {
        "c": feat(i["c"]), "c2": feat(i["c_2"]), "ng0": feat(i["norm_g"][0]), "ng1": feat(i["norm_g"][1]),
        "adab": feat(np.concatenate([i["ada_b"].reshape(-1), i["ada_b_2"].reshape(-1)])), "fg": feat(i["final_g"]),
        "lng": feat(i["ln_g_2"]), "lnb": feat(i["ln_b_2"]), "cw": feat(i["lru_conv_w"]), "cb": feat(i["lru_conv_b"]),
        "ba": feat(i["lru_b_a"]), "bx": feat(i["lru_b_x"]), "lam": feat(i["lru_lambda"]),
        "kvn": feat(i["dsa_kv_norm_2"]), "sub": feat(i["diff_subln_2"]), "bf": i["attn_b_f"].T,
        "pek": feat(i["nsa_pe_k_2"]), "pev": feat(i["nsa_pe_v_2"]),
        "sink": np.broadcast_to(i["attn_sinks"], (P, 8)), "t31": np.broadcast_to(i["rel_bias_2"][31:32], (P, 16)),
        "dlam": i["diff_lam_2"][0].T,
    }
    CV = np.zeros((P, NCOL), np.float32)
    for name, v in vec.items():
        lo, hi = COLS[name]
        CV[:v.shape[0], lo:hi] = v
    CC, oh_band, oh_cmp = constants()
    tab = np.zeros((34, 24), np.float32)
    tab[:32, :8], tab[:32, 8:] = i["rel_bias"], i["rel_bias_2"]
    tab[32], tab[33, :8] = NEG, NEG
    OH = np.concatenate([oh_band, oh_cmp, tab], 1)
    w2k = i["nsa_w2_k_2"][0].reshape(2, P, HD).transpose(1, 0, 2)
    w2v = i["nsa_w2_v_2"][0].reshape(2, P, HD).transpose(1, 0, 2)
    uk = i["dsa_w_uk_2"][0].transpose(1, 2, 0).reshape(4, P, P).transpose(1, 0, 2)
    M2 = np.concatenate([np.concatenate([w2k, w2k], 2).reshape(P, -1), w2v.reshape(P, -1), uk.reshape(P, -1),
                         i["dsa_w_uv_2"][0].reshape(P, -1)], 1)
    X = i["x"][0].T.reshape(NC, P, S).transpose(1, 0, 2).reshape(P, -1)
    return [np.ascontiguousarray(a) for a in (W, WC, WA, X, CV, CC, OH, M2)]


def kernel(**inputs):
    import numpy as np
    import concourse.bacc as bacc
    from concourse.bass_utils import run_bass_kernel_spmd as run

    nc = bacc.Bacc("TRN2", target_bir_lowering=False, num_devices=1)
    arrays, args = {}, []
    for name, a in zip(("W", "WC", "WA", "X", "CV", "CC", "OH", "M2"), layout({k: np.asarray(v) for k, v in inputs.items()})):
        arrays[f"in_{name}"] = a
        args.append(nc.dram_tensor(f"in_{name}", a.shape, mybir.dt.from_np(a.dtype), kind="ExternalInput").ap())
    args.append(nc.dram_tensor("bias_by_distance", (24, 16, BAND), F32, kind="Internal").ap())
    args.append(nc.dram_tensor("bias_of_compressed", (24, CBAND), F32, kind="Internal").ap())
    args.append(nc.dram_tensor("out", (P, NC, S), F32, kind="ExternalOutput").ap())
    program(nc, *args)
    r = run(nc, [arrays], core_ids=[0])
    out = r.results[0]["out"]
    return out.transpose(2, 1, 0).reshape(1, S, D)
```
